# Optimizing a Trainium2 kernel written in Bass

```python
import jax, jax.numpy as jnp
from jax import lax
import numpy as np

D_MODEL = 1024
BATCH = 1
SEQ = 1024
DEPTH = 1
DEC_BATCH = 8
DEC_SEQ = 8
PAST_LEN = 1024
PAGE_SIZE = 128

D_MIX = D_MODEL
HEAD_DIM = 64
H_GLA = (3 * D_MIX) // (8 * HEAD_DIM)
GLA_DK = HEAD_DIM // 2
GLA_DV = HEAD_DIM
GLA_LR = 16
GLA_GATE_NORM = 16.0
GLA_CHUNK = 64
GLA_W = H_GLA * GLA_DV
POOL_WIDTH = D_MIX // 4
POOL_WINDOWS = (2, 4, 8, 16)
POOL_GROUP = POOL_WIDTH // 4
POOL_HIST = 16 - 1
H_FOX = (3 * D_MIX) // (8 * HEAD_DIM)
FOX_W = H_FOX * HEAD_DIM
Q_BLOCK = 128
N_META = 16
EPS = 1e-6

SPLIT_SIZES = (H_GLA * GLA_DK, H_GLA * GLA_DK, GLA_W, GLA_LR, GLA_W,
               POOL_WIDTH, POOL_WIDTH,
               FOX_W, FOX_W, FOX_W, H_FOX, FOX_W)
D_IN = sum(SPLIT_SIZES)
SPLIT_IDX = tuple(sum(SPLIT_SIZES[:i + 1]) for i in range(len(SPLIT_SIZES) - 1))

kernel_name = "hymba_gla_pool_fox_step"

def rmsnorm(x, g):
    xf = x.astype(jnp.float32)
    y = xf * lax.rsqrt(jnp.mean(xf * xf, axis=-1, keepdims=True) + EPS)
    return (y * g.astype(jnp.float32)).astype(x.dtype)

def mixer_inputs(h, pre, wi, w_up, b_gate, bf):
    B, T, _ = h.shape
    (gq, gk, gv, glr, gg, pv, pg, fq, fk, fv, ff, fg) = jnp.split(rmsnorm(h, pre) @ wi, SPLIT_IDX, axis=-1)
    f32 = jnp.float32
    q = gq.reshape(B, T, H_GLA, GLA_DK).astype(f32) * (GLA_DK ** -0.5)
    k = gk.reshape(B, T, H_GLA, GLA_DK).astype(f32)
    v = gv.reshape(B, T, H_GLA, GLA_DV).astype(f32)
    g = (jax.nn.log_sigmoid((glr @ w_up + b_gate).astype(f32)) / GLA_GATE_NORM).reshape(B, T, H_GLA, GLA_DK)
    fq = fq.reshape(B, T, H_FOX, HEAD_DIM)
    fk = fk.reshape(B, T, H_FOX, HEAD_DIM)
    fv = fv.reshape(B, T, H_FOX, HEAD_DIM)
    logf = jax.nn.log_sigmoid((ff + bf).astype(f32))
    return q, k, v, g, gg, pv, pg, fq, fk, fv, logf, fg

def gla_chunked(q, k, v, g, s0):
    B, T, H, _ = q.shape
    dv = v.shape[-1]
    c = GLA_CHUNK if T % GLA_CHUNK == 0 else T
    n = T // c

    def chunks(a):
        return a.reshape(B, n, c, H, a.shape[-1]).transpose(1, 0, 3, 2, 4)

    causal = jnp.tril(jnp.ones((c, c), dtype=bool))

    def step(s, inp):
        qc, kc, vc, gc = inp
        b = jnp.cumsum(gc, axis=2)
        qe = qc * jnp.exp(b)
        ke = kc * jnp.exp(-b)
        a = jnp.where(causal, jnp.einsum('bhtk,bhsk->bhts', qe, ke), 0.0)
        o = jnp.einsum('bhts,bhsv->bhtv', a, vc) + jnp.einsum('bhtk,bhkv->bhtv', qe, s)
        b_end = b[:, :, -1:, :]
        s_new = (jnp.exp(b_end[:, :, 0, :])[..., None] * s
                 + jnp.einsum('bhsk,bhsv->bhkv', kc * jnp.exp(b_end - b), vc))
        return s_new, o

    s, o = lax.scan(step, s0.astype(jnp.float32), (chunks(q), chunks(k), chunks(v), chunks(g)))
    return o.transpose(1, 0, 3, 2, 4).reshape(B, T, H, dv), s

def pool_mix(v, hist, pos0, pw, ps):
    B, T, C = v.shape
    P = POOL_HIST
    ext = jnp.concatenate([hist.astype(jnp.float32), v.astype(jnp.float32)], axis=1)
    c = jnp.concatenate([jnp.zeros((B, 1, C), jnp.float32), jnp.cumsum(ext, axis=1)], axis=1)
    end = c[:, P + 1:P + 1 + T]
    pos = pos0 + jnp.arange(T)
    means = []
    for gi, w in enumerate(POOL_WINDOWS):
        sl = slice(gi * POOL_GROUP, (gi + 1) * POOL_GROUP)
        cnt = jnp.minimum(pos + 1, w).astype(jnp.float32)[None, :, None]
        means.append((end[..., sl] - c[:, P + 1 - w:P + 1 - w + T, sl]) / cnt)
    d = (jnp.concatenate(means, axis=-1) - v.astype(jnp.float32)).reshape(B, T, 4, POOL_GROUP)
    y = jnp.einsum('btgc,gcd->btgd', d, pw.astype(jnp.float32)).reshape(B, T, C) * ps.astype(jnp.float32)
    return y, ext[:, -P:].astype(v.dtype)

def fox_attend(q, fq, pq, k, v, fk, pk):
    s = jnp.einsum('bqhd,bkhd->bhqk', q, k).astype(jnp.float32) * (HEAD_DIM ** -0.5)
    s = s + jnp.swapaxes(fq, 1, 2)[..., :, None] - jnp.swapaxes(fk, 1, 2)[..., None, :]
    s = jnp.where(pq[:, None] >= pk[None, :], s, -jnp.inf)
    p = jax.nn.softmax(s, axis=-1)
    return jnp.einsum('bhqk,bkhd->bqhd', p.astype(v.dtype), v)

def fox_prompt(q, k, v, F):
    B, L, H, d = q.shape
    pos = jnp.arange(L)
    m = slice(0, N_META)
    o_meta = fox_attend(q[:, m], F[:, m], pos[m], k[:, m], v[:, m], F[:, m], pos[m])
    T = L - N_META
    n_blk = T // Q_BLOCK

    def blocks(a):
        return jnp.swapaxes(a[:, N_META:].reshape((B, n_blk, Q_BLOCK) + a.shape[2:]), 0, 1)

    pq = pos[N_META:].reshape(n_blk, Q_BLOCK)
    o_real = lax.map(lambda blk: fox_attend(blk[0], blk[1], blk[2], k, v, F, pos), (blocks(q), blocks(F), pq))
    o_real = jnp.swapaxes(o_real, 0, 1).reshape(B, T, H, d)
    return jnp.concatenate([o_meta, o_real], axis=1)

def mixer_output(h, o_gla, gg, o_pool, pg, o_fox, fg, gla_g, wo, post):
    B, T, _ = h.shape
    dt = h.dtype
    o_gla = rmsnorm(o_gla, gla_g).reshape(B, T, GLA_W).astype(dt)
    y = jnp.concatenate([o_gla * jax.nn.silu(gg),
                         o_pool.astype(dt) * jax.nn.silu(pg),
                         o_fox.reshape(B, T, FOX_W).astype(dt) * jax.nn.silu(fg)], axis=-1) @ wo
    return h + rmsnorm(y, post)

def prompt_layer(h, pre, wi, w_up, b_gate, gla_g, pw, ps, bf, wo, post):
    B = h.shape[0]
    q, k, v, g, gg, pv, pg, fq, fk, fv, logf, fg = mixer_inputs(h, pre, wi, w_up, b_gate, bf)
    m = slice(0, N_META)
    r = slice(N_META, None)
    s0 = jnp.zeros((B, H_GLA, GLA_DK, GLA_DV), jnp.float32)
    o_m, s_m = gla_chunked(q[:, m], k[:, m], v[:, m], g[:, m], s0)
    o_r, s_gla = gla_chunked(q[:, r], k[:, r], v[:, r], g[:, r], s_m)
    o_gla = jnp.concatenate([o_m, o_r], axis=1)
    o_pool, hist = pool_mix(pv, jnp.zeros((B, POOL_HIST, POOL_WIDTH), pv.dtype), 0, pw, ps)
    o_fox = fox_prompt(fq, fk, fv, jnp.cumsum(logf, axis=1))
    h = mixer_output(h, o_gla, gg, o_pool, pg, o_fox, fg, gla_g, wo, post)
    return h, fk, fv, logf, s_gla, hist

def sample_layer(h, k_pages, v_pages, lf_pages, page_table, s_gla, hist, pre, wi, w_up, b_gate, gla_g, pw, ps, bf, wo, post):
    B, T, _ = h.shape
    q, k, v, g, gg, pv, pg, fq, fk, fv, logf, fg = mixer_inputs(h, pre, wi, w_up, b_gate, bf)
    past = page_table.shape[1] * k_pages.shape[1]
    o_gla, s_new = gla_chunked(q, k, v, g, s_gla)
    o_pool, hist_new = pool_mix(pv, hist, past, pw, ps)
    kp = k_pages[page_table].reshape(B, past, H_FOX, HEAD_DIM)
    vp = v_pages[page_table].reshape(B, past, H_FOX, HEAD_DIM)
    lp = lf_pages[page_table].reshape(B, past, H_FOX).astype(jnp.float32)
    F = jnp.cumsum(jnp.concatenate([lp, logf], axis=1), axis=1)
    keys = jnp.concatenate([kp.astype(fk.dtype), fk], axis=1)
    vals = jnp.concatenate([vp.astype(fv.dtype), fv], axis=1)
    pos = jnp.arange(past + T)
    o_fox = fox_attend(fq, F[:, past:], pos[past:], keys, vals, F, pos)
    h = mixer_output(h, o_gla, gg, o_pool, pg, o_fox, fg, gla_g, wo, post)
    return h, fk, fv, logf, s_new, hist_new

def setup_inputs(seed: int = 0) -> dict:
    key = jax.random.key(seed)
    ks = jax.random.split(key, 24)
    n_pages = PAST_LEN // PAGE_SIZE
    n_used = DEC_BATCH * n_pages
    n_phys = (n_used * 5) // 4
    nrm = jax.random.normal
    page_table = jax.random.permutation(ks[0], n_phys)[:n_used].reshape(DEC_BATCH, n_pages).astype(jnp.int32)
    fox_bias_base = jnp.linspace(1.0, 4.0, H_FOX)[None, :]
    return {
        "x_prompt": nrm(ks[1], (BATCH, SEQ, D_MODEL), jnp.float32),
        "x_sample": nrm(ks[2], (DEC_BATCH, DEC_SEQ, D_MODEL), jnp.float32),
        "cache_fox_k": nrm(ks[3], (DEPTH, n_phys, PAGE_SIZE, H_FOX, HEAD_DIM), jnp.float32),
        "cache_fox_v": nrm(ks[4], (DEPTH, n_phys, PAGE_SIZE, H_FOX, HEAD_DIM), jnp.float32),
        "cache_fox_logf": jax.nn.log_sigmoid(2.0 + 0.5 * nrm(ks[5], (DEPTH, n_phys, PAGE_SIZE, H_FOX), jnp.float32)),
        "state_gla": 0.5 * nrm(ks[6], (DEPTH, DEC_BATCH, H_GLA, GLA_DK, GLA_DV), jnp.float32),
        "state_pool": nrm(ks[7], (DEPTH, DEC_BATCH, POOL_HIST, POOL_WIDTH), jnp.float32),
        "page_table": page_table,
        "meta_tokens": nrm(ks[8], (N_META, D_MODEL), jnp.float32),
        "norm_pre": 1.0 + 0.05 * nrm(ks[9], (DEPTH, D_MODEL), jnp.float32),
        "norm_post": 1.0 + 0.05 * nrm(ks[10], (DEPTH, D_MODEL), jnp.float32),
        "w_in": nrm(ks[11], (DEPTH, D_MODEL, D_IN), jnp.float32) * D_MODEL ** -0.5,
        "gla_w_up": nrm(ks[12], (DEPTH, GLA_LR, H_GLA * GLA_DK), jnp.float32) * GLA_LR ** -0.5,
        "gla_b_gate": 0.1 * nrm(ks[13], (DEPTH, H_GLA * GLA_DK), jnp.float32),
        "gla_norm": 1.0 + 0.05 * nrm(ks[14], (DEPTH, GLA_DV), jnp.float32),
        "pool_w": nrm(ks[15], (DEPTH, 4, POOL_GROUP, POOL_GROUP), jnp.float32) * POOL_GROUP ** -0.5,
        "pool_scale": 1.0 + 0.1 * nrm(ks[16], (DEPTH, POOL_WIDTH), jnp.float32),
        "fox_b_f": fox_bias_base + 0.3 * nrm(ks[17], (DEPTH, H_FOX), jnp.float32),
        "w_out": nrm(ks[18], (DEPTH, D_MIX, D_MODEL), jnp.float32) * D_MIX ** -0.5,
    }

def reference(x_prompt, x_sample, cache_fox_k, cache_fox_v, cache_fox_logf, state_gla, state_pool, page_table,
              meta_tokens, norm_pre, norm_post, w_in, gla_w_up, gla_b_gate, gla_norm, pool_w, pool_scale,
              fox_b_f, w_out):
    B, _, D = x_prompt.shape
    meta = jnp.broadcast_to(meta_tokens.astype(x_prompt.dtype)[None], (B, N_META, D))
    h_p = jnp.concatenate([meta, x_prompt], axis=1)
    h_s = x_sample
    kp_l, vp_l, lfp_l, sgp_l, spp_l = [], [], [], [], []
    ks_l, vs_l, lfs_l, sgs_l, sps_l = [], [], [], [], []
    for l in range(DEPTH):
        w = (norm_pre[l], w_in[l], gla_w_up[l], gla_b_gate[l], gla_norm[l], pool_w[l], pool_scale[l],
             fox_b_f[l], w_out[l], norm_post[l])
        h_p, kp, vp, lfp, sgp, spp = prompt_layer(h_p, *w)
        h_s, ks, vs, lfs, sgs, sps = sample_layer(h_s, cache_fox_k[l], cache_fox_v[l], cache_fox_logf[l],
                                                  page_table, state_gla[l], state_pool[l], *w)
        kp_l.append(kp); vp_l.append(vp); lfp_l.append(lfp); sgp_l.append(sgp); spp_l.append(spp)
        ks_l.append(ks); vs_l.append(vs); lfs_l.append(lfs); sgs_l.append(sgs); sps_l.append(sps)
    return (h_p[:, N_META:], h_s,
            jnp.stack(kp_l), jnp.stack(vp_l), jnp.stack(lfp_l), jnp.stack(sgp_l), jnp.stack(spp_l),
            jnp.stack(ks_l), jnp.stack(vs_l), jnp.stack(lfs_l), jnp.stack(sgs_l), jnp.stack(sps_l))


_drawn_inputs = setup_inputs


def setup_inputs(seed=0):
    import zlib

    import numpy as np

    out = dict(_drawn_inputs(seed))
    spreads = {}
    factors = {'cache_fox_logf': 3.956}
    for name, (base, spread) in spreads.items():
        noise = np.random.default_rng([zlib.crc32(name.encode()), seed]).standard_normal(out[name].shape)
        drawn = base * np.exp(spread * noise) if base else spread * noise
        out[name] = __import__('jax').numpy.asarray(drawn.astype(out[name].dtype))
    for name, factor in factors.items():
        out[name] = (out[name] * factor).astype(out[name].dtype)
    return out
```

```python
from contextlib import ExitStack

import concourse.bass as bass
from concourse import mybir

F32 = mybir.dt.float32
F32R = mybir.dt.float32r
BF16 = mybir.dt.bfloat16
I32 = mybir.dt.int32
ALU = mybir.AluOpType
ACT = mybir.ActivationFunctionType
AX = mybir.AxisListType

P = 128
D = 1024
KT = D // P
SEQ, NMETA = 1024, 16
NB, TS = 8, 8
LP = NMETA + SEQ
NS = NB * TS
NT = LP + NS
TH = NT // 3
NTILE = SEQ // P
H, HD = 6, 64
DK, DV = 32, 64
LR = 16
PAGE, NPAGE = 128, 8
PAST = PAGE * NPAGE
HIST = 15
CH = 64
NCH = SEQ // CH
EPS = 1e-6
GATE = 1.0 / 16.0
NEG = -1e30
SLOT = 384

W_GQ, W_GK, W_GV, W_LR, W_GG = 0, 192, 384, 768, 784
W_PV, W_PG, W_FQ, W_FK, W_FV, W_FF, W_FG = 1168, 1424, 1680, 2064, 2448, 2832, 2838

CHUNKS = [[(W_LR, 0, LR), (W_FF, 32, H)]]
CHUNKS += [[(W_GV + P * i, 0, P)] for i in range(3)]
CHUNKS += [[(W_PV + P * i, 0, P)] for i in range(2)]
CHUNKS += [[(W_GK, 0, P)], [(W_GQ, 0, P)], [(W_GQ + P, 0, 64), (W_GK + P, 64, 64)]]
CHUNKS += [[(W_FK + P * i, 0, P)] for i in range(3)]
CHUNKS += [[(W_FQ + P * i, 0, P)] for i in range(3)]
CHUNKS += [[(W_GG + P * i, 0, P)] for i in range(3)]
CHUNKS += [[(W_PG + P * i, 0, P)] for i in range(2)]
CHUNKS += [[(W_FV + P * i, 0, P)] for i in range(3)]
CHUNKS += [[(W_FG + P * i, 0, P)] for i in range(3)]
C_LF, C_GV, C_PV, C_GKA, C_GQA, C_QKB = 0, 1, 4, 6, 7, 8
C_FK, C_FQ, C_GG, C_PG, C_FV, C_FG = 9, 12, 15, 18, 20, 23
NCHUNK = len(CHUNKS)

GBLOCKS = [(NMETA + P * j, P) for j in range(NTILE)] + [(LP, NS), (0, NMETA)]
PIECES = [(NMETA, SLOT), (NMETA + SLOT, SLOT), (NMETA + 2 * SLOT, NT - NMETA - 2 * SLOT)]


def side_jobs():
    s = {c: [] for c in range(NCHUNK)}
    s[1] = [("gate", g, t) for g in range(2) for t in range(3)]
    s[3] = [("logf_rows",), ("page_prefix",)]
    s[4] = [("v_rows", b) for b in range(10)] + [("hist",)]
    s[5] = [("pool_last", 0)] + [("pool", 0, i) for i in range(3)]
    s[6] = [("pool_last", 1)] + [("pool", 1, i) for i in range(3)]
    s[9] = [("kd_rows", i) for i in range(5)] + [("state", 0)]
    for c in range(4):
        for j in (2 * c, 2 * c + 1):
            if j:
                s[9 + c] += [("out", j - 1)]
            s[9 + c] += [("scores", j), ("state", 2 * j + 1), ("state", 2 * j + 2)]
    s[13] = [("out", 7), ("sample_scores",), ("sample_out",)]
    s[13] += [("sample_state", g, i) for g in range(2) for i in range(2)]
    s[14] = [("meansq", i, q) for i in range(3) for q in range(3)]
    s[15] = [("k_rows", t) for t in range(9)]
    s[23] = [("fv_rows", t) for t in range(9)]
    return s


SIDE = side_jobs()


def sample_jobs():
    out = []
    for b in range(NB + 1):
        if b < NB:
            out += [("page_kT", b, g) for g in range(NPAGE)]
        if b:
            out += [("s_probsT", b - 1), ("s_attend", b - 1)]
    return out


def prompt_plan():
    units = [("fox", j, h) for j in range(NTILE) for h in range(H)]
    after = {(2, 0): NTILE, (2, 2): 0, (2, 4): 1}
    after |= {(j, 3): j - 1 for j in range(3, NTILE)}
    order = []
    for n, u in enumerate(units + [None]):
        if u is not None:
            order.append(("S", u))
        if n:
            _, j, h = units[n - 1]
            order += [("R", ("probsT", j, h, i)) for i in range((j + 4) // 3)]
            order.append(("R", ("attend", j, h)))
            if h == 1 and j:
                order.append(("R", ("foxT", j - 1)))
            if (j, h) in after:
                order.append(("S", ("proj", after[j, h])))
    return order + [("R", ("foxT", NTILE - 1)), ("S", ("proj", NTILE - 1))]


PLAN = prompt_plan()
RING = [k for c in range(NCHUNK) for k in SIDE[c]] + sample_jobs() + [k for t, k in PLAN if t == "R"]
RI = {k: i for i, k in enumerate(RING)}
SUSERS = [("seq", b) for b in range(NB)] + [k for t, k in PLAN if t == "S"]
SI = {k: i for i, k in enumerate(SUSERS)}
UNITS = [k for t, k in PLAN if k[0] == "fox"]
UI = {k: i for i, k in enumerate(UNITS)}
PROJ = [k[1] for k in SUSERS if k[0] == "proj"]


def build(nc, a, o):
    with ExitStack() as ctx:
        def sb(name, shape, dt=F32):
            return ctx.enter_context(nc.sbuf_tensor(name, shape, dt))

        def sem(name):
            return ctx.enter_context(nc.semaphore(name))

        YF = sb("YF", [P, 14 * NT])
        Y = YF[:, 0:8 * NT].rearrange("p (s t) -> p s t", t=NT)
        QK = YF[:, 8 * NT:14 * NT].rearrange("p (s t) -> p s t", t=NT)
        xrows = YF[:, 0:9 * D].rearrange("p (t n) -> p t n", n=D)
        RA = sb("RA", [P, 6 * NT])
        E = RA[:, :].rearrange("p (s t) -> p s t", t=NT)
        VR = sb("VR", [P, 10, 384])
        ident = sb("ident", [P, P])
        identb = sb("identb", [P, P], BF16)
        causal = sb("causal", [P, CH])
        causal_s = sb("causal_s", [NS, NS])
        same_seq = sb("same_seq", [NS, NB])
        page_before = sb("page_before", [NS, NS])
        pick_row = sb("pick_row", [P, H, P], BF16)
        mask_neg = sb("mask_neg", [P, P], BF16)
        pick_q = sb("pick_q", [TS, H * TS], BF16)
        mask_new = sb("mask_new", [TS, TS], BF16)
        block_mean = sb("block_mean", [P, P])
        pool_w = sb("pool_w", [P, 2, P])
        negF = sb("negF", [P, LP], BF16)
        small = sb("small", [P, 42])
        gpre = small[:, 0:8]
        bgate = small[:, 8:10]
        gnorm = small[:, 10:11]
        pscale = small[:, 11:13]
        eps = small[:, 13:14]
        one = small[:, 14:15]
        ssq = small[:, 15:24]
        nmax = small[:, 24:28]
        rsum = small[:, 28:32]
        rinv = small[:, 32:36]
        zstat = small[:, 36:38]
        head_of = small[:, 38:42]
        bfox = sb("bfox", [H, 1])
        w_up = sb("w_up", [LR, H * DK])
        ebend = sb("ebend", [P, 2, 25])
        gstate = sb("gstate", [P, 3, 2, DV])
        logf_t = sb("logf_t", [P, 9, H])
        f_sum = sb("f_sum", [H, NS])
        f_last = sb("f_last", [H, NB])
        q_odd = sb("q_odd", [P, H * P])
        ptab = sb("ptab", [1, NB * NPAGE], I32)
        pidx = sb("pidx", [NB * NPAGE, 1], I32)
        PS = ctx.enter_context(nc.psum_tensor("PS", [P, 8, 512], F32))

        with ExitStack() as s2:
            t = lambda n, s, d=F32: s2.enter_context(nc.sbuf_tensor(n, s, d))
            wr, wh, wl = t("wr", [P, 2, KT, P]), t("wh", [P, 2, KT, P], F32R), t("wl", [P, 2, KT, P], F32R)
            xh, xl = t("xh", [P, KT, NT], F32R), t("xl", [P, KT, NT], F32R)
        with ExitStack() as s3:
            t = lambda n, s, d=F32: s3.enter_context(nc.sbuf_tensor(n, s, d))
            pagesB = t("pagesB", [P, 2, NPAGE, 384])
            kT = t("kT", [P, 2, 3, PAST])
            sbias = t("sbias", [H * TS, 2, PAST + TS])
            sprob = t("sprob", [H * TS, 2, PAST + TS])
            sprobT = t("sprobT", [P, 2, NPAGE + 1, H * TS])
            v_new = t("v_new", [TS, 2, 384])
            q_diag = t("q_diag", [P, 3, NB, H * TS])
        with ExitStack() as s4:
            t = lambda n, s, d=F32: s4.enter_context(nc.sbuf_tensor(n, s, d))
            yh, yl = t("yh", [P, KT, P], F32R), t("yl", [P, KT, P], F32R)
            wo_raw = t("wo_raw", [P, 2, D])
            xres, zout = t("xres", [P, D]), t("zout", [P, D])
            woh, wol = t("woh", [P, KT, D], F32R), t("wol", [P, KT, D], F32R)

        pages = [RA[:, 0:2 * NPAGE * 384].rearrange("p (w g n) -> p w g n", w=2, n=384), pagesB[:, :, :, :]]
        glr = Y[0:LR, 5, :]
        reset = Y[:, 7, :]
        ones_row = QK[0:NS, 5, 0:LP]
        logf, ftmp, fcum = QK[0:H, 0, :], QK[0:H, 1, :], QK[0:H, 2, :]
        page_lf = QK[0:NS, 3, 0:PAGE * H].rearrange("p (k h) -> p k h", h=H)
        page_F = QK[0:NS, 4, 0:PAGE * H].rearrange("p (h k) -> p h k", h=H)
        pv, psA, psB = Y[:, 5, :], Y[:, 6, :], Y[:, 7, :]
        hist_rows = Y[0:NB * HIST, 4, 0:256]
        HX = HIST + TS
        hx = [Y[:, 0, 192 * i:192 * i + NB * HX].rearrange("p (b t) -> p b t", b=NB) for i in range(2)]
        hA, hB = (Y[:, 0, 384 + 192 * i:384 + 192 * i + NB * HX].rearrange("p (b t) -> p b t", b=NB) for i in range(2))
        last_p, last_s = Y[0:HIST, 1, 0:256], Y[0:NS, 1, 256:512]
        kd_rows = Y[:, 5:7, :].rearrange("p s t -> p (s t)")[:, 0:9 * 192].rearrange("p (b n) -> p b n", n=192)
        kd_meta = QK[0:NMETA, 4, H * P:H * P + 192]
        kd_seq = Y[:, 5:7, :].rearrange("p s t -> p (s t)")[0:NS, 0:NB * 192].rearrange("p (b n) -> p b n", n=192)
        aT = YF[:, 5 * NT + 9 * 192:5 * NT + 9 * 192 + 2 * H * P].rearrange("p (a h t) -> p a h t", a=2, h=H)
        q_heads = [x.rearrange("p (h t) -> p h t", h=H) for x in (QK[:, 4, 0:H * P], q_odd[:, :])]
        gstate_s = QK[:, 5, 0:2 * NB * DV].rearrange("p (g b v) -> p g b v", g=2, b=NB)
        k_out = RA[:, 0:9 * 384].rearrange("p (t n) -> p t n", n=384)
        gtmp = [E[:, 4, :], E[:, 5, :]]
        xg = RA[:, 0:3 * D].rearrange("p (a k t) -> p a k t", a=3, k=KT)
        prob = RA[:, 0:2 * LP].rearrange("p (a k) -> p a k", a=2)
        at = 2 * LP
        probT = RA[:, at:at + 2 * 9 * P].rearrange("p (a b q) -> p a b q", a=2, b=9)
        at += 2 * 9 * P
        fox_o = RA[:, at:at + 768].rearrange("p (a n) -> p a n", a=2)
        at += 768
        gpost = RA[:, at:at + D]
        nf_d = nc.dram_tensor("minus_F", [NB, H, PAST + TS], F32, kind="Internal").ap()

        d_x = [sem(f"d_x{t}") for t in range(9)]
        d_const, d_poolw = sem("d_const"), sem("d_poolw")
        d_w = [sem("d_w0"), sem("d_w1")]
        d_hist, d_idx, d_lf, d_ptab = sem("d_hist"), sem("d_idx"), sem("d_lf"), sem("d_ptab")
        d_nf, d_fl, d_s0 = sem("d_nf"), sem("d_fl"), sem("d_s0")
        d_out = sem("d_out")
        d_pool_out, d_state_out, d_k_out = sem("d_pool_out"), sem("d_state_out"), sem("d_k_out")
        d_k, d_v = [sem("d_k0"), sem("d_k1")], [sem("d_v0"), sem("d_v1")]
        d_bias = [sem("d_bias0"), sem("d_bias1")]
        d_wo = [sem("d_wo0"), sem("d_wo1")]
        d_post, d_xres, d_y = sem("d_post"), sem("d_xres"), sem("d_y")
        consts_set, pool_step = sem("consts_set"), sem("pool_step")
        wz = sem("wz")
        sq_done, rstd_done, xs_done = sem("sq_done"), sem("rstd_done"), sem("xs_done")
        xt_full, xg_done, xhi_done, xlo_done = sem("xt_full"), sem("xg_done"), sem("xhi_done"), sem("xlo_done")
        whi_done, wlo_done = sem("whi_done"), sem("wlo_done")
        in_full = sem("in_full")
        in_free = [sem("in_free0"), sem("in_free1")]
        ring_full = sem("ring_full")
        ring_free = [sem("ring_free0"), sem("ring_free1")]
        s_full = sem("s_full")
        s_free = [sem("s_free0"), sem("s_free1")]
        act_step, dve_step = sem("act_step"), sem("dve_step")
        abs_done, ln_done, b_done, e_done, kd_sub, kd_exp = (
            sem("abs_done"), sem("ln_done"), sem("b_done"), sem("e_done"), sem("kd_sub"), sem("kd_exp"))
        zf_done, negF_done, page_scanned, fnew_done = sem("zf_done"), sem("negF_done"), sem("page_scanned"), sem("fnew_done")
        kb_moved = sem("kb_moved")
        qheads_done = sem("qheads_done")
        pool_done, kdseq_done, s0_scaled = sem("pool_done"), sem("kdseq_done"), sem("s0_scaled")
        osq_done, orstd_done, o_normed = sem("osq_done"), sem("orstd_done"), sem("o_normed")
        gexp_done = sem("gexp_done")
        qdiag_zero, qdiag_done = sem("qdiag_zero"), sem("qdiag_done")
        smax_done, sexp_done, sprob_done = sem("smax_done"), sem("sexp_done"), sem("sprob_done")
        fmax_done = sem("fmax_done")
        wohi_done, wolo_done = sem("wohi_done"), sem("wolo_done")
        yhi_done, ylo_done = sem("yhi_done"), sem("ylo_done")
        zstat_done, z_done, y_done = sem("zstat_done"), sem("z_done"), sem("y_done")

        def bank(key):
            return PS[:, 6 + RI[key] % 2, :]

        def ring_take(pe, key):
            if RI[key] >= 2:
                pe.wait_ge(ring_free[RI[key] % 2], RI[key] // 2)
            return bank(key)

        def ring_ready(eng, key):
            eng.wait_ge(ring_full, RI[key] + 1)
            return bank(key)

        def freed(key):
            return ring_free[RI[key] % 2]

        def drained(eng, key):
            eng.wait_ge(ring_free[RI[key] % 2], RI[key] // 2 + 1)

        def chunk_psum(c):
            return PS[:, 3 * (c % 2):3 * (c % 2) + 3, 0:TH]

        def thirds(ap):
            return ap.rearrange("p (a t) -> p a t", t=TH)

        def chunk_stored(eng, c):
            eng.wait_ge(in_free[c % 2], c // 2 + 1)

        def s_slot(user):
            n = SI[user] % 2
            return PS[:, 3 * n:3 * n + 3, :].rearrange("p b t -> p (b t)")

        def s_taken(pe, user):
            if SI[user] >= 2:
                pe.wait_ge(s_free[SI[user] % 2], SI[user] // 2)

        def s_emptied(eng, user):
            eng.wait_ge(s_free[SI[user] % 2], SI[user] // 2 + 1)

        def head_rows(h):
            return slice(DK * (h % 4), DK * (h % 4) + DK)

        def group_rows(h):
            return slice(0, P) if h < 4 else slice(0, 64)

        def xcols(t):
            return [(0, P, NMETA + P * t)] if t < NTILE else [(0, NS, LP), (NS, NS + NMETA, 0)]

        def n_of(t):
            return P if t < NTILE else NS + NMETA

        def ycol(t):
            return NMETA + P * t if t < NTILE else LP

        def prev_gate(c):
            return c - 2 if c != C_FG and c != C_FG + 1 else {C_FG: C_PG + 1, C_FG + 1: C_PG}[c]

        def probsT_drain(eng, key, copy):
            _, j, h, i = key
            u = UI[("fox", j, h)]
            src = ring_ready(eng, key)
            if u < 2:
                pass
            lo, hi = 3 * i, min(3 * i + 3, j + 2)
            full = min(hi, j + 1) - lo
            ins = None
            if full:
                ins = copy(probT[:, u % 2, lo:lo + full, :], src[:, 0:P * full].rearrange("p (b q) -> p b q", q=P))
            if hi == j + 2:
                ins = copy(probT[0:NMETA, u % 2, j + 1, :], src[0:NMETA, P * full:P * full + P])
            ins.then_inc(freed(key), 1)

        XORDER = [NTILE] + list(range(NTILE))
        GROUPS = [XORDER[0:3], XORDER[3:6], XORDER[6:9]]
        block = ctx.enter_context(nc.Block())
        wdst = wr[:, :, :, :]
        w_src = a["w_in"][0].rearrange("(k p) n -> p k n", p=P)
        W_COUNT = []
        for c in range(NCHUNK):
            W_COUNT.append((W_COUNT[c - 2] if c >= 2 else 0) + 16 * len(CHUNKS[c]))

        @block.sync
        def _(sp):
            def load_x(t):
                if t < NTILE:
                    sp.dma_start(xrows[:, t, :], a["x_prompt"][0, P * t:P * t + P, :]).then_inc(d_x[t], 16)
                else:
                    sp.dma_start(xrows[0:NS, t, :], a["x_sample"].rearrange("b t n -> (b t) n")).then_inc(d_x[t], 16)
                    sp.dma_start(xrows[NS:NS + NMETA, t, :], a["meta_tokens"]).then_inc(d_x[t], 16)

            def load_w(c):
                if c == 0:
                    sp.wait_ge(wz, 1)
                if c >= 2:
                    sp.wait_ge(whi_done, c - 1)
                    sp.wait_ge(wlo_done, c - 1)
                for col, at_, n in CHUNKS[c]:
                    sp.dma_start(wr[:, c % 2, :, at_:at_ + n], w_src[:, :, col:col + n]).then_inc(d_w[c % 2], 16)

            for i, t in enumerate(XORDER):
                load_x(t)
            load_w(0)
            load_w(1)

            def outputs(c):
                if c == 1:
                    sp.wait_ge(xs_done, 9)
                    sp.wait_ge(xt_full, 9)
                    sp.dma_start(hist_rows, a["state_pool"][0].rearrange("b t c -> (b t) c")).then_inc(d_hist, 16)
                if c == 3:
                    drained(sp, ("logf_rows",))
                    sp.dma_start(o["logf_p"][0, 0, 0:P * NTILE, :].rearrange("(t p) h -> p t h", p=P),
                                 logf_t[:, 0:NTILE, :]).then_inc(d_out, 16)
                    sp.dma_start(o["logf_p"][0, 0, P * NTILE:LP, :], logf_t[0:NMETA, NTILE, :]).then_inc(d_out, 16)
                    sp.dma_start(o["logf_s"][0].rearrange("b t h -> (b t) h"),
                                 logf_t[NMETA:NMETA + NS, NTILE, :]).then_inc(d_out, 16)
                    drained(sp, ("page_prefix",))
                    for b in range(NB):
                        sp.dma_start(nf_d[b, :, 0:PAST].rearrange("h (g k) -> g h k", k=PAGE),
                                     page_F[NPAGE * b:NPAGE * b + NPAGE]).then_inc(d_nf, 16)
                    sp.wait_ge(d_nf, 16 * NB)
                    with nc.allow_non_contiguous_dma(reason="one value per head and sequence"):
                        sp.dma_start(f_last[:, :], nf_d[:, :, PAST - 1].rearrange("b h -> h b")).then_inc(d_fl, 16)
                if c == 6:
                    sp.wait_ge(fnew_done, 1)
                    sp.dma_start(nf_d[:, :, PAST:PAST + TS].rearrange("b h t -> h b t"),
                                 f_sum[:, :].rearrange("h (b t) -> h b t", t=TS)).then_inc(d_nf, 16)
                    drained(sp, ("pool_last", 0))
                    drained(sp, ("pool_last", 1))
                    sp.dma_start(o["pool_p"][0, 0], last_p).then_inc(d_pool_out, 16)
                    for b in range(NB):
                        sp.dma_start(o["pool_s"][0, b, HIST - TS:HIST, :],
                                     last_s[TS * b:TS * b + TS]).then_inc(d_pool_out, 16)
                    sp.dma_start(o["pool_s"][0, :, 0:HIST - TS, :],
                                 a["state_pool"][0, :, TS:HIST, :]).then_inc(d_out, 16)
                    sp.wait_ge(fnew_done, 1)
                    for g, n in ((0, 4), (1, 2)):
                        sp.dma_start(gstate_s[0:DK * n, g],
                                     a["state_gla"][0, :, 4 * g:4 * g + n].rearrange("b h k v -> (h k) b v")
                                     ).then_inc(d_s0, 16)
                if c == 12:
                    drained(sp, ("state", NCH))
                    for g, n in ((0, 4), (1, 2)):
                        sp.dma_start(o["gla_p"][0, 0, 4 * g:4 * g + n].rearrange("h k v -> (h k) v"),
                                     gstate[0:DK * n, NCH % 3, g, :]).then_inc(d_out, 16)
                if c == 13:
                    drained(sp, ("sample_state", 1, 1))
                    drained(sp, ("sample_state", 1, 0))
                    for g, n in ((0, 4), (1, 2)):
                        sp.dma_start(o["gla_s"][0, :, 4 * g:4 * g + n].rearrange("b h k v -> (h k) b v"),
                                     gstate_s[0:DK * n, g]).then_inc(d_state_out, 16)
                if c == 15:
                    for t in range(9):
                        drained(sp, ("k_rows", t))
                        store_rows("k", k_out, t, d_k_out)
                if c == 23:
                    for t in range(9):
                        drained(sp, ("fv_rows", t))
                        store_rows("v", VR, t, d_out)

            def store_rows(which, src, t, done):
                dp, ds = (o["fox_" + which + x].rearrange("z b t h d -> (z b t) (h d)") for x in "ps")
                if t < NTILE:
                    sp.dma_start(dp[P * t:P * t + P], src[:, t, :]).then_inc(done, 16)
                else:
                    sp.dma_start(dp[P * t:LP], src[0:NMETA, t, :]).then_inc(done, 16)
                    sp.dma_start(ds, src[NMETA:NMETA + NS, t, :]).then_inc(done, 16)

            for c in range(2, NCHUNK):
                load_w(c)
                if c >= 4:
                    outputs(c - 3)
            for c in range(NCHUNK - 3, NCHUNK):
                outputs(c)

            def load_pages(b):
                u = b % 2
                if b < 2:
                    sp.wait_ge(in_full, NCHUNK)
                    chunk_stored(sp, NCHUNK - 1)
                    drained(sp, ("fv_rows", 8))
                else:
                    sp.wait_ge(ring_full, RI[("page_kT", b - 2, NPAGE - 1)] + 1)
                regs = []
                for g in range(NPAGE):
                    i = NPAGE * b + g
                    page = sp.value_load(ptab[0:1, i:i + 1], min_val=0, max_val=a["cache_fox_k"].shape[1] - 1)
                    regs.append(page)
                    sp.dma_start(pages[u][:, 0, g, :],
                                 k_cache[bass.ds(page, 1)].rearrange("a p n -> (a p) n")).then_inc(d_k[u], 16)
                if b >= 2:
                    sp.wait_ge(ring_full, RI[("s_attend", b - 2)] + 1)
                for g in range(NPAGE):
                    i = NPAGE * b + g
                    page = sp.value_load(ptab[0:1, i:i + 1], min_val=0, max_val=a["cache_fox_k"].shape[1] - 1)
                    sp.dma_start(pages[u][:, 1, g, :],
                                 v_cache[bass.ds(page, 1)].rearrange("a p n -> (a p) n")).then_inc(d_v[u], 16)
                sp.dma_start(v_new[:, u, :], VR[NMETA + TS * b:NMETA + TS * b + TS, NTILE, :]).then_inc(d_v[u], 16)
                if b >= 2:
                    sp.wait_ge(smax_done, b - 1)
                for h in range(H):
                    sp.dma_start(sbias[TS * h:TS * h + TS, u, :],
                                 nf_d[b, h:h + 1, :].to_broadcast([TS, PAST + TS])).then_inc(d_bias[u], 16)

            k_cache = a["cache_fox_k"][0].rearrange("g p h d -> g p (h d)")
            v_cache = a["cache_fox_v"][0].rearrange("g p h d -> g p (h d)")
            sp.wait_ge(d_ptab, 16)
            sp.wait_ge(d_nf, 16 * (NB + 1))
            for b in range(NB):
                load_pages(b)

            wo_src = a["w_out"][0].rearrange("(k p) n -> k p n", p=P)
            sp.wait_ge(ring_full, RI[("s_attend", NB - 1)] + 1)
            sp.dma_start(gpost, a["norm_post"][0:1, :].to_broadcast([P, D])).then_inc(d_post, 16)
            for k in range(KT):
                if k >= 2:
                    sp.wait_ge(wohi_done, k - 1)
                    sp.wait_ge(wolo_done, k - 1)
                sp.dma_start(wo_raw[:, k % 2, :], wo_src[k]).then_inc(d_wo[k % 2], 16)
            for n, t in enumerate(PROJ):
                if n:
                    sp.wait_ge(y_done, n)
                if t < NTILE:
                    sp.dma_start(xres[:, :], a["x_prompt"][0, P * t:P * t + P, :]).then_inc(d_xres, 16)
                else:
                    sp.dma_start(xres[0:NS, :], a["x_sample"].rearrange("b t n -> (b t) n")).then_inc(d_xres, 16)
                sp.wait_ge(y_done, n + 1)
                if t < NTILE:
                    sp.dma_start(o["y_p"][0, P * t:P * t + P, :], zout[:, :]).then_inc(d_y, 16)
                else:
                    sp.dma_start(o["y_s"].rearrange("b t n -> (b t) n"), zout[0:NS, :]).then_inc(d_y, 16)
            sp.wait_ge(d_y, 16 * len(PROJ))
            sp.wait_ge(d_k_out, 16 * 10)
            sp.wait_ge(d_state_out, 32)
            sp.wait_ge(d_pool_out, 16 * (NB + 1))
            sp.wait_ge(d_out, 16 * (3 + 1 + 2 + 10))

        @block.gpsimd
        def _(pool):
            g = pool
            n = [0]

            def link(ins):
                n[0] += 1
                ins.then_inc(pool_step, 1)
                g.wait_ge(pool_step, n[0])

            link(g.memset(wr[:, 0, :, :], 0.0))
            g.sem_inc(wz, 1) if False else g.memset(eps[:, :], EPS).then_inc(wz, 1)

            def keep(ap, pattern, base, mult, fill=0.0, op=ALU.is_ge):
                link(g.affine_select(out=ap, in_=ap, compare_op=op, fill=fill, base=base, pattern=pattern,
                                     channel_multiplier=mult))

            g.dma_start(pidx[:, :], a["page_table"].rearrange("b (g a) -> (b g) a", a=1)).then_inc(d_idx, 16)
            g.dma_start(ptab[:, :], a["page_table"].rearrange("(a b) g -> a (b g)", a=1)).then_inc(d_ptab, 16)
            link(g.memset(one[:, :], 1.0))
            for m in (ident, identb):
                link(g.memset(m[:, :], 0.0))
                keep(m[:, :], [[-1, P]], 0, 1, 1.0, ALU.not_equal)
            link(g.memset(block_mean[:, :], 0.0))
            for r in (slice(0, 64), slice(64, P)):
                link(g.memset(block_mean[r, r], 1.0 / DV))
            link(g.memset(causal[:, :], 1.0))
            keep(causal[:, :], [[1, CH]], CH, -1)
            keep(causal[0:CH, :], [[1, CH]], 0, -1)
            link(g.memset(causal_s[:, :], 1.0))
            cs = causal_s[:, :].rearrange("p (b t) -> p b t", t=TS)
            keep(cs, [[TS, NB], [1, TS]], 0, -1)
            keep(cs, [[-TS, NB], [0, TS]], 0, 1)
            link(g.memset(same_seq[:, :], 1.0))
            keep(same_seq[:, :], [[-TS, NB]], 0, 1)
            keep(same_seq[:, :], [[TS, NB]], TS - 1, -1)
            link(g.memset(head_of[:, :], 1.0))
            keep(head_of[:, :], [[-DK, 4]], 0, 1)
            keep(head_of[:, :], [[DK, 4]], DK - 1, -1)
            link(g.memset(page_before[:, :], 1.0))
            pb = page_before[:, :].rearrange("p (b g) -> p b g", g=NPAGE)
            keep(pb, [[-NPAGE, NB], [0, NPAGE]], 0, 1)
            keep(pb, [[NPAGE, NB], [1, NPAGE]], -1, -1)
            link(g.memset(pick_row[:, :, :], 0.0))
            for q in range(3):
                keep(pick_row[:, :, :], [[-1, H], [0, P]], -32 * q, 1, 1.0, ALU.not_equal)
            link(g.memset(mask_neg[:, :], 0.0))
            keep(mask_neg[:, :], [[-1, P]], 0, 1, NEG)
            link(g.memset(mask_new[:, :], 0.0))
            keep(mask_new[:, :], [[-1, TS]], 0, 1, NEG)
            link(g.memset(pick_q[:, :], 0.0))
            keep(pick_q[:, :].rearrange("p (h q) -> p h q", q=TS), [[0, H], [1, TS]], 0, -1, 1.0, ALU.not_equal)
            link(g.memset(pool_w[:, :, :], 0.0))
            link(g.memset(negF[:, :], 0.0))
            g.memset(one[:, :], 1.0).then_inc(consts_set, 1)
            for i in range(4):
                r = slice(64 * (i % 2), 64 * (i % 2) + 64)
                g.dma_start(pool_w[r, i // 2, r], a["pool_w"][0, i]).then_inc(d_poolw, 16)

            def w_low(c):
                g.wait_ge(d_w[c % 2], W_COUNT[c])
                g.wait_ge(whi_done, c + 1)
                if c >= 2:
                    g.wait_ge(in_full, c - 1)
                g.tensor_tensor(wl[:, c % 2], wr[:, c % 2], wh[:, c % 2].bitcast(F32), ALU.subtract
                                ).then_inc(wlo_done, 1)

            for i, t in enumerate(XORDER):
                g.wait_ge(xhi_done, i + 1)
                for r0, r1, col in xcols(t):
                    ins = g.tensor_tensor(xl[:, :, col:col + r1 - r0], xg[:, i % 3, :, r0:r1],
                                          xh[:, :, col:col + r1 - r0].bitcast(F32), ALU.subtract)
                ins.then_inc(xlo_done, 1)
                if i == 4:
                    w_low(0)
            g.wait_ge(xt_full, 9)
            link(g.memset(reset, 1.0))
            link(g.memset(reset[:, 0:1], 0.0))
            link(g.memset(reset[:, NMETA:LP].rearrange("p (c t) -> p c t", t=CH)[:, :, 0:1], 0.0))
            link(g.memset(reset[:, LP:NT].rearrange("p (c t) -> p c t", t=TS)[:, :, 0:1], 0.0))
            g.memset(ones_row, 1.0).then_inc(consts_set, 1)
            w_low(1)
            g.wait_ge(d_idx, 16)
            g.indirect_dma_start(QK[0:NS, 3, 0:PAGE * H], None,
                                 a["cache_fox_logf"][0].rearrange("g p h -> g (p h)"),
                                 bass.IndirectOffsetOnAxis(ap=pidx[:, 0:1], axis=0)).then_inc(d_lf, 16)
            for c in range(2, NCHUNK):
                w_low(c)
            g.wait_ge(in_full, NCHUNK)
            g.memset(q_diag[:, :, :, :], 0.0).then_inc(qdiag_zero, 1)
            for k in range(KT):
                g.wait_ge(wohi_done, k + 1)
                g.tensor_tensor(wol[:, k, :], wo_raw[:, k % 2, :], woh[:, k, :].bitcast(F32), ALU.subtract
                                ).then_inc(wolo_done, 1)
            for n_, t in enumerate(PROJ):
                g.wait_ge(yhi_done, n_ + 1)
                m = P if t < NTILE else NS
                g.tensor_tensor(yl[:, :, 0:m], Y[:, :, ycol(t):ycol(t) + m], yh[:, :, 0:m].bitcast(F32),
                                ALU.subtract).then_inc(ylo_done, 1)

        @block.scalar
        def _(act):
            n = [0]

            def link(ins):
                n[0] += 1
                ins.then_inc(act_step, 1)
                act.wait_ge(act_step, n[0])

            for dst, src in ((gpre[:, :], a["norm_pre"][0].rearrange("(k p) -> p k", p=P)),
                             (bgate[:, 0:1], a["gla_b_gate"][0, 0:P].rearrange("(p a) -> p a", a=1)),
                             (bgate[0:64, 1:2], a["gla_b_gate"][0, P:].rearrange("(p a) -> p a", a=1)),
                             (gnorm[0:DV, :], a["gla_norm"][0].rearrange("(p a) -> p a", a=1)),
                             (gnorm[DV:P, :], a["gla_norm"][0].rearrange("(p a) -> p a", a=1)),
                             (pscale[:, :], a["pool_scale"][0].rearrange("(i p) -> p i", p=P)),
                             (bfox[:, :], a["fox_b_f"][0].rearrange("(p a) -> p a", a=1)),
                             (w_up[:, :], a["gla_w_up"][0])):
                with nc.allow_non_contiguous_dma(reason="small vectors, one value per partition"):
                    act.dma_start(dst, src).then_inc(d_const, 16)

            act.wait_ge(wz, 1)
            act.wait_ge(consts_set, 1)
            done = 0
            for grp in GROUPS:
                for t in grp:
                    act.wait_ge(d_x[t], 16 if t < NTILE else 32)
                    m = n_of(t)
                    act.activation(xg[0:m, 0, :, :].rearrange("p k t -> p (k t)"), xrows[0:m, t, :], ACT.Square,
                                   accum_out=ssq[0:m, t:t + 1]).then_inc(sq_done, 1)
                    done += 1
                    act.wait_ge(sq_done, done)
                for t in grp:
                    m = n_of(t)
                    link(act.activation(ssq[0:m, t:t + 1], ssq[0:m, t:t + 1], ACT.Ln, bias=eps[0:m, :], scale=1.0 / D))
                for t in grp:
                    m = n_of(t)
                    act.activation(ssq[0:m, t:t + 1], ssq[0:m, t:t + 1], ACT.Exp, scale=-0.5).then_inc(rstd_done, 1)

            def x_high(i):
                t = XORDER[i]
                act.wait_ge(xg_done, i + 1)
                for r0, r1, col in xcols(t):
                    ins = act.activation(xh[:, :, col:col + r1 - r0], xg[:, i % 3, :, r0:r1], ACT.Copy)
                ins.then_inc(xhi_done, 1)

            def w_high(c):
                if c >= NCHUNK:
                    return
                act.wait_ge(d_w[c % 2], W_COUNT[c])
                if c >= 2:
                    act.wait_ge(in_full, c - 1)
                act.activation(wh[:, c % 2], wr[:, c % 2], ACT.Copy).then_inc(whi_done, 1)

            for i in range(9):
                x_high(i)
                if i == 2:
                    w_high(0)
            w_high(1)

            def drain(key):
                kind = key[0]
                if kind == "gate":
                    _, g, t = key
                    r = P if g == 0 else 64
                    src = ring_ready(act, key)
                    act.activation(E[0:r, g, TH * t:TH * t + TH], src[0:r, 0:TH], ACT.Identity,
                                   bias=bgate[0:r, g:g + 1]).then_inc(freed(key), 1)
                elif kind == "logf_rows":
                    src = ring_ready(act, key)
                    act.activation(logf_t[:, 0:NTILE, :], src[:, 0:NTILE * H].rearrange("p (t h) -> p t h", h=H), ACT.Copy)
                    act.activation(logf_t[0:NMETA + NS, NTILE, :], src[0:NMETA + NS, NTILE * H:9 * H],
                                   ACT.Copy).then_inc(freed(key), 1)
                elif kind == "v_rows":
                    b = key[1]
                    m = GBLOCKS[b][1]
                    src = ring_ready(act, key)
                    act.activation(VR[0:m, b, :], src[0:m, 0:384], ACT.Copy).then_inc(freed(key), 1)
                elif kind == "pool_last":
                    i = key[1]
                    src = ring_ready(act, key)
                    act.activation(last_p[:, P * i:P * i + P], src[0:HIST, 0:P], ACT.Copy)
                    act.activation(last_s[:, P * i:P * i + P], src[0:NS, P:2 * P], ACT.Copy).then_inc(freed(key), 1)
                elif kind == "pool":
                    _, i, q = key
                    col, m = PIECES[q]
                    src = ring_ready(act, key)
                    if (i, q) == (1, 0):
                        drained(act, ("hist",))
                    act.activation(Y[:, 3 + i, col:col + m], src[:, 0:m], ACT.Copy,
                                   scale=pscale[:, i:i + 1]).then_inc(freed(key), 1)
                elif kind == "kd_rows":
                    i = key[1]
                    src = ring_ready(act, key)
                    if i < 4:
                        act.activation(kd_rows[:, 2 * i:2 * i + 2, :],
                                       src[:, 0:384].rearrange("p (b n) -> p b n", b=2), ACT.Copy).then_inc(freed(key), 1)
                    else:
                        act.activation(kd_rows[0:NS, 8, :], src[0:NS, 0:192], ACT.Copy)
                        act.activation(kd_meta, src[0:NMETA, 192:384], ACT.Copy).then_inc(freed(key), 1)
                elif kind == "out":
                    j = key[1]
                    src = ring_ready(act, key)
                    if j == 0:
                        act.wait_ge(d_pool_out, 16 * (NB + 1))
                    act.activation(Y[:, 0:3, NMETA + P * j:NMETA + P * j + P],
                                   src[:, 0:384].rearrange("p (g t) -> p g t", g=3), ACT.Copy).then_inc(freed(key), 1)
                elif kind == "sample_out":
                    src = ring_ready(act, key)
                    act.activation(Y[:, 0:3, LP:NT], src[:, 0:192].rearrange("p (g t) -> p g t", g=3),
                                   ACT.Copy).then_inc(freed(key), 1)
                elif kind == "meansq":
                    _, i, q = key
                    col, m = PIECES[q]
                    src = ring_ready(act, key)
                    act.activation(E[:, 3 + i, col:col + m], src[:, 0:m], ACT.Ln, bias=eps[:, :]).then_inc(freed(key), 1)
                elif kind in ("k_rows", "fv_rows"):
                    t = key[1]
                    dst = k_out if kind == "k_rows" else VR
                    m = P if t < NTILE else NMETA + NS
                    src = ring_ready(act, key)
                    if key == ("k_rows", 0):
                        act.wait_ge(o_normed, 3)
                    act.activation(dst[0:m, t, :], src[0:m, 0:384], ACT.Copy).then_inc(freed(key), 1)

            def store(c):
                src = chunk_psum(c)
                done = in_free[c % 2]
                if c == C_LF:
                    act.wait_ge(in_full, c + 1)
                    act.activation(thirds(glr), src[0:LR], ACT.Copy)
                    act.activation(thirds(logf), src[32:32 + H], ACT.Copy).then_inc(done, 1)
                elif C_PV <= c < C_PV + 2:
                    act.wait_ge(in_full, c + 1)
                    if c == C_PV:
                        act.wait_ge(b_done, 1)
                    else:
                        act.wait_ge(pool_done, 1)
                    act.activation(thirds(pv), src, ACT.Copy).then_inc(done, 1)
                elif c == C_QKB:
                    act.wait_ge(in_full, c + 1)
                    act.activation(thirds(QK[0:64, 4, :]), src[64:P], ACT.Copy).then_inc(kb_moved, 1)
                elif C_FK <= c < C_FK + 3:
                    act.wait_ge(in_full, c + 1)
                    act.activation(thirds(QK[:, c - C_FK, :]), src, ACT.Copy).then_inc(done, 1)
                elif C_FQ <= c < C_FQ + 3:
                    act.wait_ge(in_full, c + 1)
                    if c == C_FQ + 2:
                        act.wait_ge(d_state_out, 32)
                    act.activation(thirds(QK[:, 3 + c - C_FQ, :]), src, ACT.Copy, scale=HD ** -0.5).then_inc(done, 1)
                elif C_GG <= c < C_PG + 2 or c >= C_FG:
                    act.wait_ge(in_full, c + 1)
                    act.wait_ge(o_normed, 3)
                    if c >= C_GG + 2:
                        chunk_stored(act, prev_gate(c))
                    act.activation(thirds(gtmp[c % 2]), src, ACT.Exp, scale=-1.0).then_inc(gexp_done, 1)
                elif C_FV <= c < C_FV + 3:
                    act.wait_ge(in_full, c + 1)
                    if c == C_FV:
                        act.wait_ge(d_k_out, 16 * 10)
                    act.activation(thirds(E[:, c - C_FV, :]), src, ACT.Copy).then_inc(done, 1)

            def extra(c):
                if c == 1:
                    act.wait_ge(zf_done, 1)
                    for t in range(3):
                        drained(act, ("gate", 1, t))
                        drained(act, ("gate", 0, t))
                    parts = [(E[:, 0, :], E[:, 2, :]), (E[0:64, 1, :], E[0:64, 3, :]), (logf, ftmp)]
                    for z, t in parts:
                        act.activation(t, z, ACT.Abs).then_inc(abs_done, 1)
                    act.wait_ge(abs_done, 3)
                    for z, t in parts:
                        link(act.activation(t, t, ACT.Exp, scale=-1.0))
                    for (z, t), r in zip(parts, (P, 64, H)):
                        act.activation(t, t, ACT.Ln, bias=one[0:r, :]).then_inc(ln_done, 1)
                    act.wait_ge(b_done, 1)
                    for g, r in ((0, P), (1, 64)):
                        act.activation(E[0:r, g, :], E[0:r, 4 + g, :], ACT.Exp, scale=GATE)
                        act.activation(E[0:r, 2 + g, :], E[0:r, 4 + g, :], ACT.Exp, scale=-GATE).then_inc(e_done, 1)
                    act.wait_ge(kd_sub, 1)
                    for g, r in ((0, P), (1, 64)):
                        act.activation(E[0:r, 4 + g, :], E[0:r, 4 + g, :], ACT.Exp, scale=GATE)
                        act.activation(ebend[0:r, g, :], ebend[0:r, g, :], ACT.Exp, scale=GATE).then_inc(kd_exp, 1)
                if c == 13:
                    drained(act, ("sample_out",))
                    drained(act, ("out", 7))
                    for i in range(3):
                        act.activation(E[:, i, NMETA:NT], Y[:, i, NMETA:NT], ACT.Square).then_inc(osq_done, 1)
                if c == 14:
                    for q in range(3):
                        drained(act, ("meansq", 2, q))
                    for i in range(3):
                        act.activation(E[:, 3 + i, NMETA:NT], E[:, 3 + i, NMETA:NT], ACT.Exp,
                                       scale=-0.5).then_inc(orstd_done, 1)

            for c in range(1, NCHUNK + 1):
                for key in SIDE[c - 1]:
                    drain(key)
                extra(c - 1)
                w_high(c + 1)
                store(c - 1)

            def page_kT(b, g):
                key = ("page_kT", b, g)
                src = ring_ready(act, key)
                act.activation(kT[:, b % 2, :, PAGE * g:PAGE * g + PAGE],
                               src[:, 0:384].rearrange("p (g t) -> p g t", g=3), ACT.Copy).then_inc(freed(key), 1)

            def s_exp(b):
                r = H * TS
                act.wait_ge(smax_done, b + 1)
                act.activation(sprob[:, b % 2, :], sprob[:, b % 2, :], ACT.Exp, bias=nmax[0:r, b % 2:b % 2 + 1],
                               accum_out=rsum[0:r, b % 2:b % 2 + 1]).then_inc(sexp_done, 1)

            for b in range(NB + 1):
                if b < NB:
                    for g in range(1, NPAGE, 2):
                        page_kT(b, g)
                    s_exp(b)

            def wo_high(k):
                act.wait_ge(d_wo[k % 2], 16 * (k // 2 + 1))
                act.activation(woh[:, k, :], wo_raw[:, k % 2, :], ACT.Copy).then_inc(wohi_done, 1)

            wo_next = [0]
            for kind, key in PLAN:
                if kind == "S" and key[0] == "fox":
                    _, j, h = key
                    m = NMETA + P * (j + 1)
                    u = UI[key]
                    act.wait_ge(fmax_done, u + 1)
                    if u >= 2:
                        _, pj, ph = UNITS[u - 2]
                        act.wait_ge(ring_full, RI[("probsT", pj, ph, (pj + 4) // 3 - 1)] + 1)
                    else:
                        act.wait_ge(ring_full, RI[("s_attend", NB - 1)] + 1)
                    act.activation(prob[:, u % 2, 0:m], s_slot(key)[:, 0:m], ACT.Exp, bias=nmax[:, 2 + u % 2:3 + u % 2],
                                   accum_out=rsum[:, 2 + u % 2:3 + u % 2]).then_inc(s_free[SI[key] % 2], 1)
                    if wo_next[0] < KT and u >= 1:
                        wo_high(wo_next[0])
                        wo_next[0] += 1
                elif kind == "R" and key[0] == "probsT" and key[3] % 2:
                    probsT_drain(act, key, lambda out, in_: act.activation(out, in_, ACT.Copy))
                elif kind == "S":
                    t = key[1]
                    n_ = PROJ.index(t)
                    m = P if t < NTILE else NS
                    if t < NTILE:
                        drained(act, ("foxT", t))
                    else:
                        drained(act, ("s_attend", NB - 1))
                    if n_:
                        act.wait_ge(s_full, SI[("proj", PROJ[n_ - 1])] + 1)
                    act.activation(yh[:, :, 0:m], Y[:, :, ycol(t):ycol(t) + m], ACT.Copy).then_inc(yhi_done, 1)
                    act.wait_ge(s_full, SI[key] + 1)
                    if n_:
                        act.wait_ge(d_y, 16 * n_)
                    link(act.activation(zout[0:m, :], s_slot(key)[0:m, 0:D], ACT.Square, accum_out=zstat[0:m, 0:1]))
                    link(act.activation(zstat[0:m, 0:1], zstat[0:m, 0:1], ACT.Ln, bias=eps[0:m, :], scale=1.0 / D))
                    act.activation(zstat[0:m, 1:2], zstat[0:m, 0:1], ACT.Exp, scale=-0.5).then_inc(zstat_done, 1)

        @block.vector
        def _(dve):
            n = [0]

            def link(ins):
                n[0] += 1
                ins.then_inc(dve_step, 1)
                dve.wait_ge(dve_step, n[0])

            def x_scale(i):
                t = XORDER[i]
                m = n_of(t)
                dve.wait_ge(rstd_done, i + 1)
                dve.tensor_scalar(xrows[0:m, t, :], xrows[0:m, t, :], ssq[0:m, t:t + 1], None, ALU.mult
                                  ).then_inc(xs_done, 1)

            def x_pre(i):
                m = n_of(XORDER[i])
                u = 2 * i % 8
                dve.wait_ge(xt_full, i + 1)
                if i >= 3:
                    dve.wait_ge(xlo_done, i - 2)
                else:
                    dve.wait_ge(sq_done, 9)
                src = PS[:, u:u + 2, :].rearrange("p b (k t) -> p (b k) t", t=P)[:, :, 0:m]
                dve.tensor_tensor(xg[:, i % 3, :, 0:m], src, gpre[:, :, None].to_broadcast([P, KT, m]), ALU.mult
                                  ).then_inc(xg_done, 1)

            dve.wait_ge(d_const, 16 * 8)
            for i in range(2):
                x_scale(i)
            for i in range(9):
                if i + 2 < 9:
                    x_scale(i + 2)
                x_pre(i)

            def split_heads(j):
                c0, m = GBLOCKS[j]
                if j >= 2:
                    dve.wait_ge(ring_full, RI[("out", j - 2)] + 1)
                for g, r, n_ in ((0, P, 4), (1, 64, 2)):
                    ins = dve.tensor_tensor(q_heads[j % 2][0:r, 4 * g:4 * g + n_, 0:m],
                                            E[0:r, g, c0:c0 + m][:, None, :].to_broadcast([r, n_, m]),
                                            head_of[0:r, 0:n_, None].to_broadcast([r, n_, m]), ALU.mult)
                ins.then_inc(qheads_done, 1)

            def drain(key):
                kind = key[0]
                if kind == "page_prefix":
                    src = ring_ready(dve, key)
                    dve.wait_ge(page_scanned, H)
                    dve.scalar_tensor_tensor(out=page_F, in0=page_F, scalar=-1.0,
                                             in1=src[0:NS, 0:H, None].to_broadcast([NS, H, PAGE]),
                                             op0=ALU.mult, op1=ALU.subtract).then_inc(freed(key), 1)
                elif kind == "hist":
                    src = ring_ready(dve, key)
                    for i in range(2):
                        ins = dve.tensor_copy(hx[i][:, :, 0:HIST], src[:, 128 * i:128 * i + NB * HIST].rearrange(
                            "p (b t) -> p b t", b=NB))
                    ins.then_inc(freed(key), 1)
                elif kind == "state":
                    c = key[1]
                    src = ring_ready(dve, key)
                    if c >= 3 and c % 2:
                        split_heads((c + 1) // 2)
                    if c == 0:
                        dve.tensor_copy(gstate[:, 0, 0, :], src[:, 0:DV])
                        dve.tensor_copy(gstate[0:64, 0, 1, :], src[0:64, DV:2 * DV]).then_inc(freed(key), 1)
                        return
                    drained(dve, ("state", c - 1))
                    for g, r in ((0, P), (1, 64)):
                        ins = dve.scalar_tensor_tensor(out=gstate[0:r, c % 3, g, :], in0=gstate[0:r, (c - 1) % 3, g, :],
                                                       scalar=ebend[0:r, g, c:c + 1], in1=src[0:r, DV * g:DV * g + DV],
                                                       op0=ALU.mult, op1=ALU.add)
                    ins.then_inc(freed(key), 1)
                elif kind == "scores":
                    j = key[1]
                    src = ring_ready(dve, key)
                    for i in range(2):
                        r = slice(CH * i, CH * i + CH)
                        ins = dve.tensor_tensor(aT[r, j % 2, :, r], src[r, 0:384].rearrange("p (h t) -> p h t", h=H),
                                                causal[r, None, :].to_broadcast([CH, H, CH]), ALU.mult)
                    ins.then_inc(freed(key), 1)
                elif kind == "sample_scores":
                    src = ring_ready(dve, key)
                    dve.tensor_tensor(aT[0:NS, 0, :, 0:NS], src[0:NS, 0:384].rearrange("p (h t) -> p h t", h=H),
                                      causal_s[:, None, :].to_broadcast([NS, H, NS]), ALU.mult).then_inc(freed(key), 1)
                    dve.tensor_tensor(kd_seq, kd_rows[0:NS, 8:9, :].to_broadcast([NS, NB, 192]),
                                      same_seq[:, :, None].to_broadcast([NS, NB, 192]), ALU.mult).then_inc(kdseq_done, 1)
                elif kind == "sample_state":
                    _, g, i = key
                    r = P if g == 0 else 64
                    src = ring_ready(dve, key)
                    if (g, i) == (0, 0):
                        for gg, rr in ((0, P), (1, 64)):
                            dve.tensor_tensor(gstate_s[0:rr, gg], gstate_s[0:rr, gg],
                                              ebend[0:rr, gg, 17:25, None].to_broadcast([rr, NB, DV]),
                                              ALU.mult).then_inc(s0_scaled, 1)
                        dve.wait_ge(s0_scaled, 2)
                    part = gstate_s[0:r, g, 4 * i:4 * i + 4, :]
                    dve.tensor_tensor(part, part, src[0:r, 0:4 * DV].rearrange("p (b v) -> p b v", v=DV),
                                      ALU.add).then_inc(freed(key), 1)

            def store(c):
                src = chunk_psum(c)
                done = in_free[c % 2]
                if C_GV <= c < C_GV + 3:
                    dve.wait_ge(in_full, c + 1)
                    dve.tensor_copy(thirds(Y[:, c - C_GV, :]), src).then_inc(done, 1)
                elif c == C_GKA:
                    dve.wait_ge(in_full, c + 1)
                    dve.wait_ge(kd_exp, 2)
                    dve.tensor_tensor(thirds(E[:, 2, :]), thirds(E[:, 2, :]), src, ALU.mult)
                    dve.tensor_tensor(thirds(E[:, 4, :]), thirds(E[:, 4, :]), src, ALU.mult).then_inc(done, 1)
                elif c == C_GQA:
                    dve.wait_ge(in_full, c + 1)
                    dve.scalar_tensor_tensor(out=thirds(E[:, 0, :]), in0=src, scalar=DK ** -0.5,
                                             in1=thirds(E[:, 0, :]), op0=ALU.mult, op1=ALU.mult).then_inc(done, 1)
                elif c == C_QKB:
                    dve.wait_ge(in_full, c + 1)
                    dve.wait_ge(kb_moved, 1)
                    kb = QK[0:64, 4, :]
                    dve.tensor_tensor(E[0:64, 3, :], E[0:64, 3, :], kb, ALU.mult)
                    dve.tensor_tensor(E[0:64, 5, :], E[0:64, 5, :], kb, ALU.mult)
                    dve.scalar_tensor_tensor(out=thirds(E[0:64, 1, :]), in0=src[0:64], scalar=DK ** -0.5,
                                             in1=thirds(E[0:64, 1, :]), op0=ALU.mult, op1=ALU.mult).then_inc(done, 1)
                elif C_GG <= c < C_PG + 2 or c >= C_FG:
                    gates = [x for x in range(NCHUNK) if C_GG <= x < C_PG + 2 or x >= C_FG]
                    g = gtmp[c % 2]
                    dve.wait_ge(gexp_done, gates.index(c) + 1)
                    link(dve.tensor_scalar(g, g, 1.0, None, ALU.add))
                    link(dve.reciprocal(g, g))
                    if c < C_FG:
                        y = Y[:, c - C_GG, NMETA:NT]
                        link(dve.tensor_tensor(thirds(g), src, thirds(g), ALU.mult))
                        if c >= C_PG:
                            drained(dve, ("pool", 1, 2))
                            drained(dve, ("pool", 1, 1))
                        dve.tensor_tensor(y, y, g[:, NMETA:NT], ALU.mult).then_inc(done, 1)
                    else:
                        dve.tensor_tensor(thirds(Y[:, 5 + c - C_FG, :]), src, thirds(g), ALU.mult).then_inc(done, 1)

            def pool_windows(i):
                chunk_stored(dve, C_PV + i)
                if i == 0:
                    drained(dve, ("hist",))
                link(dve.tensor_copy(hx[i][:, :, HIST:HX], pv[:, LP:NT].rearrange("p (b t) -> p b t", t=TS)))
                if i == 1:
                    dve.wait_ge(ring_full, RI[("pool", 0, 2)] + 1)
                views = []
                for v, pa, pb_, lead, n_ in ((pv, psA, psB, 1, LP), (hx[i], hA, hB, 2, HX)):
                    cut = (lambda x, r, s0, s1, ld=lead: x[r, s0:s1] if ld == 1 else x[r, :, s0:s1])
                    views.append((v, pa, pb_, n_, cut))

                def add(dst, src, r, w):
                    for v, pa, pb_, n_, cut in views:
                        t = {"v": v, "a": pa, "b": pb_}
                        ins = dve.tensor_tensor(cut(t[dst], r, 2 * w - 1, n_), cut(t[src], r, 2 * w - 1, n_),
                                                cut(t[src], r, w - 1, n_ - w), ALU.add)
                    link(ins)

                every, low, high = slice(0, P), slice(0, 64), slice(64, P)
                add("a", "v", every, 1)
                if i == 0:
                    add("b", "a", high, 2)
                    ends = ((low, "a", 2), (high, "b", 4))
                else:
                    add("b", "a", every, 2)
                    add("a", "b", every, 4)
                    add("b", "a", high, 8)
                    ends = ((low, "a", 8), (high, "b", 16))
                for r, which, w in ends:
                    s = psA if which == "a" else psB
                    hs = hA if which == "a" else hB
                    dve.scalar_tensor_tensor(out=psA[r, NMETA:LP], in0=s[r, NMETA:LP], scalar=1.0 / w,
                                             in1=pv[r, NMETA:LP], op0=ALU.mult, op1=ALU.subtract)
                    ins = dve.scalar_tensor_tensor(out=psA[r, LP:NT].rearrange("p (b t) -> p b t", t=TS),
                                                   in0=hs[r, :, HIST:HX], scalar=1.0 / w, in1=hx[i][r, :, HIST:HX],
                                                   op0=ALU.mult, op1=ALU.subtract)
                ins.then_inc(pool_done, 1)

            def extra(c):
                if c == 0:
                    chunk_stored(dve, C_LF)
                    dve.tensor_scalar(logf, logf, bfox[:, 0:1], None, ALU.add).then_inc(zf_done, 1)
                if c == 1:
                    dve.wait_ge(abs_done, 3)
                    dve.wait_ge(zf_done, 1)
                    parts = [(E[:, 0, :], E[:, 2, :]), (E[0:64, 1, :], E[0:64, 3, :]), (logf, ftmp)]
                    for z, t in parts:
                        link(dve.tensor_scalar(z, z, 0.0, None, ALU.min))
                    dve.wait_ge(ln_done, 3)
                    for z, t in parts:
                        link(dve.tensor_tensor(z, z, t, ALU.subtract))
                    dve.wait_ge(consts_set, 2)
                    for g, r in ((0, P), (1, 64)):
                        b = E[0:r, 4 + g, :]
                        link(dve.tensor_tensor_scan(b, reset[0:r, :], E[0:r, g, :], 0.0, ALU.mult, ALU.add))
                        dve.tensor_copy(ebend[0:r, g, 0:1], b[:, NMETA - 1:NMETA])
                        dve.tensor_copy(ebend[0:r, g, 1:17, None],
                                        b[:, NMETA:LP].rearrange("p (c t) -> p c t", t=CH)[:, :, CH - 1:CH])
                        link(dve.tensor_copy(ebend[0:r, g, 17:25, None],
                                             b[:, LP:NT].rearrange("p (c t) -> p c t", t=TS)[:, :, TS - 1:TS]))
                    dve.tensor_tensor_scan(f_sum[:, :], reset[0:H, LP:NT], logf[:, LP:NT], 0.0, ALU.mult, ALU.add
                                           ).then_inc(b_done, 1)
                    link(dve.tensor_tensor_scan(fcum[:, 0:LP], ones_row[0:H, :], logf[:, 0:LP], 0.0, ALU.mult, ALU.add))
                    dve.wait_ge(e_done, 2)
                    for g, r in ((0, P), (1, 64)):
                        for s, e_, c0, c1, w in ((0, NMETA, 0, 1, NMETA), (NMETA, LP, 1, 17, CH), (LP, NT, 17, 25, TS)):
                            b = E[0:r, 4 + g, s:e_].rearrange("p (c t) -> p c t", t=w)
                            ins = dve.tensor_tensor(b, ebend[0:r, g, c0:c1, None].to_broadcast([r, c1 - c0, w]), b,
                                                    ALU.subtract)
                    ins.then_inc(kd_sub, 1)
                    f, r1 = fcum[:, 0:LP], ftmp[:, 0:LP]
                    link(dve.tensor_scalar(negF[0:H, :], f, -1.0, None, ALU.mult))
                    link(dve.scalar_tensor_tensor(out=r1, in0=f, scalar=-1.0, in1=negF[0:H, :], op0=ALU.mult,
                                                  op1=ALU.subtract))
                    link(dve.tensor_copy(negF[32:32 + H, :], r1))
                    link(dve.tensor_copy(f, negF[32:32 + H, :]))
                    link(dve.tensor_tensor(r1, r1, f, ALU.subtract))
                    dve.tensor_copy(negF[64:64 + H, :], r1).then_inc(negF_done, 1)
                if c == 2:
                    dve.wait_ge(d_lf, 16)
                    for h in range(H):
                        dve.tensor_tensor_scan(page_F[:, h, :], ones_row[:, 0:PAGE], page_lf[:, :, h], 0.0,
                                               ALU.mult, ALU.add).then_inc(page_scanned, 1)
                if c == C_QKB:
                    dve.wait_ge(in_free[0], C_QKB // 2 + 1)
                    for x in (gstate[64:P, :, 1, :], gstate_s[64:P, 1], q_heads[0][64:P, 4:H, :], q_heads[1][64:P, 4:H, :]):
                        dve.memset(x, 0.0)
                    dve.wait_ge(ring_full, RI[("pool", 1, 2)] + 1)
                    dve.memset(aT[:, :, :, :], 0.0)
                    split_heads(0)
                    split_heads(1)
                if c in (C_PV, C_PV + 1):
                    pool_windows(c - C_PV)
                if c == C_PV + 1:
                    dve.wait_ge(d_fl, 16)
                    fs = f_sum[:, :].rearrange("h (b t) -> h b t", t=TS)
                    dve.tensor_tensor(fs, f_last[:, :, None].to_broadcast([H, NB, TS]), fs, ALU.subtract
                                      ).then_inc(fnew_done, 1)
                if c == 14:
                    dve.wait_ge(orstd_done, 3)
                    for i in range(3):
                        y = Y[:, i, NMETA:NT]
                        dve.scalar_tensor_tensor(out=y, in0=y, scalar=gnorm[:, 0:1], in1=E[:, 3 + i, NMETA:NT],
                                                 op0=ALU.mult, op1=ALU.mult).then_inc(o_normed, 1)
                    dve.wait_ge(o_normed, 3)

            for c in range(1, NCHUNK + 1):
                for key in SIDE[c - 1]:
                    drain(key)
                if c - 1 in (1, 14):
                    extra(c - 1)
                store(c - 1)
                if c - 1 not in (1, 14):
                    extra(c - 1)

            dve.wait_ge(qdiag_zero, 1)
            for p_ in range(3):
                for i in range(2):
                    r = slice(64 * i, 64 * i + 64)
                    col = 16 * p_ + TS * i
                    ins = dve.tensor_copy(q_diag[r, p_, :, col:col + TS],
                                          QK[r, 3 + p_, LP:NT].rearrange("p (b t) -> p b t", t=TS))
            ins.then_inc(qdiag_done, 1)

            def s_softmax(b):
                u, r = b % 2, H * TS
                dve.wait_ge(s_full, SI[("seq", b)] + 1)
                dve.wait_ge(d_bias[u], 16 * H * (b // 2 + 1))
                if b >= 2:
                    dve.wait_ge(ring_full, RI[("s_probsT", b - 2)] + 1)
                dve.tensor_tensor_reduce(sprob[:, u, :], s_slot(("seq", b))[0:r, 0:PAST + TS], sbias[:, u, :], 1.0,
                                         -3e38, ALU.add, ALU.max, nmax[0:r, 2 + u:3 + u]
                                         ).then_inc(s_free[SI[("seq", b)] % 2], 1)
                dve.wait_ge(s_free[SI[("seq", b)] % 2], SI[("seq", b)] // 2 + 1)
                dve.tensor_scalar(nmax[0:r, u:u + 1], nmax[0:r, 2 + u:3 + u], -1.0, None, ALU.mult
                                  ).then_inc(smax_done, 1)

            def s_normalise(b):
                u, r = b % 2, H * TS
                dve.wait_ge(sexp_done, b + 1)
                link(dve.reciprocal(rinv[0:r, u:u + 1], rsum[0:r, u:u + 1]))
                dve.tensor_scalar(sprob[:, u, :], sprob[:, u, :], rinv[0:r, u:u + 1], None, ALU.mult
                                  ).then_inc(sprob_done, 1)

            def page_kT(b, g):
                key = ("page_kT", b, g)
                src = ring_ready(dve, key)
                dve.tensor_copy(kT[:, b % 2, :, PAGE * g:PAGE * g + PAGE],
                                src[:, 0:384].rearrange("p (g t) -> p g t", g=3)).then_inc(freed(key), 1)

            for b in range(NB + 1):
                if b < NB:
                    for g in range(0, NPAGE, 2):
                        page_kT(b, g)
                if b:
                    key = ("s_probsT", b - 1)
                    u = (b - 1) % 2
                    src = ring_ready(dve, key)
                    dve.tensor_copy(sprobT[:, u, 0:NPAGE, :], src[:, 0:384].rearrange("p (g q) -> p g q", g=NPAGE))
                    dve.tensor_copy(sprobT[0:TS, u, NPAGE, :], src[0:TS, 384:432]).then_inc(freed(key), 1)
                    key = ("s_attend", b - 1)
                    src = ring_ready(dve, key)
                    c0 = LP + TS * (b - 1)
                    for i in range(2):
                        r = slice(64 * i, 64 * i + 64)
                        y = Y[r, 5:8, c0:c0 + TS]
                        ins = dve.tensor_tensor(y, y, src[r, 0:48].rearrange("p (g q) -> p g q", g=3)[
                            :, :, TS * i:TS * i + TS], ALU.mult)
                    ins.then_inc(freed(key), 1)
                if b < NB:
                    s_softmax(b)
                    s_normalise(b)

            dve.wait_ge(d_post, 16)
            for kind, key in PLAN:
                if kind == "S" and key[0] == "fox":
                    _, j, h = key
                    m = NMETA + P * (j + 1)
                    u = UI[key]
                    dve.wait_ge(s_full, SI[key] + 1)
                    dve.tensor_reduce(nmax[:, 2 + u % 2:3 + u % 2], s_slot(key)[:, 0:m], AX.X, ALU.max, negate=True
                                      ).then_inc(fmax_done, 1)
                elif kind == "R" and key[0] == "probsT" and key[3] % 2 == 0:
                    probsT_drain(dve, key, dve.tensor_copy)
                elif kind == "R" and key[0] == "attend":
                    _, j, h = key
                    u = UI[("fox", j, h)]
                    s_emptied(dve, ("fox", j, h))
                    link(dve.reciprocal(rinv[:, 2 + u % 2:3 + u % 2], rsum[:, 2 + u % 2:3 + u % 2]))
                    src = ring_ready(dve, key)
                    if h == 0 and j >= 2:
                        dve.wait_ge(ring_full, RI[("foxT", j - 2)] + 1)
                    dve.tensor_scalar(fox_o[:, j % 2, HD * h:HD * h + HD], src[:, 0:HD],
                                      rinv[:, 2 + u % 2:3 + u % 2], None, ALU.mult).then_inc(freed(key), 1)
                elif kind == "R" and key[0] == "foxT":
                    j = key[1]
                    src = ring_ready(dve, key)
                    y = Y[:, 5:8, NMETA + P * j:NMETA + P * j + P]
                    dve.tensor_tensor(y, y, src[:, 0:384].rearrange("p (g t) -> p g t", g=3), ALU.mult
                                      ).then_inc(freed(key), 1)
                elif kind == "S":
                    t = key[1]
                    n_ = PROJ.index(t)
                    m = P if t < NTILE else NS
                    dve.wait_ge(zstat_done, n_ + 1)
                    dve.scalar_tensor_tensor(out=zout[0:m, :], in0=s_slot(key)[0:m, 0:D], scalar=zstat[0:m, 1:2],
                                             in1=gpost[0:m, :], op0=ALU.mult, op1=ALU.mult
                                             ).then_inc(s_free[SI[key] % 2], 1)
                    dve.wait_ge(s_free[SI[key] % 2], SI[key] // 2 + 1)
                    dve.wait_ge(d_xres, 16 * (n_ + 1))
                    dve.tensor_tensor(zout[0:m, :], zout[0:m, :], xres[0:m, :], ALU.add).then_inc(y_done, 1)

        @block.tensor
        def _(pe):
            pe.wait_ge(consts_set, 1)
            pe.wait_ge(d_const, 16 * 8)
            for i, t in enumerate(XORDER):
                u = 2 * i % 8
                m = n_of(t)
                pe.wait_ge(xs_done, i + 1)
                if i >= 4:
                    pe.wait_ge(xg_done, i - 3)
                for k in range(KT):
                    ins = pe.transpose(PS[:, u + k // 4, P * (k % 4):P * (k % 4) + m],
                                       xrows[0:m, t, P * k:P * k + P], ident[0:m, 0:m])
                ins.then_inc(xt_full, 1)

            def product(out, parts, rhs_of, start, stop):
                for k in range(KT):
                    sh, sl = parts(k)
                    mh, ml = rhs_of(k)
                    pe.matmul(out, sh, mh, start=(k == 0), stop=False)
                    pe.matmul(out, sh, ml, start=False, stop=False)
                    ins = pe.matmul(out, sl, mh, start=False, stop=(k == KT - 1))
                return ins

            def project_in(c):
                pe.wait_ge(wlo_done, c + 1)
                pe.wait_ge(whi_done, c + 1)
                if c >= 2:
                    chunk_stored(pe, c - 2)
                for t in range(3):
                    cols = slice(TH * t, TH * t + TH)
                    ins = product(PS[:, 3 * (c % 2) + t, 0:TH], lambda k: (wh[:, c % 2, k, :], wl[:, c % 2, k, :]),
                                  lambda k: (xh[:, k, cols], xl[:, k, cols]), True, True)
                ins.then_inc(in_full, 1)

            def side(key):
                kind = key[0]
                out = ring_take(pe, key)
                if kind == "gate":
                    _, g, t = key
                    if (g, t) == (0, 0):
                        chunk_stored(pe, C_LF)
                    m = P if g == 0 else 64
                    ins = pe.matmul(out[0:m, 0:TH], w_up[:, P * g:P * g + m], glr[:, TH * t:TH * t + TH],
                                    start=True, stop=True)
                elif kind == "logf_rows":
                    pe.wait_ge(b_done, 1)
                    for t in range(9):
                        m = P if t < NTILE else NMETA + NS
                        ins = pe.transpose(out[0:m, H * t:H * t + H], logf[:, P * t:P * t + m], ident[0:H, 0:H])
                elif kind == "page_prefix":
                    pe.wait_ge(page_scanned, H)
                    ins = pe.matmul(out[0:NS, 0:H], page_before[:, :], page_F[:, :, PAGE - 1], start=True, stop=True)
                elif kind == "v_rows":
                    b = key[1]
                    col, m = GBLOCKS[b]
                    if b == 0:
                        chunk_stored(pe, C_GV + 1)
                        chunk_stored(pe, C_GV + 2)
                    for i in range(3):
                        ins = pe.transpose(out[0:m, P * i:P * i + P], Y[:, i, col:col + m], ident[:, :])
                elif kind == "hist":
                    pe.wait_ge(d_hist, 16)
                    m = NB * HIST
                    for i in range(2):
                        ins = pe.transpose(out[:, 128 * i:128 * i + m], hist_rows[:, P * i:P * i + P], ident[0:m, 0:m])
                elif kind == "pool_last":
                    i = key[1]
                    chunk_stored(pe, C_PV + i)
                    pe.transpose(out[0:HIST, 0:P], pv[:, LP - HIST:LP], ident[:, :])
                    ins = pe.transpose(out[0:NS, P:2 * P], pv[:, LP:NT], ident[:, :])
                elif kind == "pool":
                    _, i, q = key
                    col, m = PIECES[q]
                    pe.wait_ge(pool_done, i + 1)
                    pe.wait_ge(d_poolw, 16 * 4)
                    ins = pe.matmul(out[:, 0:m], pool_w[:, i, :], psA[:, col:col + m], start=True, stop=True)
                elif kind == "kd_rows":
                    i = key[1]
                    if i == 0:
                        chunk_stored(pe, C_QKB)
                        chunk_stored(pe, C_GQA)
                        drained(pe, ("pool", 1, 2))
                    for n_, b in enumerate((2 * i, 2 * i + 1)):
                        col, m = GBLOCKS[b]
                        pe.transpose(out[0:m, 192 * n_:192 * n_ + P], E[:, 4, col:col + m], ident[:, :])
                        ins = pe.transpose(out[0:m, 192 * n_ + P:192 * n_ + 192], E[0:64, 5, col:col + m],
                                           ident[0:64, 0:64])
                elif kind == "state":
                    c = key[1]
                    b, r0, m = (9, 0, NMETA) if c == 0 else ((c - 1) // 2, CH * ((c - 1) % 2), CH)
                    if c == 0:
                        drained(pe, ("kd_rows", 4))
                        drained(pe, ("kd_rows", 3))
                        drained(pe, ("v_rows", 9))
                        drained(pe, ("v_rows", 8))
                    rows = slice(r0, r0 + m)
                    kd = kd_meta if c == 0 else kd_rows[rows, b, :]
                    for h in range(H):
                        ins = pe.matmul(out[head_rows(h), DV * (h // 4):DV * (h // 4) + DV],
                                        kd[:, DK * h:DK * h + DK], VR[rows, b, DV * h:DV * h + DV],
                                        start=True, stop=True)
                elif kind == "scores":
                    j = key[1]
                    pe.wait_ge(qheads_done, j + 1)
                    for i in range(2):
                        c0 = NMETA + P * j + CH * i
                        for h in range(H):
                            r = group_rows(h)
                            ins = pe.matmul(out[CH * i:CH * i + CH, CH * h:CH * h + CH], E[r, 2 + h // 4, c0:c0 + CH],
                                            q_heads[j % 2][r, h, CH * i:CH * i + CH], start=True, stop=True)
                elif kind == "out":
                    j = key[1]
                    drained(pe, ("scores", j))
                    drained(pe, ("state", 2 * j + 1))
                    drained(pe, ("state", 2 * j))
                    for h in range(H):
                        rows = slice(64 * (h % 2), 64 * (h % 2) + 64)
                        dst = out[rows, P * (h // 2):P * (h // 2) + P]
                        pe.matmul(dst, VR[:, j, DV * h:DV * h + DV], aT[:, j % 2, h, :], start=True, stop=False,
                                  skip_group_check=True)
                        for i in range(2):
                            ins = pe.matmul(dst[:, CH * i:CH * i + CH], gstate[:, (2 * j + i) % 3, h // 4, :],
                                            q_heads[j % 2][:, h, CH * i:CH * i + CH], start=False, stop=(i == 1),
                                            skip_group_check=True)
                elif kind == "sample_scores":
                    pe.wait_ge(qheads_done, NTILE + 1)
                    for h in range(H):
                        r = group_rows(h)
                        ins = pe.matmul(out[0:NS, CH * h:CH * h + CH], E[r, 2 + h // 4, LP:NT],
                                        q_heads[0][r, h, 0:NS], start=True, stop=True)
                elif kind == "sample_out":
                    drained(pe, ("sample_scores",))
                    pe.wait_ge(d_s0, 32)
                    for h in range(H):
                        rows, c0 = slice(64 * (h % 2), 64 * (h % 2) + 64), NS * (h // 2)
                        pe.matmul(out[rows, c0:c0 + NS], VR[0:NS, 8, DV * h:DV * h + DV], aT[0:NS, 0, h, 0:NS],
                                  start=True, stop=False, skip_group_check=True)
                        for b in range(NB):
                            ins = pe.matmul(out[rows, c0 + TS * b:c0 + TS * b + TS], gstate_s[:, h // 4, b, :],
                                            q_heads[0][:, h, TS * b:TS * b + TS],
                                            start=False, stop=(b == NB - 1), skip_group_check=True)
                elif kind == "sample_state":
                    _, g, i = key
                    pe.wait_ge(kdseq_done, 1)
                    for h in range(4 * g, min(4 * g + 4, H)):
                        for b in range(4):
                            ins = pe.matmul(out[head_rows(h), DV * b:DV * b + DV],
                                            kd_seq[:, 4 * i + b, DK * h:DK * h + DK], VR[0:NS, 8, DV * h:DV * h + DV],
                                            start=True, stop=True)
                elif kind == "meansq":
                    _, i, q = key
                    col, m = PIECES[q]
                    pe.wait_ge(osq_done, i + 1)
                    ins = pe.matmul(out[:, 0:m], block_mean[:, :], E[:, i, col:col + m], start=True, stop=True)
                elif kind in ("k_rows", "fv_rows"):
                    t = key[1]
                    src = QK if kind == "k_rows" else E
                    last = C_FK if kind == "k_rows" else C_FV
                    if t == 0:
                        chunk_stored(pe, last + 1)
                        chunk_stored(pe, last + 2)
                    m = P if t < NTILE else NMETA + NS
                    for i in range(3):
                        ins = pe.transpose(out[0:m, P * i:P * i + P], src[:, i, P * t:P * t + m], ident[:, :])
                ins.then_inc(ring_full, 1)

            pe.wait_ge(xlo_done, 9)
            for c in range(NCHUNK):
                project_in(c)
                for key in SIDE[c]:
                    side(key)

            def page_kT(b, g):
                key = ("page_kT", b, g)
                out = ring_take(pe, key)
                if g == 0:
                    pe.wait_ge(d_k[b % 2], 16 * NPAGE * (b // 2 + 1))
                for i in range(3):
                    ins = pe.transpose(out[:, P * i:P * i + P], pages[b % 2][:, 0, g, P * i:P * i + P], ident[:, :])
                ins.then_inc(ring_full, 1)

            def s_scores(b):
                user = ("seq", b)
                s_taken(pe, user)
                out = s_slot(user)
                drained(pe, ("page_kT", b, NPAGE - 1))
                drained(pe, ("page_kT", b, NPAGE - 2))
                pe.wait_ge(qdiag_done, 1)
                for half in range(2):
                    for p_ in range(3):
                        pe.matmul(out[0:H * TS, 512 * half:512 * half + 512], q_diag[:, p_, b, :],
                                  kT[:, b % 2, p_, 512 * half:512 * half + 512], start=(p_ == 0), stop=(p_ == 2))
                for p_ in range(3):
                    pe.matmul(out[0:H * TS, PAST:PAST + TS], q_diag[:, p_, b, :],
                              QK[:, p_, LP + TS * b:LP + TS * b + TS], start=(p_ == 0), stop=False)
                pe.matmul(out[0:H * TS, PAST:PAST + TS], pick_q[:, :], mask_new[:, :], start=False, stop=True
                          ).then_inc(s_full, 1)

            def s_attend(b):
                u = b % 2
                key = ("s_probsT", b)
                out = ring_take(pe, key)
                pe.wait_ge(sprob_done, b + 1)
                r = H * TS
                for g in range(NPAGE):
                    pe.transpose(out[:, r * g:r * g + r], sprob[:, u, PAGE * g:PAGE * g + PAGE], ident[0:r, 0:r])
                pe.transpose(out[0:TS, 384:384 + r], sprob[:, u, PAST:PAST + TS], ident[0:r, 0:r]).then_inc(ring_full, 1)
                drained(pe, key)
                key = ("s_attend", b)
                out = ring_take(pe, key)
                pe.wait_ge(d_v[u], 16 * (NPAGE + 1) * (b // 2 + 1))
                for p_ in range(3):
                    cols, qs = slice(P * p_, P * p_ + P), slice(16 * p_, 16 * p_ + 16)
                    for g in range(NPAGE):
                        pe.matmul(out[:, qs], pages[u][:, 1, g, cols], sprobT[:, u, g, qs], start=(g == 0), stop=False)
                    ins = pe.matmul(out[:, qs], v_new[:, u, cols], sprobT[0:TS, u, NPAGE, qs], start=False, stop=True)
                ins.then_inc(ring_full, 1)

            for b in range(NB + 1):
                if b < NB:
                    for g in range(NPAGE):
                        page_kT(b, g)
                    s_scores(b)
                if b:
                    s_attend(b - 1)

            pe.wait_ge(negF_done, 1)

            def fox_scores(key):
                _, j, h = key
                s_taken(pe, key)
                out = s_slot(key)
                m = NMETA + P * (j + 1)
                rows = slice(64 * (h % 2), 64 * (h % 2) + 64)
                q0 = NMETA + P * j
                for c0 in range(0, m, 512):
                    c1 = min(c0 + 512, m)
                    d0 = max(c0, q0)
                    pe.matmul(out[:, c0:c1], QK[rows, 3 + h // 2, q0:q0 + P], QK[rows, h // 2, c0:c1],
                              start=True, stop=False)
                    ins = pe.matmul(out[:, c0:c1], pick_row[0:64 + H, h, :], negF[0:64 + H, c0:c1],
                                    start=False, stop=(d0 >= c1))
                    if d0 < c1:
                        ins = pe.matmul(out[:, d0:c1], identb[:, :], mask_neg[:, d0 - q0:c1 - q0],
                                        start=False, stop=True)
                ins.then_inc(s_full, 1)

            def project_out(key):
                t = key[1]
                n_ = PROJ.index(t)
                m = P if t < NTILE else NS
                s_taken(pe, key)
                out = s_slot(key)
                pe.wait_ge(yhi_done, n_ + 1)
                pe.wait_ge(ylo_done, n_ + 1)
                pe.wait_ge(wolo_done, KT)
                for half in range(2):
                    cols = slice(512 * half, 512 * half + 512)
                    ins = product(out[0:m, cols], lambda k: (yh[:, k, 0:m], yl[:, k, 0:m]),
                                  lambda k: (woh[:, k, cols], wol[:, k, cols]), True, True)
                ins.then_inc(s_full, 1)

            for kind, key in PLAN:
                if kind == "S" and key[0] == "fox":
                    fox_scores(key)
                elif kind == "S":
                    project_out(key)
                elif kind == "R" and key[0] == "probsT":
                    _, j, h, i = key
                    u = UI[("fox", j, h)]
                    out = ring_take(pe, key)
                    s_emptied(pe, ("fox", j, h))
                    for n_, b in enumerate(range(3 * i, min(3 * i + 3, j + 2))):
                        w = P if b <= j else NMETA
                        ins = pe.transpose(out[0:w, P * n_:P * n_ + P], prob[:, u % 2, P * b:P * b + w], ident[:, :])
                    ins.then_inc(ring_full, 1)
                elif key[0] == "attend":
                    _, j, h = key
                    u = UI[("fox", j, h)]
                    out = ring_take(pe, key)
                    last = (j + 4) // 3 - 1
                    drained(pe, ("probsT", j, h, last))
                    if last:
                        drained(pe, ("probsT", j, h, last - 1))
                    for b in range(j + 2):
                        w = P if b <= j else NMETA
                        ins = pe.matmul(out[:, 0:HD], probT[0:w, u % 2, b, :], VR[0:w, b, HD * h:HD * h + HD],
                                        start=(b == 0), stop=(b == j + 1))
                    ins.then_inc(ring_full, 1)
                else:
                    j = key[1]
                    out = ring_take(pe, key)
                    drained(pe, ("attend", j, H - 1))
                    drained(pe, ("attend", j, H - 2))
                    for i in range(3):
                        ins = pe.transpose(out[:, P * i:P * i + P], fox_o[:, j % 2, P * i:P * i + P], ident[:, :])
                    ins.then_inc(ring_full, 1)


INPUTS = ["x_prompt", "x_sample", "cache_fox_k", "cache_fox_v", "cache_fox_logf", "state_gla", "state_pool",
          "page_table", "meta_tokens", "norm_pre", "norm_post", "w_in", "gla_w_up", "gla_b_gate", "gla_norm",
          "pool_w", "pool_scale", "fox_b_f", "w_out"]
OUTPUTS = [("y_p", (1, SEQ, D)), ("y_s", (NB, TS, D)), ("fox_kp", (1, 1, LP, H, HD)), ("fox_vp", (1, 1, LP, H, HD)),
           ("logf_p", (1, 1, LP, H)), ("gla_p", (1, 1, H, DK, DV)), ("pool_p", (1, 1, HIST, 256)),
           ("fox_ks", (1, NB, TS, H, HD)), ("fox_vs", (1, NB, TS, H, HD)), ("logf_s", (1, NB, TS, H)),
           ("gla_s", (1, NB, H, DK, DV)), ("pool_s", (1, NB, HIST, 256))]


def kernel(**inputs):
    import numpy as np
    import concourse.bacc as bacc
    from concourse.bass_utils import run_bass_kernel_spmd

    nc = bacc.Bacc("TRN2", target_bir_lowering=False, num_devices=1)
    arrays, a, o = {}, {}, {}
    for name in INPUTS:
        x = np.ascontiguousarray(inputs[name])
        arrays[f"in_{name}_dram"] = x
        a[name] = nc.dram_tensor(f"in_{name}_dram", x.shape, mybir.dt.from_np(x.dtype), kind="ExternalInput").ap()
    for name, shape in OUTPUTS:
        o[name] = nc.dram_tensor(f"out_{name}_dram", shape, F32, kind="ExternalOutput").ap()
    build(nc, a, o)
    r = run_bass_kernel_spmd(nc, [arrays], core_ids=[0])
    return tuple(r.results[0][f"out_{name}_dram"] for name, _ in OUTPUTS)
```

```python
from contextlib import ExitStack

import concourse.bass as bass
from concourse import mybir

F32 = mybir.dt.float32
F32R = mybir.dt.float32r
BF16 = mybir.dt.bfloat16
I32 = mybir.dt.int32
ALU = mybir.AluOpType
ACT = mybir.ActivationFunctionType
AX = mybir.AxisListType

P = 128
D = 1024
KT = D // P
SEQ, NMETA = 1024, 16
NB, TS = 8, 8
LP = NMETA + SEQ
NS = NB * TS
NT = LP + NS
TH = NT // 3
NTILE = SEQ // P
H, HD = 6, 64
DK, DV = 32, 64
LR = 16
PAGE, NPAGE = 128, 8
PAST = PAGE * NPAGE
HIST = 15
CH = 64
NCH = SEQ // CH
EPS = 1e-6
GATE = 1.0 / 16.0
NEG = -1e30
SLOT = 384

W_GQ, W_GK, W_GV, W_LR, W_GG = 0, 192, 384, 768, 784
W_PV, W_PG, W_FQ, W_FK, W_FV, W_FF, W_FG = 1168, 1424, 1680, 2064, 2448, 2832, 2838

CHUNKS = [[(W_LR, 0, LR), (W_FF, 32, H)]]
CHUNKS += [[(W_GV + P * i, 0, P)] for i in range(3)]
CHUNKS += [[(W_PV + P * i, 0, P)] for i in range(2)]
CHUNKS += [[(W_GK, 0, P)], [(W_GQ, 0, P)], [(W_GQ + P, 0, 64), (W_GK + P, 64, 64)]]
CHUNKS += [[(W_FK + P * i, 0, P)] for i in range(3)]
CHUNKS += [[(W_FQ + P * i, 0, P)] for i in range(3)]
CHUNKS += [[(W_GG + P * i, 0, P)] for i in range(3)]
CHUNKS += [[(W_PG + P * i, 0, P)] for i in range(2)]
CHUNKS += [[(W_FG + P * i, 0, P)] for i in range(3)]
CHUNKS += [[(W_FV + P * i, 0, P)] for i in range(3)]
C_LF, C_GV, C_PV, C_GKA, C_GQA, C_QKB = 0, 1, 4, 6, 7, 8
C_FK, C_FQ, C_GG, C_PG, C_FG, C_FV = 9, 12, 15, 18, 20, 23
NCHUNK = len(CHUNKS)
GATES = list(range(C_GG, C_FG + 3))

GBLOCKS = [(NMETA + P * j, P) for j in range(NTILE)] + [(LP, NS), (0, NMETA)]
PIECES = [(NMETA, SLOT), (NMETA + SLOT, SLOT), (NMETA + 2 * SLOT, NT - NMETA - 2 * SLOT)]


def side_jobs():
    s = {c: [] for c in range(NCHUNK)}
    s[1] = [("gate", g, t) for g in range(2) for t in range(3)]
    s[3] = [("logf_rows",), ("page_prefix",)]
    s[4] = [("v_rows", b) for b in range(10)] + [("hist",), ("pool_last", 0)]
    s[5] = [("pool_last", 1)] + [("pool", 0, i) for i in range(3)]
    s[6] = [("pool", 1, i) for i in range(3)]
    s[8] = [("kd_rows", i) for i in range(5)] + [("state", 0)]
    gla = []
    for j in range(NTILE):
        if j:
            gla += [("out", j - 1)]
        gla += [("scores", j), ("state", 2 * j + 1), ("state", 2 * j + 2)]
    gla += [("sample_scores",), ("out", 7), ("sample_out",), ("sample_state", 0, 0), ("sample_state", 0, 1),
            ("sample_state", 1, 0), ("sample_state", 1, 1)]
    for c in range(4):
        s[9 + c] = gla[len(gla) * c // 4:len(gla) * (c + 1) // 4]
    s[13] = [("meansq", i, q) for i in range(3) for q in range(3)]
    s[14] = [("k_rows", t) for t in range(9)]
    s[25] = [("fv_rows", t) for t in range(9)]
    return s


FIRST_STEP = {4: 2, 5: 12, 6: 12}


SIDE = side_jobs()


def plan():
    units = [(j, p) for j in range(NTILE) for p in range(3)]
    steps = []
    for b in range(NB):
        steps += [("R", ("page_kT", b, g)) for g in range(NPAGE)] + [("S", ("seq", b))]
        if b:
            steps += [("R", (k, b - 1)) for k in ("s_probsT_a", "s_probsT_b", "s_attend", "s_outT")]
    tail = [("R", (k, NB - 1)) for k in ("s_probsT_a", "s_probsT_b", "s_attend", "s_outT")]
    last = 3 * SAMPLES_END
    weight = [j + 2 for j, _ in units[1:last]]
    order, given = [], 0

    def post(j, p):
        out = []
        for h in (2 * p, 2 * p + 1):
            out += [("R", ("probsT", j, h, i)) for i in range((j + 4) // 3)]
        return out + [("R", ("attend", j, p))]

    for n, (j, p) in enumerate(units):
        order += [("S", ("fox", j, 2 * p)), ("S", ("fox", j, 2 * p + 1))]
        mine = []
        if 1 <= n < last:
            upto = round(len(steps) * sum(weight[:n]) / sum(weight))
            mine, given = steps[given:upto], upto
        if n == last + 1:
            mine = tail
        behind = post(*units[n - 1]) if n else []
        order += behind[:-1] + mine + behind[-1:]
    order.append(("S", ("proj", NTILE)))
    order += post(*units[-1])
    return order + [("S", ("proj", t)) for t in range(NTILE)]


SAMPLES_END = 6
PLAN = plan()
RING = [k for c in range(NCHUNK) for k in SIDE[c]] + [k for t, k in PLAN if t == "R"]
RI = {k: i for i, k in enumerate(RING)}
SUSERS = [k for t, k in PLAN if t == "S"]
SF = {k: i for i, k in enumerate(SUSERS)}
PROJ = [k[1] for k in SUSERS if k[0] == "proj"]


def slot_of(user):
    if user[0] == "fox":
        return user[2] % 2
    return user[1] % 2 if user[0] == "seq" else PROJ.index(user[1]) % 2


SN = {k: sum(slot_of(x) == slot_of(k) for x in SUSERS[:SF[k]]) for k in SUSERS}


def drains_on_act(key):
    if key[0] == "page_kT":
        return key[2] % 2 == 1
    return key[0] == "probsT" and not (key[2] % 2 and key[3] == (key[1] + 4) // 3 - 1)


UNITS = [k for k in SUSERS if k[0] == "fox"]
UI = {k: i for i, k in enumerate(UNITS)}


def build(nc, a, o):
    with ExitStack() as ctx:
        def sb(name, shape, dt=F32):
            return ctx.enter_context(nc.sbuf_tensor(name, shape, dt))

        def sem(name):
            return ctx.enter_context(nc.semaphore(name))

        YF = sb("YF", [P, 14 * NT])
        Y = YF[:, 0:8 * NT].rearrange("p (s t) -> p s t", t=NT)
        QK = YF[:, 8 * NT:14 * NT].rearrange("p (s t) -> p s t", t=NT)
        xrows = YF[:, 0:9 * D].rearrange("p (t n) -> p t n", n=D)
        VR = sb("VR", [P, 10, 384])
        ident = sb("ident", [P, P])
        identb = sb("identb", [P, P], BF16)
        causal = sb("causal", [P, CH])
        causal_s = sb("causal_s", [NS, NS])
        same_seq = sb("same_seq", [NS, NB])
        page_before = sb("page_before", [NS, NS])
        pick_row = sb("pick_row", [P, H, P], BF16)
        mask_neg = sb("mask_neg", [P, P], BF16)
        pick_q = sb("pick_q", [TS, 96], BF16)
        mask_new = sb("mask_new", [TS, TS], BF16)
        block_mean = sb("block_mean", [P, P])
        pool_w = sb("pool_w", [P, 2, P])
        negF = sb("negF", [P, LP], BF16)
        small = sb("small", [P, 44])
        gpre = small[:, 0:8]
        bgate = small[:, 8:10]
        gnorm = small[:, 10:11]
        pscale = small[:, 11:13]
        eps = small[:, 13:14]
        one = small[:, 14:15]
        ssq = small[:, 15:24]
        nmax = small[:, 24:30]
        rsum = small[:, 30:34]
        rinv = small[:, 34:38]
        zstat = small[:, 38:40]
        head_of = small[:, 40:44]
        bfox = sb("bfox", [H, 1])
        w_up = sb("w_up", [LR, H * DK])
        ebend = sb("ebend", [P, 2, 25])
        gstate = sb("gstate", [P, 3, 2, DV])
        logf_t = sb("logf_t", [P, 9, H])
        f_sum = sb("f_sum", [H, NS])
        f_last = sb("f_last", [H, NB])
        q_odd = sb("q_odd", [P, H * P])
        ptab = sb("ptab", [1, NB * NPAGE], I32)
        pidx = sb("pidx", [NB * NPAGE, 1], I32)
        PS = ctx.enter_context(nc.psum_tensor("PS", [P, 8, 512], F32))

        def stage(*tensors):
            with ExitStack() as s:
                return [s.enter_context(nc.sbuf_tensor(n, d, t)) for n, d, t in tensors]

        region_a = ("RA", [P, 6 * NT], F32)
        RA, wr, wh, wl, xh, xl = stage(
            region_a, ("wr", [P, 2, KT, P], F32), ("wh", [P, 2, KT, P], F32R), ("wl", [P, 2, KT, P], F32R),
            ("xh", [P, KT, NT], F32R), ("xl", [P, KT, NT], F32R))
        _, pagesB, kT, sbias, sprob, q_diag, sprobT0, prob, probT = stage(
            ("RA2", [P, 6 * NT], F32), ("pagesB", [P, 2, NPAGE, 384], F32), ("kT", [P, 2, 3, PAST], F32),
            ("sbias", [96, 2, PAST + TS], F32), ("sprob", [96, 2, PAST + TS], F32),
            ("q_diag", [P, 3, NB, 32], F32), ("sprobT0", [P, NPAGE + 1, H * TS], F32),
            ("prob", [P, 3, LP], F32), ("probT", [P, 2, 9, P], F32))
        wol_a, _, yh0, yl0, wo_raw, xres, zout, woh, wol_b, gpost = stage(
            ("wol_a", [P, 6, D], F32R), ("pad_a", [P, 6 * NT - 6 * D], F32),
            ("yh0", [P, KT, P], F32R), ("yl0", [P, KT, P], F32R), ("wo_raw", [P, 2, D], F32),
            ("xres", [P, D], F32), ("zout", [P, D], F32),
            ("woh", [P, KT, D], F32R), ("wol_b", [P, 2, D], F32R), ("gpost", [P, D], F32))
        _, _, _, yh1, yl1 = stage(
            ("pad_b", [P, 6 * NT], F32), ("pad_c", [P, KT, P], F32), ("pad_d", [P, KT, P], F32),
            ("yh1", [P, KT, P], F32R), ("yl1", [P, KT, P], F32R))
        yh, yl = [yh0, yh1], [yl0, yl1]
        wol = [wol_a[:, k, :] for k in range(6)] + [wol_b[:, k, :] for k in range(2)]
        E = RA[:, :].rearrange("p (s t) -> p s t", t=NT)

        pages = [pagesB[:, :, :, :], RA[:, 0:2 * NPAGE * 384].rearrange("p (w g n) -> p w g n", w=2, n=384)]
        glr = Y[0:LR, 5, :]
        reset = Y[:, 7, :]
        ones_row = QK[0:NS, 5, 0:LP]
        logf, ftmp, fcum = QK[0:H, 0, :], QK[0:H, 1, :], QK[0:H, 2, :]
        page_lf = QK[0:NS, 3, 0:PAGE * H].rearrange("p (k h) -> p k h", h=H)
        page_F = QK[0:NS, 4, 0:PAGE * H].rearrange("p (h k) -> p h k", h=H)
        pv, psA, psB = Y[:, 5, :], Y[:, 6, :], Y[:, 7, :]
        hist_rows = Y[0:NB * HIST, 4, 0:256]
        HX = HIST + TS
        hx = [Y[:, 0, 192 * i:192 * i + NB * HX].rearrange("p (b t) -> p b t", b=NB) for i in range(2)]
        hA, hB = (Y[:, 0, 384 + 192 * i:384 + 192 * i + NB * HX].rearrange("p (b t) -> p b t", b=NB) for i in range(2))
        last_p, last_s = Y[0:HIST, 1, 0:256], Y[0:NS, 1, 256:512]
        kd_rows = Y[:, 5:7, :].rearrange("p s t -> p (s t)")[:, 0:9 * 192].rearrange("p (b n) -> p b n", n=192)
        kd_meta = QK[0:NMETA, 4, H * P:H * P + 192]
        kd_seq = Y[:, 5:7, :].rearrange("p s t -> p (s t)")[0:NS, 0:NB * 192].rearrange("p (b n) -> p b n", n=192)
        aT = YF[:, 5 * NT + 9 * 192:5 * NT + 9 * 192 + 2 * H * P].rearrange("p (a h t) -> p a h t", a=2, h=H)
        q_heads = [x.rearrange("p (h t) -> p h t", h=H) for x in (QK[:, 4, 0:H * P], q_odd[:, :])]
        gstate_s = QK[:, 5, 0:2 * NB * DV].rearrange("p (g b v) -> p g b v", g=2, b=NB)
        k_out = RA[:, 0:9 * 384].rearrange("p (t n) -> p t n", n=384)
        gtmp = [E[:, 4, :], E[:, 5, :]]
        xg = RA[:, 0:3 * D].rearrange("p (a k t) -> p a k t", a=3, k=KT)
        squares = RA[:, 3 * D:4 * D]
        rstd, refine = RA[:, 4 * D:4 * D + 9], RA[:, 4 * D + 9:4 * D + 18]
        at = 2 * NPAGE * 384
        sprobT = [sprobT0[:, :, :], RA[:, at:at + 9 * H * TS].rearrange("p (g q) -> p g q", q=H * TS)]
        v_new = q_odd[0:TS, :].rearrange("p (a n) -> p a n", a=2)
        s_rows = VR[0:96, 9, 0:P]
        nf_d = nc.dram_tensor("minus_F", [NB, H, PAST + TS], F32, kind="Internal").ap()

        d_x = [sem(f"d_x{t}") for t in range(9)]
        d_const, d_poolw = sem("d_const"), sem("d_poolw")
        d_w = [sem("d_w0"), sem("d_w1")]
        d_hist, d_idx, d_lf, d_ptab = sem("d_hist"), sem("d_idx"), sem("d_lf"), sem("d_ptab")
        d_nf, d_fl, d_s0 = sem("d_nf"), sem("d_fl"), sem("d_s0")
        d_out = sem("d_out")
        d_pool_out, d_state_out, d_k_out = sem("d_pool_out"), sem("d_state_out"), sem("d_k_out")
        d_k, d_v = [sem("d_k0"), sem("d_k1")], [sem("d_v0"), sem("d_v1")]
        d_bias = [sem("d_bias0"), sem("d_bias1")]
        d_wo = [sem("d_wo0"), sem("d_wo1")]
        d_post, d_xres, d_y = sem("d_post"), sem("d_xres"), sem("d_y")
        consts_set, pool_step = sem("consts_set"), sem("pool_step")
        wz = sem("wz")
        sq_done, rms_done, xs_done = sem("sq_done"), sem("rms_done"), sem("xs_done")
        xt_full, xg_done, xhi_done, xlo_done = sem("xt_full"), sem("xg_done"), sem("xhi_done"), sem("xlo_done")
        xlo_dve = sem("xlo_dve")
        whi_done, wlo_done = sem("whi_done"), sem("wlo_done")
        in_full = sem("in_full")
        in_free = [sem("in_free0"), sem("in_free1")]
        ring_full = sem("ring_full")
        ring_free = [sem("ring_free0"), sem("ring_free1")]
        s_full = sem("s_full")
        s_free = [sem("s_free0"), sem("s_free1")]
        act_step, dve_step = sem("act_step"), sem("dve_step")
        abs_done, ln_done, b_done, e_done, kd_sub, kd_exp = (
            sem("abs_done"), sem("ln_done"), sem("b_done"), sem("e_done"), sem("kd_sub"), sem("kd_exp"))
        zf_done, negF_done, page_scanned, fnew_done = sem("zf_done"), sem("negF_done"), sem("page_scanned"), sem("fnew_done")
        kb_moved = sem("kb_moved")
        qheads_done = sem("qheads_done")
        pool_done, kdseq_done, s0_scaled = sem("pool_done"), sem("kdseq_done"), sem("s0_scaled")
        osq_done, orstd_done, o_normed = sem("osq_done"), sem("orstd_done"), sem("o_normed")
        gexp_done, gated = sem("gexp_done"), sem("gated")
        sbias_zero, fprob_done, srows_zero = sem("sbias_zero"), sem("fprob_done"), sem("srows_zero")
        qdiag_zero, qdiag_done = sem("qdiag_zero"), sem("qdiag_done")
        smax_done, sexp_done, sprob_done = sem("smax_done"), sem("sexp_done"), sem("sprob_done")
        fmax_done = sem("fmax_done")
        wohi_done, wolo_done = sem("wohi_done"), sem("wolo_done")
        yhi_done, ylo_done = sem("yhi_done"), sem("ylo_done")
        zstat_done, z_done, y_done = sem("zstat_done"), sem("z_done"), sem("y_done")

        def bank(key):
            return PS[:, 6 + RI[key] % 2, :]

        def ring_take(pe, key):
            if RI[key] >= 2:
                pe.wait_ge(ring_free[RI[key] % 2], RI[key] // 2)
            return bank(key)

        def ring_ready(eng, key):
            eng.wait_ge(ring_full, RI[key] + 1)
            return bank(key)

        def freed(key):
            return ring_free[RI[key] % 2]

        def drained(eng, key):
            eng.wait_ge(ring_free[RI[key] % 2], RI[key] // 2 + 1)

        def chunk_psum(c):
            return PS[:, 3 * (c % 2):3 * (c % 2) + 3, 0:TH]

        def thirds(ap):
            return ap.rearrange("p (a t) -> p a t", t=TH)

        def chunk_stored(eng, c):
            eng.wait_ge(in_free[c % 2], c // 2 + 1)

        def s_slot(user):
            n = slot_of(user)
            return PS[:, 3 * n:3 * n + 3, :].rearrange("p b t -> p (b t)")

        def s_taken(pe, user):
            if SN[user]:
                pe.wait_ge(s_free[slot_of(user)], SN[user])

        def s_emptied(eng, user):
            eng.wait_ge(s_free[slot_of(user)], SN[user] + 1)

        def s_ready(eng, user):
            eng.wait_ge(s_full, SF[user] + 1)

        def head_rows(h):
            return slice(DK * (h % 4), DK * (h % 4) + DK)

        def group_rows(h):
            return slice(0, P) if h < 4 else slice(0, 64)

        def xcols(t):
            return [(0, P, NMETA + P * t)] if t < NTILE else [(0, NS, LP), (NS, NS + NMETA, 0)]

        def n_of(t):
            return P if t < NTILE else NS + NMETA

        def ycol(t):
            return NMETA + P * t if t < NTILE else LP

        def probsT_drain(eng, key, copy):
            _, j, h, i = key
            u = UI[("fox", j, h)]
            src = ring_ready(eng, key)
            lo, hi = 3 * i, min(3 * i + 3, j + 2)
            full = min(hi, j + 1) - lo
            if full:
                ins = copy(probT[:, u % 2, lo:lo + full, :], src[:, 0:P * full].rearrange("p (b q) -> p b q", q=P))
            if hi == j + 2:
                ins = copy(probT[0:NMETA, u % 2, j + 1, :], src[0:NMETA, P * full:P * full + P])
            ins.then_inc(freed(key), 1)

        def x_low(eng, i):
            eng.wait_ge(xhi_done, i + 1)
            for r0, r1, col in xcols(XORDER[i]):
                ins = eng.tensor_tensor(xl[:, :, col:col + r1 - r0], xg[:, i % 3, :, r0:r1],
                                        xh[:, :, col:col + r1 - r0].bitcast(F32), ALU.subtract)
            return ins

        XORDER = [NTILE] + list(range(NTILE))
        block = ctx.enter_context(nc.Block())
        wdst = wr[:, :, :, :]
        w_src = a["w_in"][0].rearrange("(k p) n -> p k n", p=P)
        W_COUNT = []
        for c in range(NCHUNK):
            W_COUNT.append((W_COUNT[c - 2] if c >= 2 else 0) + 16 * len(CHUNKS[c]))

        @block.sync
        def _(sp):
            def load_x(t):
                if t < NTILE:
                    sp.dma_start(xrows[:, t, :], a["x_prompt"][0, P * t:P * t + P, :]).then_inc(d_x[t], 16)
                else:
                    sp.dma_start(xrows[0:NS, t, :], a["x_sample"].rearrange("b t n -> (b t) n")).then_inc(d_x[t], 16)
                    sp.dma_start(xrows[NS:NS + NMETA, t, :], a["meta_tokens"]).then_inc(d_x[t], 16)

            def load_w(c):
                if c == 0:
                    sp.wait_ge(wz, 1)
                if c >= 2:
                    sp.wait_ge(whi_done, c - 1)
                    sp.wait_ge(wlo_done, c - 1)
                for col, at_, n in CHUNKS[c]:
                    sp.dma_start(wr[:, c % 2, :, at_:at_ + n], w_src[:, :, col:col + n]).then_inc(d_w[c % 2], 16)

            for i, t in enumerate(XORDER):
                load_x(t)
                if i == 3:
                    load_w(0)
            load_w(1)

            def outputs(c):
                if c == 1:
                    sp.wait_ge(xs_done, 9)
                    sp.wait_ge(xt_full, 9)
                    sp.dma_start(hist_rows, a["state_pool"][0].rearrange("b t c -> (b t) c")).then_inc(d_hist, 16)
                if c == 3:
                    drained(sp, ("logf_rows",))
                    sp.dma_start(o["logf_p"][0, 0, 0:P * NTILE, :].rearrange("(t p) h -> p t h", p=P),
                                 logf_t[:, 0:NTILE, :]).then_inc(d_out, 16)
                    sp.dma_start(o["logf_p"][0, 0, P * NTILE:LP, :], logf_t[0:NMETA, NTILE, :]).then_inc(d_out, 16)
                    sp.dma_start(o["logf_s"][0].rearrange("b t h -> (b t) h"),
                                 logf_t[NMETA:NMETA + NS, NTILE, :]).then_inc(d_out, 16)
                    drained(sp, ("page_prefix",))
                    for b in range(NB):
                        sp.dma_start(nf_d[b, :, 0:PAST].rearrange("h (g k) -> g h k", k=PAGE),
                                     page_F[NPAGE * b:NPAGE * b + NPAGE]).then_inc(d_nf, 16)
                    sp.wait_ge(d_nf, 16 * NB)
                    with nc.allow_non_contiguous_dma(reason="one value per head and sequence"):
                        sp.dma_start(f_last[:, :], nf_d[:, :, PAST - 1].rearrange("b h -> h b")).then_inc(d_fl, 16)
                if c == 6:
                    sp.wait_ge(fnew_done, 1)
                    sp.dma_start(nf_d[:, :, PAST:PAST + TS].rearrange("b h t -> h b t"),
                                 f_sum[:, :].rearrange("h (b t) -> h b t", t=TS)).then_inc(d_nf, 16)
                    drained(sp, ("pool_last", 0))
                    drained(sp, ("pool_last", 1))
                    sp.dma_start(o["pool_p"][0, 0], last_p).then_inc(d_pool_out, 16)
                    for b in range(NB):
                        sp.dma_start(o["pool_s"][0, b, HIST - TS:HIST, :],
                                     last_s[TS * b:TS * b + TS]).then_inc(d_pool_out, 16)
                    sp.dma_start(o["pool_s"][0, :, 0:HIST - TS, :],
                                 a["state_pool"][0, :, TS:HIST, :]).then_inc(d_out, 16)
                    sp.wait_ge(fnew_done, 1)
                    for g, n in ((0, 4), (1, 2)):
                        sp.dma_start(gstate_s[0:DK * n, g],
                                     a["state_gla"][0, :, 4 * g:4 * g + n].rearrange("b h k v -> (h k) b v")
                                     ).then_inc(d_s0, 16)
                if c == 12:
                    drained(sp, ("state", NCH))
                    for g, n in ((0, 4), (1, 2)):
                        sp.dma_start(o["gla_p"][0, 0, 4 * g:4 * g + n].rearrange("h k v -> (h k) v"),
                                     gstate[0:DK * n, NCH % 3, g, :]).then_inc(d_out, 16)
                if c == 12:
                    drained(sp, ("sample_state", 1, 1))
                    drained(sp, ("sample_state", 1, 0))
                    for g, n in ((0, 4), (1, 2)):
                        sp.dma_start(o["gla_s"][0, :, 4 * g:4 * g + n].rearrange("b h k v -> (h k) b v"),
                                     gstate_s[0:DK * n, g]).then_inc(d_state_out, 16)
                if c == 14:
                    for t in range(9):
                        drained(sp, ("k_rows", t))
                        store_rows("k", k_out, t, d_k_out)
                if c == 25:
                    for t in range(9):
                        drained(sp, ("fv_rows", t))
                        store_rows("v", VR, t, d_out)

            def store_rows(which, src, t, done):
                dp, ds = (o["fox_" + which + x].rearrange("z b t h d -> (z b t) (h d)") for x in "ps")
                if t < NTILE:
                    sp.dma_start(dp[P * t:P * t + P], src[:, t, :]).then_inc(done, 16)
                else:
                    sp.dma_start(dp[P * t:LP], src[0:NMETA, t, :]).then_inc(done, 16)
                    sp.dma_start(ds, src[NMETA:NMETA + NS, t, :]).then_inc(done, 16)

            for c in range(2, NCHUNK):
                load_w(c)
                if c >= 4:
                    outputs(c - 3)
            for c in range(NCHUNK - 3, NCHUNK - 1):
                outputs(c)

            k_cache = a["cache_fox_k"][0].rearrange("g p h d -> g p (h d)")
            sp.wait_ge(d_ptab, 16)
            for b in range(NB):
                u = b % 2
                if b == 0:
                    sp.wait_ge(in_full, NCHUNK)
                elif b == 1:
                    outputs(NCHUNK - 1)
                    drained(sp, ("fv_rows", 7))
                else:
                    sp.wait_ge(ring_full, RI[("page_kT", b - 2, NPAGE - 1)] + 1)
                for g in range(NPAGE):
                    i = NPAGE * b + g
                    page = sp.value_load(ptab[0:1, i:i + 1], min_val=0, max_val=a["cache_fox_k"].shape[1] - 1)
                    sp.dma_start(pages[u][:, 0, g, :],
                                 k_cache[bass.ds(page, 1)].rearrange("a p n -> (a p) n")).then_inc(d_k[u], 16)
                if b == 0:
                    sp.wait_ge(d_nf, 16 * (NB + 1))
                    sp.wait_ge(sbias_zero, 1)
                if b >= 2:
                    sp.wait_ge(smax_done, b - 1)
                for h in range(H):
                    r = 32 * (h // 2) + TS * (h % 2)
                    sp.dma_start(sbias[r:r + TS, u, :],
                                 nf_d[b, h:h + 1, :].to_broadcast([TS, PAST + TS])).then_inc(d_bias[u], 16)

            wo_src = a["w_out"][0].rearrange("(k p) n -> k p n", p=P)
            drained(sp, ("s_outT", NB - 1))
            sp.dma_start(gpost[:, :], a["norm_post"][0:1, :].to_broadcast([P, D])).then_inc(d_post, 16)
            for k in range(KT):
                if k >= 2:
                    sp.wait_ge(wohi_done, k - 1)
                    sp.wait_ge(wolo_done, k - 1)
                sp.dma_start(wo_raw[:, k % 2, :], wo_src[k]).then_inc(d_wo[k % 2], 16)
            for n, t in enumerate(PROJ):
                if n:
                    sp.wait_ge(y_done, n)
                if t < NTILE:
                    sp.dma_start(xres[:, :], a["x_prompt"][0, P * t:P * t + P, :]).then_inc(d_xres, 16)
                else:
                    sp.dma_start(xres[0:NS, :], a["x_sample"].rearrange("b t n -> (b t) n")).then_inc(d_xres, 16)
                sp.wait_ge(y_done, n + 1)
                if t < NTILE:
                    sp.dma_start(o["y_p"][0, P * t:P * t + P, :], zout[:, :]).then_inc(d_y, 16)
                else:
                    sp.dma_start(o["y_s"].rearrange("b t n -> (b t) n"), zout[0:NS, :]).then_inc(d_y, 16)
            sp.wait_ge(d_y, 16 * len(PROJ))
            sp.wait_ge(d_k_out, 16 * 10)
            sp.wait_ge(d_state_out, 32)
            sp.wait_ge(d_pool_out, 16 * (NB + 1))
            sp.wait_ge(d_out, 16 * (3 + 1 + 2 + 10))

        @block.gpsimd
        def _(pool):
            g = pool
            n = [0]

            def link(ins):
                n[0] += 1
                ins.then_inc(pool_step, 1)
                g.wait_ge(pool_step, n[0])

            link(g.memset(wr[:, 0, :, :], 0.0))
            g.memset(eps[:, :], EPS).then_inc(wz, 1)

            def keep(ap, pattern, base, mult, fill=0.0, op=ALU.is_ge):
                link(g.affine_select(out=ap, in_=ap, compare_op=op, fill=fill, base=base, pattern=pattern,
                                     channel_multiplier=mult))

            g.dma_start(pidx[:, :], a["page_table"].rearrange("b (g a) -> (b g) a", a=1)).then_inc(d_idx, 16)
            g.dma_start(ptab[:, :], a["page_table"].rearrange("(a b) g -> a (b g)", a=1)).then_inc(d_ptab, 16)
            link(g.memset(one[:, :], 1.0))
            for m in (ident, identb):
                link(g.memset(m[:, :], 0.0))
                keep(m[:, :], [[-1, P]], 0, 1, 1.0, ALU.not_equal)
            link(g.memset(block_mean[:, :], 0.0))
            for r in (slice(0, 64), slice(64, P)):
                link(g.memset(block_mean[r, r], 1.0 / DV))
            link(g.memset(causal[:, :], 1.0))
            keep(causal[:, :], [[1, CH]], CH, -1)
            keep(causal[0:CH, :], [[1, CH]], 0, -1)
            link(g.memset(causal_s[:, :], 1.0))
            cs = causal_s[:, :].rearrange("p (b t) -> p b t", t=TS)
            keep(cs, [[TS, NB], [1, TS]], 0, -1)
            keep(cs, [[-TS, NB], [0, TS]], 0, 1)
            link(g.memset(same_seq[:, :], 1.0))
            keep(same_seq[:, :], [[-TS, NB]], 0, 1)
            keep(same_seq[:, :], [[TS, NB]], TS - 1, -1)
            link(g.memset(head_of[:, :], 1.0))
            keep(head_of[:, :], [[-DK, 4]], 0, 1)
            keep(head_of[:, :], [[DK, 4]], DK - 1, -1)
            link(g.memset(page_before[:, :], 1.0))
            pb = page_before[:, :].rearrange("p (b g) -> p b g", g=NPAGE)
            keep(pb, [[-NPAGE, NB], [0, NPAGE]], 0, 1)
            keep(pb, [[NPAGE, NB], [1, NPAGE]], -1, -1)
            link(g.memset(pick_row[:, :, :], 0.0))
            for q in range(3):
                keep(pick_row[:, :, :], [[-1, H], [0, P]], -32 * q, 1, 1.0, ALU.not_equal)
            link(g.memset(mask_neg[:, :], 0.0))
            keep(mask_neg[:, :], [[-1, P]], 0, 1, NEG)
            link(g.memset(mask_new[:, :], 0.0))
            keep(mask_new[:, :], [[-1, TS]], 0, 1, NEG)
            link(g.memset(pick_q[:, :], 0.0))
            pq = pick_q[:, :].rearrange("p (h i q) -> p h i q", i=4, q=TS)[:, :, 0:2, :]
            keep(pq, [[0, 3], [0, 2], [1, TS]], 0, -1, 1.0, ALU.not_equal)
            link(g.memset(pool_w[:, :, :], 0.0))
            link(g.memset(negF[:, :], 0.0))
            g.memset(one[:, :], 1.0).then_inc(consts_set, 1)
            for i in range(4):
                r = slice(64 * (i % 2), 64 * (i % 2) + 64)
                g.dma_start(pool_w[r, i // 2, r], a["pool_w"][0, i]).then_inc(d_poolw, 16)

            def w_low(c):
                g.wait_ge(d_w[c % 2], W_COUNT[c])
                g.wait_ge(whi_done, c + 1)
                if c >= 2:
                    g.wait_ge(in_full, c - 1)
                g.tensor_tensor(wl[:, c % 2], wr[:, c % 2], wh[:, c % 2].bitcast(F32), ALU.subtract
                                ).then_inc(wlo_done, 1)

            for i in range(0, 9, 2):
                x_low(g, i).then_inc(xlo_done, 1)
                if i == 2:
                    w_low(0)
            g.wait_ge(xt_full, 9)
            link(g.memset(reset, 1.0))
            link(g.memset(reset[:, 0:1], 0.0))
            link(g.memset(reset[:, NMETA:LP].rearrange("p (c t) -> p c t", t=CH)[:, :, 0:1], 0.0))
            link(g.memset(reset[:, LP:NT].rearrange("p (c t) -> p c t", t=TS)[:, :, 0:1], 0.0))
            g.memset(ones_row, 1.0).then_inc(consts_set, 1)
            w_low(1)
            g.wait_ge(d_idx, 16)
            g.indirect_dma_start(QK[0:NS, 3, 0:PAGE * H], None,
                                 a["cache_fox_logf"][0].rearrange("g p h -> g (p h)"),
                                 bass.IndirectOffsetOnAxis(ap=pidx[:, 0:1], axis=0)).then_inc(d_lf, 16)
            for c in range(2, NCHUNK):
                w_low(c)
            g.wait_ge(in_full, NCHUNK)
            g.memset(q_diag[:, :, :, :], 0.0).then_inc(qdiag_zero, 1)
            g.memset(sbias[:, :, :], 0.0).then_inc(sbias_zero, 1)

            v_cache = a["cache_fox_v"][0].rearrange("g p h d -> g p (h d)")
            g.wait_ge(d_ptab, 16)
            for b in range(NB):
                u = b % 2
                if b == 1:
                    g.wait_ge(gated, len(GATES))
                    drained(g, ("fv_rows", 8))
                    drained(g, ("fv_rows", 7))
                elif b >= 2:
                    drained(g, ("s_attend", b - 2))
                for i in range(NPAGE * b, NPAGE * b + NPAGE):
                    page = g.value_load(ptab[0:1, i:i + 1], min_val=0, max_val=a["cache_fox_v"].shape[1] - 1)
                    g.dma_start(pages[u][:, 1, i % NPAGE, :],
                                v_cache[bass.ds(page, 1)].rearrange("a p n -> (a p) n")).then_inc(d_v[u], 16)
                if b == 0:
                    drained(g, ("fv_rows", 8))
                g.dma_start(v_new[:, u, :], VR[NMETA + TS * b:NMETA + TS * b + TS, NTILE, :]).then_inc(d_v[u], 16)
            for k in range(KT):
                g.wait_ge(wohi_done, k + 1)
                g.tensor_tensor(wol[k], wo_raw[:, k % 2, :], woh[:, k, :].bitcast(F32), ALU.subtract
                                ).then_inc(wolo_done, 1)
            for n_, t in enumerate(PROJ):
                g.wait_ge(yhi_done, n_ + 1)
                m = P if t < NTILE else NS
                g.tensor_tensor(yl[n_ % 2][:, :, 0:m], Y[:, :, ycol(t):ycol(t) + m], yh[n_ % 2][:, :, 0:m].bitcast(F32),
                                ALU.subtract).then_inc(ylo_done, 1)

        @block.scalar
        def _(act):
            n = [0]

            def link(ins):
                n[0] += 1
                ins.then_inc(act_step, 1)
                act.wait_ge(act_step, n[0])

            for dst, src in ((gpre[:, :], a["norm_pre"][0].rearrange("(k p) -> p k", p=P)),
                             (bgate[:, 0:1], a["gla_b_gate"][0, 0:P].rearrange("(p a) -> p a", a=1)),
                             (bgate[0:64, 1:2], a["gla_b_gate"][0, P:].rearrange("(p a) -> p a", a=1)),
                             (gnorm[0:DV, :], a["gla_norm"][0].rearrange("(p a) -> p a", a=1)),
                             (gnorm[DV:P, :], a["gla_norm"][0].rearrange("(p a) -> p a", a=1)),
                             (pscale[:, :], a["pool_scale"][0].rearrange("(i p) -> p i", p=P)),
                             (bfox[:, :], a["fox_b_f"][0].rearrange("(p a) -> p a", a=1)),
                             (w_up[:, :], a["gla_w_up"][0])):
                with nc.allow_non_contiguous_dma(reason="small vectors, one value per partition"):
                    act.dma_start(dst, src).then_inc(d_const, 16)

            def x_squares(t):
                act.wait_ge(d_x[t], 16 if t < NTILE else 32)
                m = n_of(t)
                act.activation(squares[0:m, :], xrows[0:m, t, :], ACT.Square,
                               accum_out=ssq[0:m, t:t + 1]).then_inc(sq_done, 1)
                act.wait_ge(sq_done, XORDER.index(t) + 1)
                act.activation(rstd[0:m, t:t + 1], ssq[0:m, t:t + 1], ACT.Sqrt, bias=eps[0:m, :], scale=1.0 / D
                               ).then_inc(rms_done, 1)

            def x_high(i):
                t = XORDER[i]
                act.wait_ge(xg_done, i + 1)
                for r0, r1, col in xcols(t):
                    ins = act.activation(xh[:, :, col:col + r1 - r0], xg[:, i % 3, :, r0:r1], ACT.Copy)
                ins.then_inc(xhi_done, 1)

            def w_high(c):
                if c >= NCHUNK:
                    return
                act.wait_ge(d_w[c % 2], W_COUNT[c])
                if c >= 2:
                    act.wait_ge(in_full, c - 1)
                act.activation(wh[:, c % 2], wr[:, c % 2], ACT.Copy).then_inc(whi_done, 1)

            act.wait_ge(wz, 1)
            for i, t in enumerate(XORDER):
                x_squares(t)
                if i >= 2:
                    x_high(i - 2)
                if i == 4:
                    w_high(0)
            x_high(7)
            x_high(8)
            w_high(1)

            def drain(key):
                kind = key[0]
                if kind == "gate":
                    _, g, t = key
                    r = P if g == 0 else 64
                    src = ring_ready(act, key)
                    act.activation(E[0:r, g, TH * t:TH * t + TH], src[0:r, 0:TH], ACT.Identity,
                                   bias=bgate[0:r, g:g + 1]).then_inc(freed(key), 1)
                elif kind == "logf_rows":
                    src = ring_ready(act, key)
                    act.activation(logf_t[:, 0:NTILE, :], src[:, 0:NTILE * H].rearrange("p (t h) -> p t h", h=H), ACT.Copy)
                    act.activation(logf_t[0:NMETA + NS, NTILE, :], src[0:NMETA + NS, NTILE * H:9 * H],
                                   ACT.Copy).then_inc(freed(key), 1)
                elif kind == "v_rows":
                    b = key[1]
                    m = GBLOCKS[b][1]
                    src = ring_ready(act, key)
                    act.activation(VR[0:m, b, :], src[0:m, 0:384], ACT.Copy).then_inc(freed(key), 1)
                elif kind == "pool_last":
                    i = key[1]
                    src = ring_ready(act, key)
                    act.activation(last_p[:, P * i:P * i + P], src[0:HIST, 0:P], ACT.Copy)
                    act.activation(last_s[:, P * i:P * i + P], src[0:NS, P:2 * P], ACT.Copy).then_inc(freed(key), 1)
                elif kind == "pool":
                    _, i, q = key
                    col, m = PIECES[q]
                    src = ring_ready(act, key)
                    if (i, q) == (1, 0):
                        drained(act, ("hist",))
                    act.activation(Y[:, 3 + i, col:col + m], src[:, 0:m], ACT.Copy,
                                   scale=pscale[:, i:i + 1]).then_inc(freed(key), 1)
                elif kind == "kd_rows":
                    i = key[1]
                    src = ring_ready(act, key)
                    if i < 4:
                        act.activation(kd_rows[:, 2 * i:2 * i + 2, :],
                                       src[:, 0:384].rearrange("p (b n) -> p b n", b=2), ACT.Copy).then_inc(freed(key), 1)
                    else:
                        act.activation(kd_rows[0:NS, 8, :], src[0:NS, 0:192], ACT.Copy)
                        act.activation(kd_meta, src[0:NMETA, 192:384], ACT.Copy).then_inc(freed(key), 1)
                elif kind == "out":
                    j = key[1]
                    src = ring_ready(act, key)
                    if j == 0:
                        act.wait_ge(d_pool_out, 16 * (NB + 1))
                    act.activation(Y[:, 0:3, NMETA + P * j:NMETA + P * j + P],
                                   src[:, 0:384].rearrange("p (g t) -> p g t", g=3), ACT.Copy).then_inc(freed(key), 1)
                elif kind == "sample_out":
                    src = ring_ready(act, key)
                    act.activation(Y[:, 0:3, LP:NT], src[:, 0:192].rearrange("p (g t) -> p g t", g=3),
                                   ACT.Copy).then_inc(freed(key), 1)
                elif kind == "meansq":
                    _, i, q = key
                    col, m = PIECES[q]
                    src = ring_ready(act, key)
                    act.activation(E[:, 3 + i, col:col + m], src[:, 0:m], ACT.Ln, bias=eps[:, :]).then_inc(freed(key), 1)
                elif kind in ("k_rows", "fv_rows"):
                    t = key[1]
                    dst = k_out if kind == "k_rows" else VR
                    m = P if t < NTILE else NMETA + NS
                    src = ring_ready(act, key)
                    if key == ("k_rows", 0):
                        act.wait_ge(o_normed, 3)
                    act.activation(dst[0:m, t, :], src[0:m, 0:384], ACT.Copy).then_inc(freed(key), 1)

            def store(c):
                src = chunk_psum(c)
                done = in_free[c % 2]
                if c == C_LF:
                    act.wait_ge(in_full, c + 1)
                    act.activation(thirds(glr), src[0:LR], ACT.Copy)
                    act.activation(thirds(logf), src[32:32 + H], ACT.Copy).then_inc(done, 1)
                elif C_PV <= c < C_PV + 2:
                    act.wait_ge(in_full, c + 1)
                    if c == C_PV:
                        act.wait_ge(b_done, 1)
                    else:
                        act.wait_ge(pool_done, 1)
                    act.activation(thirds(pv), src, ACT.Copy).then_inc(done, 1)
                elif c == C_QKB:
                    act.wait_ge(in_full, c + 1)
                    act.activation(thirds(QK[0:64, 4, :]), src[64:P], ACT.Copy).then_inc(kb_moved, 1)
                elif C_FK <= c < C_FK + 3:
                    act.wait_ge(in_full, c + 1)
                    act.activation(thirds(QK[:, c - C_FK, :]), src, ACT.Copy).then_inc(done, 1)
                elif C_FQ <= c < C_FQ + 3:
                    act.wait_ge(in_full, c + 1)
                    if c == C_FQ + 2:
                        act.wait_ge(d_state_out, 32)
                    act.activation(thirds(QK[:, 3 + c - C_FQ, :]), src, ACT.Copy, scale=HD ** -0.5).then_inc(done, 1)
                elif c in GATES:
                    act.wait_ge(in_full, c + 1)
                    act.wait_ge(o_normed, 3)
                    if c >= C_GG + 2:
                        act.wait_ge(gated, GATES.index(c) - 1)
                    act.activation(thirds(gtmp[GATES.index(c) % 2]), src, ACT.Exp, scale=-1.0).then_inc(gexp_done, 1)
                elif C_FV <= c < C_FV + 3:
                    act.wait_ge(in_full, c + 1)
                    if c == C_FV:
                        act.wait_ge(d_k_out, 16 * 10)
                    act.activation(thirds(E[:, c - C_FV, :]), src, ACT.Copy).then_inc(done, 1)

            def extra(c):
                if c == 1:
                    act.wait_ge(zf_done, 1)
                    for t in range(3):
                        drained(act, ("gate", 1, t))
                        drained(act, ("gate", 0, t))
                    parts = [(E[:, 0, :], E[:, 2, :]), (E[0:64, 1, :], E[0:64, 3, :]), (logf, ftmp)]
                    for z, t in parts:
                        act.activation(t, z, ACT.Abs).then_inc(abs_done, 1)
                    act.wait_ge(abs_done, 3)
                    for z, t in parts:
                        link(act.activation(t, t, ACT.Exp, scale=-1.0))
                    for (z, t), r in zip(parts, (P, 64, H)):
                        act.activation(t, t, ACT.Ln, bias=one[0:r, :]).then_inc(ln_done, 1)
                if c == 2:
                    act.wait_ge(b_done, 1)
                    for g, r in ((0, P), (1, 64)):
                        act.activation(E[0:r, g, :], E[0:r, 4 + g, :], ACT.Exp, scale=GATE)
                        act.activation(E[0:r, 2 + g, :], E[0:r, 4 + g, :], ACT.Exp, scale=-GATE).then_inc(e_done, 1)
                if c == 3:
                    act.wait_ge(kd_sub, 1)
                    for g, r in ((0, P), (1, 64)):
                        act.activation(E[0:r, 4 + g, :], E[0:r, 4 + g, :], ACT.Exp, scale=GATE)
                        act.activation(ebend[0:r, g, :], ebend[0:r, g, :], ACT.Exp, scale=GATE).then_inc(kd_exp, 1)
                if c == 12:
                    drained(act, ("sample_out",))
                    drained(act, ("out", 7))
                    for i in range(3):
                        act.activation(E[:, i, NMETA:NT], Y[:, i, NMETA:NT], ACT.Square).then_inc(osq_done, 1)
                if c == 13:
                    for q in range(3):
                        drained(act, ("meansq", 2, q))
                    for i in range(3):
                        act.activation(E[:, 3 + i, NMETA:NT], E[:, 3 + i, NMETA:NT], ACT.Exp,
                                       scale=-0.5).then_inc(orstd_done, 1)

            for c in range(1, NCHUNK + 1):
                store(c - 1)
                w_high(c + 1)
                for key in SIDE[c - 1]:
                    drain(key)
                extra(c - 1)

            def softmax_exp(user):
                if user[0] == "seq":
                    b = user[1]
                    act.wait_ge(smax_done, b + 1)
                    act.activation(sprob[:, b % 2, :], sprob[:, b % 2, :], ACT.Exp, bias=nmax[0:96, b % 2:b % 2 + 1],
                                   accum_out=rsum[0:96, b % 2:b % 2 + 1]).then_inc(sexp_done, 1)
                elif user[0] == "fox":
                    _, j, h = user
                    m = NMETA + P * (j + 1)
                    u = UI[user]
                    act.wait_ge(fmax_done, u + 1)
                    if u >= 3:
                        _, pj, ph = UNITS[u - 3]
                        act.wait_ge(ring_full, RI[("probsT", pj, ph, (pj + 4) // 3 - 1)] + 1)
                    act.activation(prob[:, u % 3, 0:m], s_slot(user)[:, 0:m], ACT.Exp,
                                   bias=nmax[:, 2 + u % 2:3 + u % 2],
                                   accum_out=rsum[:, 2 + u % 2:3 + u % 2]).then_inc(s_free[slot_of(user)], 1)
                else:
                    t = user[1]
                    n_ = PROJ.index(t)
                    m = P if t < NTILE else NS
                    s_ready(act, user)
                    if n_:
                        act.wait_ge(d_y, 16 * n_)
                    link(act.activation(zout[0:m, :], s_slot(user)[0:m, 0:D], ACT.Square, accum_out=zstat[0:m, 0:1]))
                    link(act.activation(zstat[0:m, 0:1], zstat[0:m, 0:1], ACT.Ln, bias=eps[0:m, :], scale=1.0 / D))
                    act.activation(zstat[0:m, 1:2], zstat[0:m, 0:1], ACT.Exp, scale=-0.5).then_inc(zstat_done, 1)

            def wo_high(k):
                if k == 0:
                    drained(act, ("s_outT", NB - 1))
                act.wait_ge(d_wo[k % 2], 16 * (k // 2 + 1))
                act.activation(woh[:, k, :], wo_raw[:, k % 2, :], ACT.Copy).then_inc(wohi_done, 1)

            def y_high(n_):
                t = PROJ[n_]
                m = P if t < NTILE else NS
                if t < NTILE:
                    for p_ in range(3):
                        drained(act, ("attend", t, p_))
                else:
                    drained(act, ("s_outT", NB - 1))
                if n_ >= 2:
                    s_ready(act, ("proj", PROJ[n_ - 2]))
                elif n_ == 1:
                    act.wait_ge(wolo_done, KT)
                act.activation(yh[n_ % 2][:, :, 0:m], Y[:, :, ycol(t):ycol(t) + m], ACT.Copy).then_inc(yhi_done, 1)

            wo_next, pending, samples_over = 0, [], False
            for kind, key in PLAN:
                if kind == "S":
                    if key[0] == "proj":
                        y_high(PROJ.index(key[1]))
                    if not (key[0] == "fox" and key[2] % 2):
                        for user in pending:
                            softmax_exp(user)
                        pending = []
                    pending.append(key)
                    if samples_over and key[0] == "fox" and not key[2] % 2:
                        for k in range(wo_next, min(wo_next + 2, KT)):
                            wo_high(k)
                        wo_next = min(wo_next + 2, KT)
                elif key[0] == "page_kT" and drains_on_act(key):
                    _, b, g = key
                    src = ring_ready(act, key)
                    act.activation(kT[:, b % 2, :, PAGE * g:PAGE * g + PAGE],
                                   src[:, 0:384].rearrange("p (g t) -> p g t", g=3), ACT.Copy).then_inc(freed(key), 1)
                elif key[0] == "probsT" and drains_on_act(key):
                    probsT_drain(act, key, lambda out, in_: act.activation(out, in_, ACT.Copy))
                elif key == ("s_outT", NB - 1):
                    samples_over = True
            for user in pending:
                softmax_exp(user)

        @block.vector
        def _(dve):
            n = [0]

            def link(ins):
                n[0] += 1
                ins.then_inc(dve_step, 1)
                dve.wait_ge(dve_step, n[0])

            def x_scale(i):
                t = XORDER[i]
                m = n_of(t)
                dve.wait_ge(rms_done, i + 1)
                v, r, f = (x[0:m, t:t + 1] for x in (ssq, rstd, refine))
                link(dve.reciprocal(r, r))
                link(dve.tensor_scalar(v, v, 1.0 / D, EPS, ALU.mult, ALU.add))
                link(dve.scalar_tensor_tensor(out=f, in0=v, scalar=r, in1=r, op0=ALU.mult, op1=ALU.mult))
                link(dve.tensor_scalar(f, f, -0.5, 1.5, ALU.mult, ALU.add))
                dve.tensor_scalar(xrows[0:m, t, :], xrows[0:m, t, :], r, f, ALU.mult, ALU.mult
                                  ).then_inc(xs_done, 1)

            def x_pre(i):
                m = n_of(XORDER[i])
                u = 4 + 2 * (i % 2)
                dve.wait_ge(xt_full, i + 1)
                if i >= 3:
                    if i % 2:
                        dve.wait_ge(xlo_done, (i - 3) // 2 + 1)
                    else:
                        dve.wait_ge(xlo_dve, (i - 4) // 2 + 1)
                src = PS[:, u:u + 2, :].rearrange("p b (k t) -> p (b k) t", t=P)[:, :, 0:m]
                dve.tensor_tensor(xg[:, i % 3, :, 0:m], src, gpre[:, :, None].to_broadcast([P, KT, m]), ALU.mult
                                  ).then_inc(xg_done, 1)

            dve.wait_ge(d_const, 16 * 8)
            x_scale(0)
            for i in range(9):
                if i + 1 < 9:
                    x_scale(i + 1)
                x_pre(i)
                if i % 2 == 0 and i:
                    x_low(dve, i - 1).then_inc(xlo_dve, 1)

            def split_heads(j):
                c0, m = GBLOCKS[j]
                if j >= 2:
                    dve.wait_ge(ring_full, RI[("out", j - 2)] + 1)
                for g, r, n_ in ((0, P, 4), (1, 64, 2)):
                    ins = dve.tensor_tensor(q_heads[j % 2][0:r, 4 * g:4 * g + n_, 0:m],
                                            E[0:r, g, c0:c0 + m][:, None, :].to_broadcast([r, n_, m]),
                                            head_of[0:r, 0:n_, None].to_broadcast([r, n_, m]), ALU.mult)
                ins.then_inc(qheads_done, 1)

            def drain(key):
                kind = key[0]
                if kind == "page_prefix":
                    src = ring_ready(dve, key)
                    dve.wait_ge(page_scanned, H)
                    dve.scalar_tensor_tensor(out=page_F, in0=page_F, scalar=-1.0,
                                             in1=src[0:NS, 0:H, None].to_broadcast([NS, H, PAGE]),
                                             op0=ALU.mult, op1=ALU.subtract).then_inc(freed(key), 1)
                elif kind == "hist":
                    src = ring_ready(dve, key)
                    for i in range(2):
                        ins = dve.tensor_copy(hx[i][:, :, 0:HIST], src[:, 128 * i:128 * i + NB * HIST].rearrange(
                            "p (b t) -> p b t", b=NB))
                    ins.then_inc(freed(key), 1)
                elif kind == "state":
                    c = key[1]
                    src = ring_ready(dve, key)
                    if c >= 3 and c % 2:
                        split_heads((c + 1) // 2)
                    if c == 0:
                        dve.tensor_copy(gstate[:, 0, 0, :], src[:, 0:DV])
                        dve.tensor_copy(gstate[0:64, 0, 1, :], src[0:64, DV:2 * DV]).then_inc(freed(key), 1)
                        return
                    drained(dve, ("state", c - 1))
                    for g, r in ((0, P), (1, 64)):
                        ins = dve.scalar_tensor_tensor(out=gstate[0:r, c % 3, g, :], in0=gstate[0:r, (c - 1) % 3, g, :],
                                                       scalar=ebend[0:r, g, c:c + 1], in1=src[0:r, DV * g:DV * g + DV],
                                                       op0=ALU.mult, op1=ALU.add)
                    ins.then_inc(freed(key), 1)
                elif kind == "scores":
                    j = key[1]
                    src = ring_ready(dve, key)
                    for i in range(2):
                        r = slice(CH * i, CH * i + CH)
                        ins = dve.tensor_tensor(aT[r, j % 2, :, r], src[r, 0:384].rearrange("p (h t) -> p h t", h=H),
                                                causal[r, None, :].to_broadcast([CH, H, CH]), ALU.mult)
                    ins.then_inc(freed(key), 1)
                elif kind == "sample_scores":
                    src = ring_ready(dve, key)
                    dve.tensor_tensor(aT[0:NS, 0, :, 0:NS], src[0:NS, 0:384].rearrange("p (h t) -> p h t", h=H),
                                      causal_s[:, None, :].to_broadcast([NS, H, NS]), ALU.mult).then_inc(freed(key), 1)
                    dve.tensor_tensor(kd_seq, kd_rows[0:NS, 8:9, :].to_broadcast([NS, NB, 192]),
                                      same_seq[:, :, None].to_broadcast([NS, NB, 192]), ALU.mult).then_inc(kdseq_done, 1)
                elif kind == "sample_state":
                    _, g, i = key
                    r = P if g == 0 else 64
                    src = ring_ready(dve, key)
                    if (g, i) == (0, 0):
                        for gg, rr in ((0, P), (1, 64)):
                            dve.tensor_tensor(gstate_s[0:rr, gg], gstate_s[0:rr, gg],
                                              ebend[0:rr, gg, 17:25, None].to_broadcast([rr, NB, DV]),
                                              ALU.mult).then_inc(s0_scaled, 1)
                        dve.wait_ge(s0_scaled, 2)
                    part = gstate_s[0:r, g, 4 * i:4 * i + 4, :]
                    dve.tensor_tensor(part, part, src[0:r, 0:4 * DV].rearrange("p (b v) -> p b v", v=DV),
                                      ALU.add).then_inc(freed(key), 1)

            def store(c):
                src = chunk_psum(c)
                done = in_free[c % 2]
                if C_GV <= c < C_GV + 3:
                    dve.wait_ge(in_full, c + 1)
                    dve.tensor_copy(thirds(Y[:, c - C_GV, :]), src).then_inc(done, 1)
                elif c == C_GKA:
                    dve.wait_ge(in_full, c + 1)
                    dve.wait_ge(kd_exp, 2)
                    dve.tensor_tensor(thirds(E[:, 2, :]), thirds(E[:, 2, :]), src, ALU.mult)
                    dve.tensor_tensor(thirds(E[:, 4, :]), thirds(E[:, 4, :]), src, ALU.mult).then_inc(done, 1)
                elif c == C_GQA:
                    dve.wait_ge(in_full, c + 1)
                    dve.scalar_tensor_tensor(out=thirds(E[:, 0, :]), in0=src, scalar=DK ** -0.5,
                                             in1=thirds(E[:, 0, :]), op0=ALU.mult, op1=ALU.mult).then_inc(done, 1)
                elif c == C_QKB:
                    dve.wait_ge(in_full, c + 1)
                    dve.wait_ge(kb_moved, 1)
                    kb = QK[0:64, 4, :]
                    dve.tensor_tensor(E[0:64, 3, :], E[0:64, 3, :], kb, ALU.mult)
                    dve.tensor_tensor(E[0:64, 5, :], E[0:64, 5, :], kb, ALU.mult)
                    dve.scalar_tensor_tensor(out=thirds(E[0:64, 1, :]), in0=src[0:64], scalar=DK ** -0.5,
                                             in1=thirds(E[0:64, 1, :]), op0=ALU.mult, op1=ALU.mult).then_inc(done, 1)
                elif c in GATES:
                    g = gtmp[GATES.index(c) % 2]
                    dve.wait_ge(gexp_done, GATES.index(c) + 1)
                    if c < C_FG:
                        y = Y[:, c - C_GG, NMETA:NT]
                        if c >= C_PG:
                            drained(dve, ("pool", 1, 2))
                            drained(dve, ("pool", 1, 1))
                        for t in range(3):
                            c0, c1 = max(TH * t, NMETA), TH * t + TH
                            yt = Y[:, c - C_GG, c0:c1]
                            ins = dve.tensor_tensor(yt, yt, src[:, t, c0 - TH * t:], ALU.mult)
                    else:
                        y, g = Y[:, 5 + c - C_FG, :], g
                        ins = dve.tensor_copy(thirds(y), src)
                    ins.then_inc(done, 1)
                    link(dve.tensor_scalar(g, g, 1.0, None, ALU.add))
                    link(dve.reciprocal(g, g))
                    chunk_stored(dve, c)
                    dve.tensor_tensor(y, y, g if c >= C_FG else g[:, NMETA:NT], ALU.mult).then_inc(gated, 1)

            def pool_windows(i):
                chunk_stored(dve, C_PV + i)
                if i == 0:
                    drained(dve, ("hist",))
                link(dve.tensor_copy(hx[i][:, :, HIST:HX], pv[:, LP:NT].rearrange("p (b t) -> p b t", t=TS)))
                if i == 1:
                    dve.wait_ge(ring_full, RI[("pool", 0, 2)] + 1)
                views = []
                for v, pa, pb_, lead, n_ in ((pv, psA, psB, 1, LP), (hx[i], hA, hB, 2, HX)):
                    cut = (lambda x, r, s0, s1, ld=lead: x[r, s0:s1] if ld == 1 else x[r, :, s0:s1])
                    views.append((v, pa, pb_, n_, cut))

                def add(dst, src, r, w):
                    for v, pa, pb_, n_, cut in views:
                        t = {"v": v, "a": pa, "b": pb_}
                        ins = dve.tensor_tensor(cut(t[dst], r, 2 * w - 1, n_), cut(t[src], r, 2 * w - 1, n_),
                                                cut(t[src], r, w - 1, n_ - w), ALU.add)
                    link(ins)

                every, low, high = slice(0, P), slice(0, 64), slice(64, P)
                add("a", "v", every, 1)
                if i == 0:
                    add("b", "a", high, 2)
                    ends = ((low, "a", 2), (high, "b", 4))
                else:
                    add("b", "a", every, 2)
                    add("a", "b", every, 4)
                    add("b", "a", high, 8)
                    ends = ((low, "a", 8), (high, "b", 16))
                for r, which, w in ends:
                    s = psA if which == "a" else psB
                    hs = hA if which == "a" else hB
                    dve.scalar_tensor_tensor(out=psA[r, NMETA:LP], in0=s[r, NMETA:LP], scalar=1.0 / w,
                                             in1=pv[r, NMETA:LP], op0=ALU.mult, op1=ALU.subtract)
                    ins = dve.scalar_tensor_tensor(out=psA[r, LP:NT].rearrange("p (b t) -> p b t", t=TS),
                                                   in0=hs[r, :, HIST:HX], scalar=1.0 / w, in1=hx[i][r, :, HIST:HX],
                                                   op0=ALU.mult, op1=ALU.subtract)
                ins.then_inc(pool_done, 1)

            def extra(c):
                if c == 0:
                    chunk_stored(dve, C_LF)
                    dve.tensor_scalar(logf, logf, bfox[:, 0:1], None, ALU.add).then_inc(zf_done, 1)
                if c == 1:
                    dve.wait_ge(abs_done, 3)
                    dve.wait_ge(zf_done, 1)
                    parts = [(E[:, 0, :], E[:, 2, :]), (E[0:64, 1, :], E[0:64, 3, :]), (logf, ftmp)]
                    for z, t in parts:
                        link(dve.tensor_scalar(z, z, 0.0, None, ALU.min))
                    dve.wait_ge(ln_done, 3)
                    for z, t in parts:
                        link(dve.tensor_tensor(z, z, t, ALU.subtract))
                    dve.wait_ge(consts_set, 2)
                    for g, r in ((0, P), (1, 64)):
                        b = E[0:r, 4 + g, :]
                        link(dve.tensor_tensor_scan(b, reset[0:r, :], E[0:r, g, :], 0.0, ALU.mult, ALU.add))
                        dve.tensor_copy(ebend[0:r, g, 0:1], b[:, NMETA - 1:NMETA])
                        dve.tensor_copy(ebend[0:r, g, 1:17, None],
                                        b[:, NMETA:LP].rearrange("p (c t) -> p c t", t=CH)[:, :, CH - 1:CH])
                        link(dve.tensor_copy(ebend[0:r, g, 17:25, None],
                                             b[:, LP:NT].rearrange("p (c t) -> p c t", t=TS)[:, :, TS - 1:TS]))
                    dve.tensor_tensor_scan(f_sum[:, :], reset[0:H, LP:NT], logf[:, LP:NT], 0.0, ALU.mult, ALU.add
                                           ).then_inc(b_done, 1)
                    link(dve.tensor_tensor_scan(fcum[:, 0:LP], ones_row[0:H, :], logf[:, 0:LP], 0.0, ALU.mult, ALU.add))
                if c == 2:
                    dve.wait_ge(e_done, 2)
                    for g, r in ((0, P), (1, 64)):
                        for s, e_, c0, c1, w in ((0, NMETA, 0, 1, NMETA), (NMETA, LP, 1, 17, CH), (LP, NT, 17, 25, TS)):
                            b = E[0:r, 4 + g, s:e_].rearrange("p (c t) -> p c t", t=w)
                            ins = dve.tensor_tensor(b, ebend[0:r, g, c0:c1, None].to_broadcast([r, c1 - c0, w]), b,
                                                    ALU.subtract)
                    ins.then_inc(kd_sub, 1)
                if c == 3:
                    f, r1 = fcum[:, 0:LP], ftmp[:, 0:LP]
                    link(dve.tensor_scalar(negF[0:H, :], f, -1.0, None, ALU.mult))
                    link(dve.scalar_tensor_tensor(out=r1, in0=f, scalar=-1.0, in1=negF[0:H, :], op0=ALU.mult,
                                                  op1=ALU.subtract))
                    link(dve.tensor_copy(negF[32:32 + H, :], r1))
                    link(dve.tensor_copy(f, negF[32:32 + H, :]))
                    link(dve.tensor_tensor(r1, r1, f, ALU.subtract))
                    dve.tensor_copy(negF[64:64 + H, :], r1).then_inc(negF_done, 1)
                if c == 2:
                    dve.wait_ge(d_lf, 16)
                    for h in range(H):
                        dve.tensor_tensor_scan(page_F[:, h, :], ones_row[:, 0:PAGE], page_lf[:, :, h], 0.0,
                                               ALU.mult, ALU.add).then_inc(page_scanned, 1)
                if c == C_QKB:
                    dve.wait_ge(in_free[0], C_QKB // 2 + 1)
                    for x in (gstate[64:P, :, 1, :], gstate_s[64:P, 1], q_heads[0][64:P, 4:H, :], q_heads[1][64:P, 4:H, :]):
                        dve.memset(x, 0.0)
                    dve.wait_ge(ring_full, RI[("pool", 1, 2)] + 1)
                    dve.memset(aT[:, :, :, :], 0.0)
                    split_heads(0)
                    split_heads(1)
                if c in (C_PV, C_PV + 1):
                    pool_windows(c - C_PV)
                if c == C_PV + 1:
                    dve.wait_ge(d_fl, 16)
                    fs = f_sum[:, :].rearrange("h (b t) -> h b t", t=TS)
                    dve.tensor_tensor(fs, f_last[:, :, None].to_broadcast([H, NB, TS]), fs, ALU.subtract
                                      ).then_inc(fnew_done, 1)
                if c == 13:
                    dve.wait_ge(orstd_done, 3)
                    for i in range(3):
                        y = Y[:, i, NMETA:NT]
                        dve.scalar_tensor_tensor(out=y, in0=y, scalar=gnorm[:, 0:1], in1=E[:, 3 + i, NMETA:NT],
                                                 op0=ALU.mult, op1=ALU.mult).then_inc(o_normed, 1)
                    dve.wait_ge(o_normed, 3)

            for c in range(1, NCHUNK + 1):
                store(c - 1)
                for key in SIDE[c - 1]:
                    drain(key)
                extra(c - 1)

            dve.wait_ge(gated, len(GATES))
            dve.wait_ge(qdiag_zero, 1)
            for p_ in range(3):
                for i in range(2):
                    r = slice(64 * i, 64 * i + 64)
                    ins = dve.tensor_copy(q_diag[r, p_, :, TS * i:TS * i + TS],
                                          QK[r, 3 + p_, LP:NT].rearrange("p (b t) -> p b t", t=TS))
            ins.then_inc(qdiag_done, 1)
            dve.memset(s_rows, 0.0).then_inc(srows_zero, 1)

            def row_max(user):
                if user[0] == "seq":
                    b = user[1]
                    u = b % 2
                    s_ready(dve, user)
                    if b == 0:
                        dve.wait_ge(sbias_zero, 1)
                    dve.wait_ge(d_bias[u], 16 * H * (b // 2 + 1))
                    if b >= 2:
                        dve.wait_ge(ring_full, RI[("s_probsT_b", b - 2)] + 1)
                    dve.tensor_tensor_reduce(sprob[:, u, :], s_slot(user)[0:96, 0:PAST + TS], sbias[:, u, :], 1.0,
                                             -3e38, ALU.add, ALU.max, nmax[0:96, 4 + u:5 + u]
                                             ).then_inc(s_free[slot_of(user)], 1)
                    s_emptied(dve, user)
                    dve.tensor_scalar(nmax[0:96, u:u + 1], nmax[0:96, 4 + u:5 + u], -1.0, None, ALU.mult
                                      ).then_inc(smax_done, 1)
                elif user[0] == "fox":
                    u = UI[user]
                    s_ready(dve, user)
                    dve.tensor_reduce(nmax[:, 2 + u % 2:3 + u % 2], s_slot(user)[:, 0:NMETA + P * (user[1] + 1)],
                                      AX.X, ALU.max, negate=True).then_inc(fmax_done, 1)

            def finish(user):
                if user[0] == "seq":
                    b = user[1]
                    u = b % 2
                    dve.wait_ge(sexp_done, b + 1)
                    link(dve.reciprocal(rinv[0:96, u:u + 1], rsum[0:96, u:u + 1]))
                    dve.tensor_scalar(sprob[:, u, :], sprob[:, u, :], rinv[0:96, u:u + 1], None, ALU.mult
                                      ).then_inc(sprob_done, 1)
                elif user[0] == "fox":
                    u = UI[user]
                    m = NMETA + P * (user[1] + 1)
                    s_emptied(dve, user)
                    link(dve.reciprocal(rinv[:, 2 + u % 2:3 + u % 2], rsum[:, 2 + u % 2:3 + u % 2]))
                    dve.tensor_scalar(prob[:, u % 3, 0:m], prob[:, u % 3, 0:m], rinv[:, 2 + u % 2:3 + u % 2], None,
                                      ALU.mult).then_inc(fprob_done, 1)
                else:
                    t = user[1]
                    n_ = PROJ.index(t)
                    m = P if t < NTILE else NS
                    dve.wait_ge(zstat_done, n_ + 1)
                    if n_ == 0:
                        dve.wait_ge(d_post, 16)
                    dve.scalar_tensor_tensor(out=zout[0:m, :], in0=s_slot(user)[0:m, 0:D], scalar=zstat[0:m, 1:2],
                                             in1=gpost[0:m, :], op0=ALU.mult, op1=ALU.mult
                                             ).then_inc(s_free[slot_of(user)], 1)
                    s_emptied(dve, user)
                    dve.wait_ge(d_xres, 16 * (n_ + 1))
                    dve.tensor_tensor(zout[0:m, :], zout[0:m, :], xres[0:m, :], ALU.add).then_inc(y_done, 1)

            pending = []
            for kind, key in PLAN:
                if kind == "S":
                    if not (key[0] == "fox" and key[2] % 2):
                        for user in pending:
                            finish(user)
                        pending = []
                    pending.append(key)
                    row_max(key)
                    continue
                if key[0] == "page_kT" and not drains_on_act(key):
                    _, b, g = key
                    src = ring_ready(dve, key)
                    dve.tensor_copy(kT[:, b % 2, :, PAGE * g:PAGE * g + PAGE],
                                    src[:, 0:384].rearrange("p (g t) -> p g t", g=3)).then_inc(freed(key), 1)
                elif key[0] == "probsT" and not drains_on_act(key):
                    probsT_drain(dve, key, dve.tensor_copy)
                elif key[0] in ("s_probsT_a", "s_probsT_b"):
                    u = key[1] % 2
                    g0 = 0 if key[0] == "s_probsT_a" else 4
                    src = ring_ready(dve, key)
                    ins = dve.tensor_copy(sprobT[u][:, g0:g0 + 4, :].rearrange("p g (a q) -> p g a q", a=3),
                                          src[:, 0:384].rearrange("p (g a q) -> p g a q", g=4, a=3)[:, :, :, 0:16])
                    if g0:
                        ins = dve.tensor_copy(sprobT[u][0:TS, NPAGE, :].rearrange("p (a q) -> p a q", a=3),
                                              src[0:TS, 384:480].rearrange("p (a q) -> p a q", a=3)[:, :, 0:16])
                    ins.then_inc(freed(key), 1)
                elif key[0] == "s_attend":
                    src = ring_ready(dve, key)
                    dve.wait_ge(srows_zero, 1)
                    for p_ in range(3):
                        r = slice(32 * p_, 32 * p_ + 16)
                        ins = dve.tensor_copy(s_rows[r, :], src[r, 0:P])
                    ins.then_inc(freed(key), 1)
                elif key[0] == "s_outT":
                    src = ring_ready(dve, key)
                    c0 = LP + TS * key[1]
                    for i in range(2):
                        r = slice(64 * i, 64 * i + 64)
                        y = Y[r, 5:8, c0:c0 + TS]
                        ins = dve.tensor_tensor(y, y, src[r, 0:96].rearrange("p (g q) -> p g q", g=3)[
                            :, :, TS * i:TS * i + TS], ALU.mult)
                    ins.then_inc(freed(key), 1)
                elif key[0] == "attend":
                    _, j, p_ = key
                    src = ring_ready(dve, key)
                    y = Y[:, 5 + p_, NMETA + P * j:NMETA + P * j + P]
                    dve.tensor_tensor(y, y, src[:, 0:P], ALU.mult).then_inc(freed(key), 1)
            for user in pending:
                finish(user)

        @block.tensor
        def _(pe):
            pe.wait_ge(consts_set, 1)
            pe.wait_ge(d_const, 16 * 8)
            def product(out, parts, rhs_of):
                for k in range(KT):
                    sh, sl = parts(k)
                    mh, ml = rhs_of(k)
                    pe.matmul(out, sh, mh, start=(k == 0), stop=False)
                    pe.matmul(out, sh, ml, start=False, stop=False)
                    ins = pe.matmul(out, sl, mh, start=False, stop=(k == KT - 1))
                return ins

            def x_transposes(i):
                t = XORDER[i]
                u = 4 + 2 * (i % 2)
                m = n_of(t)
                pe.wait_ge(xs_done, i + 1)
                if i >= 2:
                    pe.wait_ge(xg_done, i - 1)
                for k in range(KT):
                    ins = pe.transpose(PS[:, u + k // 4, P * (k % 4):P * (k % 4) + m],
                                       xrows[0:m, t, P * k:P * k + P], ident[0:m, 0:m])
                ins.then_inc(xt_full, 1)

            def project_in(c):
                pe.wait_ge(wlo_done, c + 1)
                pe.wait_ge(whi_done, c + 1)
                if c >= 2:
                    chunk_stored(pe, c - 2)
                if c == 1:
                    pe.wait_ge(xg_done, 9)
                jobs = SIDE[c - 1] if c else []
                steps, first, given = 3 * KT, FIRST_STEP.get(c - 1, 3), 0
                for t in range(3):
                    if c == 0:
                        for i in ((), (6, 7, 8), ())[t]:
                            x_transposes(i)
                        pe.wait_ge(xlo_done, (2, 4, 5)[t])
                        pe.wait_ge(xlo_dve, (2, 3, 4)[t])
                    cols = slice(TH * t, TH * t + TH)
                    out = PS[:, 3 * (c % 2) + t, 0:TH]
                    for k in range(KT):
                        high, low = wh[:, c % 2, k, :], wl[:, c % 2, k, :]
                        pe.matmul(out, high, xh[:, k, cols], start=(k == 0), stop=False)
                        pe.matmul(out, high, xl[:, k, cols], start=False, stop=False)
                        ins = pe.matmul(out, low, xh[:, k, cols], start=False, stop=(k == KT - 1))
                        if (t, k) == (2, KT - 1):
                            ins.then_inc(in_full, 1)
                        step = KT * t + k + 1
                        upto = max(0, len(jobs) * (step - first) // (steps - first)) if step > first else 0
                        for key in jobs[given:upto]:
                            side(key)
                        given = max(given, upto)

            def side(key):
                kind = key[0]
                out = ring_take(pe, key)
                if kind == "gate":
                    _, g, t = key
                    if (g, t) == (0, 0):
                        chunk_stored(pe, C_LF)
                    m = P if g == 0 else 64
                    ins = pe.matmul(out[0:m, 0:TH], w_up[:, P * g:P * g + m], glr[:, TH * t:TH * t + TH],
                                    start=True, stop=True)
                elif kind == "logf_rows":
                    pe.wait_ge(b_done, 1)
                    for t in range(9):
                        m = P if t < NTILE else NMETA + NS
                        ins = pe.transpose(out[0:m, H * t:H * t + H], logf[:, P * t:P * t + m], ident[0:H, 0:H])
                elif kind == "page_prefix":
                    pe.wait_ge(page_scanned, H)
                    ins = pe.matmul(out[0:NS, 0:H], page_before[:, :], page_F[:, :, PAGE - 1], start=True, stop=True)
                elif kind == "v_rows":
                    b = key[1]
                    col, m = GBLOCKS[b]
                    if b == 0:
                        chunk_stored(pe, C_GV + 1)
                        chunk_stored(pe, C_GV + 2)
                    for i in range(3):
                        ins = pe.transpose(out[0:m, P * i:P * i + P], Y[:, i, col:col + m], ident[:, :])
                elif kind == "hist":
                    pe.wait_ge(d_hist, 16)
                    m = NB * HIST
                    for i in range(2):
                        ins = pe.transpose(out[:, 128 * i:128 * i + m], hist_rows[:, P * i:P * i + P], ident[0:m, 0:m])
                elif kind == "pool_last":
                    i = key[1]
                    chunk_stored(pe, C_PV + i)
                    pe.transpose(out[0:HIST, 0:P], pv[:, LP - HIST:LP], ident[:, :])
                    ins = pe.transpose(out[0:NS, P:2 * P], pv[:, LP:NT], ident[:, :])
                elif kind == "pool":
                    _, i, q = key
                    col, m = PIECES[q]
                    pe.wait_ge(pool_done, i + 1)
                    pe.wait_ge(d_poolw, 16 * 4)
                    ins = pe.matmul(out[:, 0:m], pool_w[:, i, :], psA[:, col:col + m], start=True, stop=True)
                elif kind == "kd_rows":
                    i = key[1]
                    if i == 0:
                        chunk_stored(pe, C_QKB)
                        chunk_stored(pe, C_GQA)
                        drained(pe, ("pool", 1, 2))
                    for n_, b in enumerate((2 * i, 2 * i + 1)):
                        col, m = GBLOCKS[b]
                        pe.transpose(out[0:m, 192 * n_:192 * n_ + P], E[:, 4, col:col + m], ident[:, :])
                        ins = pe.transpose(out[0:m, 192 * n_ + P:192 * n_ + 192], E[0:64, 5, col:col + m],
                                           ident[0:64, 0:64])
                elif kind == "state":
                    c = key[1]
                    b, r0, m = (9, 0, NMETA) if c == 0 else ((c - 1) // 2, CH * ((c - 1) % 2), CH)
                    if c == 0:
                        drained(pe, ("kd_rows", 4))
                        drained(pe, ("kd_rows", 3))
                        drained(pe, ("v_rows", 9))
                        drained(pe, ("v_rows", 8))
                    rows = slice(r0, r0 + m)
                    kd = kd_meta if c == 0 else kd_rows[rows, b, :]
                    for h in range(H):
                        ins = pe.matmul(out[head_rows(h), DV * (h // 4):DV * (h // 4) + DV],
                                        kd[:, DK * h:DK * h + DK], VR[rows, b, DV * h:DV * h + DV],
                                        start=True, stop=True)
                elif kind == "scores":
                    j = key[1]
                    pe.wait_ge(qheads_done, j + 1)
                    for i in range(2):
                        c0 = NMETA + P * j + CH * i
                        for h in range(H):
                            r = group_rows(h)
                            ins = pe.matmul(out[CH * i:CH * i + CH, CH * h:CH * h + CH], E[r, 2 + h // 4, c0:c0 + CH],
                                            q_heads[j % 2][r, h, CH * i:CH * i + CH], start=True, stop=True)
                elif kind == "out":
                    j = key[1]
                    drained(pe, ("scores", j))
                    drained(pe, ("state", 2 * j + 1))
                    drained(pe, ("state", 2 * j))
                    for h in range(H):
                        rows = slice(64 * (h % 2), 64 * (h % 2) + 64)
                        dst = out[rows, P * (h // 2):P * (h // 2) + P]
                        pe.matmul(dst, VR[:, j, DV * h:DV * h + DV], aT[:, j % 2, h, :], start=True, stop=False,
                                  skip_group_check=True)
                        for i in range(2):
                            ins = pe.matmul(dst[:, CH * i:CH * i + CH], gstate[:, (2 * j + i) % 3, h // 4, :],
                                            q_heads[j % 2][:, h, CH * i:CH * i + CH], start=False, stop=(i == 1),
                                            skip_group_check=True)
                elif kind == "sample_scores":
                    pe.wait_ge(qheads_done, NTILE + 1)
                    for h in range(H):
                        r = group_rows(h)
                        ins = pe.matmul(out[0:NS, CH * h:CH * h + CH], E[r, 2 + h // 4, LP:NT],
                                        q_heads[0][r, h, 0:NS], start=True, stop=True)
                elif kind == "sample_out":
                    drained(pe, ("sample_scores",))
                    pe.wait_ge(d_s0, 32)
                    for h in range(H):
                        rows, c0 = slice(64 * (h % 2), 64 * (h % 2) + 64), NS * (h // 2)
                        pe.matmul(out[rows, c0:c0 + NS], VR[0:NS, 8, DV * h:DV * h + DV], aT[0:NS, 0, h, 0:NS],
                                  start=True, stop=False, skip_group_check=True)
                        for b in range(NB):
                            ins = pe.matmul(out[rows, c0 + TS * b:c0 + TS * b + TS], gstate_s[:, h // 4, b, :],
                                            q_heads[0][:, h, TS * b:TS * b + TS],
                                            start=False, stop=(b == NB - 1), skip_group_check=True)
                elif kind == "sample_state":
                    _, g, i = key
                    pe.wait_ge(kdseq_done, 1)
                    for h in range(4 * g, min(4 * g + 4, H)):
                        for b in range(4):
                            ins = pe.matmul(out[head_rows(h), DV * b:DV * b + DV],
                                            kd_seq[:, 4 * i + b, DK * h:DK * h + DK], VR[0:NS, 8, DV * h:DV * h + DV],
                                            start=True, stop=True)
                elif kind == "meansq":
                    _, i, q = key
                    col, m = PIECES[q]
                    pe.wait_ge(osq_done, i + 1)
                    ins = pe.matmul(out[:, 0:m], block_mean[:, :], E[:, i, col:col + m], start=True, stop=True)
                elif kind in ("k_rows", "fv_rows"):
                    t = key[1]
                    src = QK if kind == "k_rows" else E
                    last = C_FK if kind == "k_rows" else C_FV
                    if t == 0:
                        chunk_stored(pe, last + 1)
                        chunk_stored(pe, last + 2)
                    m = P if t < NTILE else NMETA + NS
                    for i in range(3):
                        ins = pe.transpose(out[0:m, P * i:P * i + P], src[:, i, P * t:P * t + m], ident[:, :])
                ins.then_inc(ring_full, 1)

            for i in range(6):
                x_transposes(i)
            for c in range(NCHUNK):
                project_in(c)

            def page_kT(key):
                _, b, g = key
                out = ring_take(pe, key)
                if g == 0:
                    pe.wait_ge(d_k[b % 2], 16 * NPAGE * (b // 2 + 1))
                for i in range(3):
                    ins = pe.transpose(out[:, P * i:P * i + P], pages[b % 2][:, 0, g, P * i:P * i + P], ident[:, :])
                ins.then_inc(ring_full, 1)

            def sample_scores(user):
                b = user[1]
                s_taken(pe, user)
                out = s_slot(user)
                drained(pe, ("page_kT", b, NPAGE - 1))
                drained(pe, ("page_kT", b, NPAGE - 2))
                pe.wait_ge(qdiag_done, 1)
                for half in range(2):
                    for p_ in range(3):
                        pe.matmul(out[32 * p_:32 * p_ + 32, 512 * half:512 * half + 512], q_diag[:, p_, b, :],
                                  kT[:, b % 2, p_, 512 * half:512 * half + 512], start=True, stop=True)
                for p_ in range(3):
                    pe.matmul(out[32 * p_:32 * p_ + 32, PAST:PAST + TS], q_diag[:, p_, b, :],
                              QK[:, p_, LP + TS * b:LP + TS * b + TS], start=True, stop=False)
                pe.matmul(out[0:96, PAST:PAST + TS], pick_q[:, :], mask_new[:, :], start=False, stop=True
                          ).then_inc(s_full, 1)

            def sample_probsT(key):
                b = key[1]
                u = b % 2
                out = ring_take(pe, key)
                pe.wait_ge(sprob_done, b + 1)
                g0 = 0 if key[0] == "s_probsT_a" else 4
                for g in range(4):
                    c0 = PAGE * (g0 + g)
                    ins = pe.transpose(out[:, 96 * g:96 * g + 96], sprob[:, u, c0:c0 + PAGE], ident[0:96, 0:96])
                if g0:
                    ins = pe.transpose(out[0:TS, 384:480], sprob[:, u, PAST:PAST + TS], ident[0:96, 0:96])
                ins.then_inc(ring_full, 1)

            def sample_attend(key):
                b = key[1]
                u = b % 2
                drained(pe, ("s_probsT_a", b))
                drained(pe, ("s_probsT_b", b))
                out = ring_take(pe, key)
                pe.wait_ge(d_v[u], 16 * (NPAGE + 1) * (b // 2 + 1))
                for g in range(NPAGE + 1):
                    for p_ in range(3):
                        cols, qs = slice(P * p_, P * p_ + P), slice(16 * p_, 16 * p_ + 16)
                        v = pages[u][:, 1, g, cols] if g < NPAGE else v_new[:, u, cols]
                        pt = sprobT[u][:, g, qs] if g < NPAGE else sprobT[u][0:TS, g, qs]
                        ins = pe.matmul(out[32 * p_:32 * p_ + 16, 0:P], pt, v, start=(g == 0), stop=(g == NPAGE))
                ins.then_inc(ring_full, 1)

            def sample_outT(key):
                drained(pe, ("s_attend", key[1]))
                out = ring_take(pe, key)
                pe.transpose(out[:, 0:96], s_rows, ident[0:96, 0:96]).then_inc(ring_full, 1)

            pe.wait_ge(negF_done, 1)
            chunk_stored(pe, NCHUNK - 1)
            chunk_stored(pe, NCHUNK - 2)

            def fox_scores(j, p_):
                m = NMETA + P * (j + 1)
                q0 = NMETA + P * j
                heads = [(h, s_slot(("fox", j, h)), slice(64 * (h % 2), 64 * (h % 2) + 64))
                         for h in (2 * p_, 2 * p_ + 1)]
                for h, _, _ in heads:
                    s_taken(pe, ("fox", j, h))
                for c0 in range(0, m, 512):
                    c1 = min(c0 + 512, m)
                    for h, out, rows in heads:
                        pe.matmul(out[:, c0:c1], QK[rows, 3 + p_, q0:q0 + P], QK[rows, p_, c0:c1],
                                  start=True, stop=False)
                for h, out, rows in heads:
                    for c0 in range(0, m, 512):
                        c1 = min(c0 + 512, m)
                        d0 = max(c0, q0)
                        ins = pe.matmul(out[:, c0:c1], pick_row[0:64 + H, h, :], negF[0:64 + H, c0:c1],
                                        start=False, stop=(d0 >= c1))
                        if d0 < c1:
                            ins = pe.matmul(out[:, d0:c1], identb[:, :], mask_neg[:, d0 - q0:c1 - q0],
                                            start=False, stop=True)
                    ins.then_inc(s_full, 1)

            def project_out(user):
                t = user[1]
                n_ = PROJ.index(t)
                m = P if t < NTILE else NS
                s_taken(pe, user)
                out = s_slot(user)
                pe.wait_ge(yhi_done, n_ + 1)
                pe.wait_ge(ylo_done, n_ + 1)
                pe.wait_ge(wolo_done, KT)
                for half in range(2):
                    cols = slice(512 * half, 512 * half + 512)
                    ins = product(out[0:m, cols], lambda k: (yh[n_ % 2][:, k, 0:m], yl[n_ % 2][:, k, 0:m]),
                                  lambda k: (woh[:, k, cols], wol[k][:, cols]))
                ins.then_inc(s_full, 1)

            fox_scores(0, 0)
            for key in SIDE[NCHUNK - 1]:
                side(key)
            for kind, key in PLAN:
                if kind == "S" and key[0] == "fox":
                    if key[2] % 2 == 0 and key[1:] != (0, 0):
                        fox_scores(key[1], key[2] // 2)
                elif kind == "S" and key[0] == "seq":
                    sample_scores(key)
                elif kind == "S":
                    project_out(key)
                elif key[0] == "page_kT":
                    page_kT(key)
                elif key[0] in ("s_probsT_a", "s_probsT_b"):
                    sample_probsT(key)
                elif key[0] == "s_attend":
                    sample_attend(key)
                elif key[0] == "s_outT":
                    sample_outT(key)
                elif key[0] == "probsT":
                    _, j, h, i = key
                    u = UI[("fox", j, h)]
                    out = ring_take(pe, key)
                    pe.wait_ge(fprob_done, u + 1)
                    for n_, b in enumerate(range(3 * i, min(3 * i + 3, j + 2))):
                        w = P if b <= j else NMETA
                        ins = pe.transpose(out[0:w, P * n_:P * n_ + P], prob[:, u % 3, P * b:P * b + w], ident[:, :])
                    ins.then_inc(ring_full, 1)
                else:
                    _, j, p_ = key
                    out = ring_take(pe, key)
                    for h in (2 * p_, 2 * p_ + 1):
                        for i in range((j + 4) // 3):
                            drained(pe, ("probsT", j, h, i))
                    for b in range(j + 2):
                        w = P if b <= j else NMETA
                        for i in range(2):
                            h = 2 * p_ + i
                            ins = pe.matmul(out[64 * i:64 * i + 64, 0:P], VR[0:w, b, HD * h:HD * h + HD],
                                            probT[0:w, UI[("fox", j, h)] % 2, b, :], start=(b == 0), stop=(b == j + 1))
                    ins.then_inc(ring_full, 1)


INPUTS = ["x_prompt", "x_sample", "cache_fox_k", "cache_fox_v", "cache_fox_logf", "state_gla", "state_pool",
          "page_table", "meta_tokens", "norm_pre", "norm_post", "w_in", "gla_w_up", "gla_b_gate", "gla_norm",
          "pool_w", "pool_scale", "fox_b_f", "w_out"]
OUTPUTS = [("y_p", (1, SEQ, D)), ("y_s", (NB, TS, D)), ("fox_kp", (1, 1, LP, H, HD)), ("fox_vp", (1, 1, LP, H, HD)),
           ("logf_p", (1, 1, LP, H)), ("gla_p", (1, 1, H, DK, DV)), ("pool_p", (1, 1, HIST, 256)),
           ("fox_ks", (1, NB, TS, H, HD)), ("fox_vs", (1, NB, TS, H, HD)), ("logf_s", (1, NB, TS, H)),
           ("gla_s", (1, NB, H, DK, DV)), ("pool_s", (1, NB, HIST, 256))]


def kernel(**inputs):
    import numpy as np
    import concourse.bacc as bacc
    from concourse.bass_utils import run_bass_kernel_spmd

    nc = bacc.Bacc("TRN2", target_bir_lowering=False, num_devices=1)
    arrays, a, o = {}, {}, {}
    for name in INPUTS:
        x = np.ascontiguousarray(inputs[name])
        arrays[f"in_{name}_dram"] = x
        a[name] = nc.dram_tensor(f"in_{name}_dram", x.shape, mybir.dt.from_np(x.dtype), kind="ExternalInput").ap()
    for name, shape in OUTPUTS:
        o[name] = nc.dram_tensor(f"out_{name}_dram", shape, F32, kind="ExternalOutput").ap()
    build(nc, a, o)
    r = run_bass_kernel_spmd(nc, [arrays], core_ids=[0])
    return tuple(r.results[0][f"out_{name}_dram"] for name, _ in OUTPUTS)
```

```python
from contextlib import ExitStack

import concourse.bass as bass
from concourse import mybir

F32 = mybir.dt.float32
F32R = mybir.dt.float32r
BF16 = mybir.dt.bfloat16
I32 = mybir.dt.int32
ALU = mybir.AluOpType
ACT = mybir.ActivationFunctionType
AX = mybir.AxisListType

P = 128
D = 1024
KT = D // P
SEQ, NMETA = 1024, 16
NB, TS = 8, 8
LP = NMETA + SEQ
NS = NB * TS
NT = LP + NS
TH = NT // 3
NTILE = SEQ // P
H, HD = 6, 64
DK, DV = 32, 64
LR = 16
PAGE, NPAGE = 128, 8
PAST = PAGE * NPAGE
HIST = 15
CH = 64
NCH = SEQ // CH
EPS = 1e-6
GATE = 1.0 / 16.0
NEG = -1e30
SLOT = 384

W_GQ, W_GK, W_GV, W_LR, W_GG = 0, 192, 384, 768, 784
W_PV, W_PG, W_FQ, W_FK, W_FV, W_FF, W_FG = 1168, 1424, 1680, 2064, 2448, 2832, 2838

CHUNKS = [[(W_LR, 0, LR), (W_FF, 32, H)]]
CHUNKS += [[(W_GV + P * i, 0, P)] for i in range(3)]
CHUNKS += [[(W_PV + P * i, 0, P)] for i in range(2)]
CHUNKS += [[(W_GK, 0, P)], [(W_GQ, 0, P)], [(W_GQ + P, 0, 64), (W_GK + P, 64, 64)]]
CHUNKS += [[(W_FK + P * i, 0, P)] for i in range(3)]
CHUNKS += [[(W_FQ + P * i, 0, P)] for i in range(3)]
CHUNKS += [[(W_GG + P * i, 0, P)] for i in range(3)]
CHUNKS += [[(W_PG + P * i, 0, P)] for i in range(2)]
CHUNKS += [[(W_FG + P * i, 0, P)] for i in range(3)]
CHUNKS += [[(W_FV + P * i, 0, P)] for i in range(3)]
C_LF, C_GV, C_PV, C_GKA, C_GQA, C_QKB = 0, 1, 4, 6, 7, 8
C_FK, C_FQ, C_GG, C_PG, C_FG, C_FV = 9, 12, 15, 18, 20, 23
NCHUNK = len(CHUNKS)
GATES = list(range(C_GG, C_FG + 3))

GBLOCKS = [(NMETA + P * j, P) for j in range(NTILE)] + [(LP, NS), (0, NMETA)]
PIECES = [(NMETA, SLOT), (NMETA + SLOT, SLOT), (NMETA + 2 * SLOT, NT - NMETA - 2 * SLOT)]


def side_jobs():
    s = {c: [] for c in range(NCHUNK)}
    s[0] = [("gate", g, t) for g in range(2) for t in range(3)]
    s[3] = [("logf_rows",), ("page_prefix",)]
    s[4] = [("v_rows", b) for b in range(10)] + [("hist",), ("pool_last", 0)]
    s[5] = [("pool_last", 1)] + [("pool", 0, i) for i in range(3)]
    s[6] = [("pool", 1, i) for i in range(3)]
    s[8] = [("kd_rows", i) for i in range(5)] + [("state", 0)]
    gla = []
    for j in range(NTILE):
        if j:
            gla += [("out", j - 1)]
        gla += [("scores", j), ("state", 2 * j + 1), ("state", 2 * j + 2)]
    gla += [("sample_scores",), ("out", 7), ("sample_out", 0), ("sample_out", 1), ("sample_out", 2)]
    gla += [("sample_state", g, i) for g in range(2) for i in range(2)]
    for c in range(4):
        s[9 + c] = gla[len(gla) * c // 4:len(gla) * (c + 1) // 4]
    s[13] = [("meansq", i, q) for i in range(3) for q in range(3)]
    s[14] = [("k_rows", t) for t in range(9)]
    s[25] = [("fv_rows", t) for t in range(9)]
    return s


STEPS = {0: (2, 14), 4: (2, 24), 5: (14, 24), 6: (12, 24), 8: (6, 24), 13: (8, 20), 14: (12, 24)}


SIDE = side_jobs()


def parts(j):
    n = -(-(j + 2) // 4)
    return [range((j + 2) * i // n, (j + 2) * (i + 1) // n) for i in range(n)]


def plan():
    units = [(j, p) for j in range(NTILE) for p in range(3)]
    steps = []
    for b in range(NB):
        keys = [("R", ("page_kT", b, g)) for g in range(NPAGE)]
        before = [("R", (k, b - 1)) for k in ("s_probsT_a", "s_probsT_b", "s_attend", "s_outT")] if b else []
        steps += keys[:3] + before[:1] + keys[3:5] + before[1:2] + keys[5:] + before[2:3]
        steps += [("S", ("seq", b))] + before[3:]
    tail = [("R", (k, NB - 1)) for k in ("s_probsT_a", "s_probsT_b", "s_attend", "s_outT")]
    last = 3 * SAMPLES_END
    weight = [j + 3 for j, _ in units[1:last]]
    order, given = [], 0

    def post(j, p):
        out = []
        for h in (2 * p, 2 * p + 1):
            out += [("R", ("probsT", j, h, i)) for i in range(len(parts(j)))]
        return out + [("R", ("attend", j, p))]

    for n, (j, p) in enumerate(units):
        order += [("S", ("fox", j, 2 * p)), ("S", ("fox", j, 2 * p + 1))]
        mine = []
        if 1 <= n < last:
            upto = round(len(steps) * sum(weight[:n]) / sum(weight))
            mine, given = steps[given:upto], upto
        if n == last + 1:
            mine = tail
        behind = post(*units[n - 1]) if n else []
        moves, products = behind[:-1], behind[-1:]
        cut = next((i for i, (t, _) in enumerate(mine) if t == "S"), len(mine))
        first, rest = mine[:cut], mine[cut:]
        k = max(len(first), len(moves), 1)
        for i in range(k):
            order += moves[i * len(moves) // k:(i + 1) * len(moves) // k]
            order += first[i * len(first) // k:(i + 1) * len(first) // k]
        if rest and rest[-1][0] != "S":
            order += rest[:-1] + products + rest[-1:]
        else:
            order += rest + products
    order.append(("S", ("proj", NTILE)))
    order += post(*units[-1])
    order += [("S", ("proj", t)) for t in range(NTILE)]

    out, scored, k = [], [], KT
    for t, key in order:
        if t == "S" and key[0] == "proj":
            out.append(("Y", key))
        second_head = key[0] == "fox" and key[2] % 2
        if (t == "S" and not second_head) or (key[0] == "s_probsT_a" and ("seq", key[1]) in scored):
            out += [("E", user) for user in scored]
            scored = []
        out.append((t, key))
        if t == "S":
            scored.append(key)
        if key == ("s_outT", NB - 1):
            k = 0
        if t == "S" and key[0] == "fox" and not second_head:
            out += [("W", i) for i in range(k, min(k + 2, KT))]
            k = min(k + 2, KT)
    return out + [("E", user) for user in scored]


SAMPLES_END = 6
PLAN = plan()
RING = [k for c in range(NCHUNK) for k in SIDE[c]] + [k for t, k in PLAN if t == "R"]
RI = {k: i for i, k in enumerate(RING)}
NSIDE = sum(len(SIDE[c]) for c in range(NCHUNK))
SUSERS = [k for t, k in PLAN if t == "S"]
SF = {k: i for i, k in enumerate(SUSERS)}
PROJ = [k[1] for k in SUSERS if k[0] == "proj"]


def slot_of(user):
    if user[0] == "fox":
        return user[2] % 2
    return 0 if user[0] == "seq" else PROJ.index(user[1]) % 2


SN = {k: sum(slot_of(x) == slot_of(k) for x in SUSERS[:SF[k]]) for k in SUSERS}


def drains_on_act(key):
    if key[0] == "page_kT":
        return key[2] % 2 == 1
    return key[0] == "probsT"


UNITS = [k for k in SUSERS if k[0] == "fox"]
UI = {k: i for i, k in enumerate(UNITS)}


def build(nc, a, o):
    with ExitStack() as ctx:
        def sb(name, shape, dt=F32):
            return ctx.enter_context(nc.sbuf_tensor(name, shape, dt))

        def sem(name):
            return ctx.enter_context(nc.semaphore(name))

        YF = sb("YF", [P, 14 * NT])
        Y = YF[:, 0:8 * NT].rearrange("p (s t) -> p s t", t=NT)
        QK = YF[:, 8 * NT:14 * NT].rearrange("p (s t) -> p s t", t=NT)
        xrows = YF[:, 0:9 * D].rearrange("p (t n) -> p t n", n=D)
        VR = sb("VR", [P, 10, 384])
        ident = sb("ident", [P, P])
        identb = sb("identb", [P, P], BF16)
        causal = sb("causal", [P, CH])
        causal_s = sb("causal_s", [NS, NS])
        same_seq = sb("same_seq", [NS, NB])
        page_before = sb("page_before", [NS, NS])
        pick_row = sb("pick_row", [P, H, P], BF16)
        mask_neg = sb("mask_neg", [P, P], BF16)
        pick_q = sb("pick_q", [TS, 96], BF16)
        mask_new = sb("mask_new", [TS, TS], BF16)
        block_mean = sb("block_mean", [P, P])
        pool_w = sb("pool_w", [P, 2, P])
        negF = sb("negF", [P, LP], BF16)
        small = sb("small", [P, 44])
        gpre = small[:, 0:8]
        bgate = small[:, 8:10]
        gnorm = small[:, 10:11]
        pscale = small[:, 11:13]
        eps = small[:, 13:14]
        one = small[:, 14:15]
        ssq = small[:, 15:24]
        nmax = small[:, 24:30]
        rsum = small[:, 30:34]
        rinv = small[:, 34:38]
        zstat = small[:, 38:40]
        zvar = small[:, 24:25]
        head_of = small[:, 40:44]
        tail_sum, tail_max = small[:, 40:42], small[:, 42:44]
        bfox = sb("bfox", [H, 1])
        w_up = sb("w_up", [LR, H * DK])
        ebend = sb("ebend", [P, 2, 25])
        gstate = sb("gstate", [P, 3, 2, DV])
        logf_t = sb("logf_t", [P, 9, H])
        f_sum = sb("f_sum", [H, NS])
        f_last = sb("f_last", [H, NB])
        q_odd = sb("q_odd", [P, H * P])
        ptab = sb("ptab", [1, NB * NPAGE], I32)
        pidx = sb("pidx", [NB * NPAGE, 1], I32)
        PS = ctx.enter_context(nc.psum_tensor("PS", [P, 8, 512], F32))

        def stage(*tensors):
            with ExitStack() as s:
                return [s.enter_context(nc.sbuf_tensor(n, d, t)) for n, d, t in tensors]

        region_a = ("RA", [P, 6 * NT], F32)
        RA, wr, wh, wl, xh, xl = stage(
            region_a, ("wr", [P, 2, KT, P], F32), ("wh", [P, 2, KT, P], F32R), ("wl", [P, 2, KT, P], F32R),
            ("xh", [P, KT, NT], F32R), ("xl", [P, KT, NT], F32R))
        _, pagesB, kT, sbias, sprob, q_diag, sprobT0, prob, probT = stage(
            ("RA2", [P, 6 * NT], F32), ("pagesB", [P, 2, NPAGE, 384], F32), ("kT", [P, 2, 3, PAST], F32),
            ("sbias", [96, 2, PAST + TS], F32), ("sprob", [96, 2, PAST + TS], F32),
            ("q_diag", [P, 3, NB, 32], F32), ("sprobT0", [P, NPAGE + 1, H * TS], F32),
            ("prob", [P, 3, LP], F32), ("probT", [P, 2, 9, P], F32))
        wol_a, _, yh0, yl0, wo_raw, xres, zout, woh, wol_b, gpost = stage(
            ("wol_a", [P, 6, D], F32R), ("pad_a", [P, 6 * NT - 6 * D], F32),
            ("yh0", [P, KT, P], F32R), ("yl0", [P, KT, P], F32R), ("wo_raw", [P, 2, D], F32),
            ("xres", [P, D], F32), ("zout", [P, D], F32),
            ("woh", [P, KT, D], F32R), ("wol_b", [P, 2, D], F32R), ("gpost", [P, D], F32))
        _, _, _, yh1, yl1 = stage(
            ("pad_b", [P, 6 * NT], F32), ("pad_c", [P, KT, P], F32), ("pad_d", [P, KT, P], F32),
            ("yh1", [P, KT, P], F32R), ("yl1", [P, KT, P], F32R))
        yh, yl = [yh0, yh1], [yl0, yl1]
        wol = [wol_a[:, k, :] for k in range(6)] + [wol_b[:, k, :] for k in range(2)]
        E = RA[:, :].rearrange("p (s t) -> p s t", t=NT)

        pages = [pagesB[:, :, :, :], RA[:, 0:2 * NPAGE * 384].rearrange("p (w g n) -> p w g n", w=2, n=384)]
        glr = Y[0:LR, 5, :]
        reset = Y[:, 7, :]
        ones_row = QK[0:NS, 5, 0:LP]
        logf, ftmp, fcum = QK[0:H, 0, :], QK[0:H, 1, :], QK[0:H, 2, :]
        page_lf = QK[0:NS, 3, 0:PAGE * H].rearrange("p (k h) -> p k h", h=H)
        page_F = QK[0:NS, 4, 0:PAGE * H].rearrange("p (h k) -> p h k", h=H)
        pv, psA, psB = Y[:, 5, :], Y[:, 6, :], Y[:, 7, :]
        hist_rows = Y[0:NB * HIST, 4, 0:256]
        HX = HIST + TS
        hx = [Y[:, 0, 192 * i:192 * i + NB * HX].rearrange("p (b t) -> p b t", b=NB) for i in range(2)]
        hA, hB = (Y[:, 0, 384 + 192 * i:384 + 192 * i + NB * HX].rearrange("p (b t) -> p b t", b=NB) for i in range(2))
        last_p, last_s = Y[0:HIST, 1, 0:256], Y[0:NS, 1, 256:512]
        kd_rows = Y[:, 5:7, :].rearrange("p s t -> p (s t)")[:, 0:9 * 192].rearrange("p (b n) -> p b n", n=192)
        kd_meta = QK[0:NMETA, 4, H * P:H * P + 192]
        kd_seq = Y[:, 5:7, :].rearrange("p s t -> p (s t)")[0:NS, 0:NB * 192].rearrange("p (b n) -> p b n", n=192)
        aT = YF[:, 5 * NT + 9 * 192:5 * NT + 9 * 192 + 2 * H * P].rearrange("p (a h t) -> p a h t", a=2, h=H)
        q_heads = [x.rearrange("p (h t) -> p h t", h=H) for x in (QK[:, 4, 0:H * P], q_odd[:, :])]
        gstate_s = QK[:, 5, 0:2 * NB * DV].rearrange("p (g b v) -> p g b v", g=2, b=NB)
        k_out = RA[:, 0:9 * 384].rearrange("p (t n) -> p t n", n=384)
        gtmp = [E[:, 4, :], E[:, 5, :]]
        gate_parts = [(E[:, 0, :], E[:, 2, :]), (E[0:64, 1, :], E[0:64, 3, :]), (logf, ftmp)]
        xg = RA[:, 0:3 * D].rearrange("p (a k t) -> p a k t", a=3, k=KT)
        squares = RA[:, 3 * D:4 * D]
        rstd, refine = RA[:, 4 * D:4 * D + 9], RA[:, 4 * D + 9:4 * D + 18]
        at = 2 * NPAGE * 384
        sprobT = [sprobT0[:, :, :], RA[:, at:at + 9 * H * TS].rearrange("p (g q) -> p g q", q=H * TS)]
        v_new = q_odd[0:TS, :].rearrange("p (a n) -> p a n", a=2)
        s_rows = VR[0:96, 9, 0:P]
        nf_d = nc.dram_tensor("minus_F", [NB, H, PAST + TS], F32, kind="Internal").ap()

        d_x = [sem(f"d_x{t}") for t in range(9)]
        d_gpre, d_const, d_poolw = sem("d_gpre"), sem("d_const"), sem("d_poolw")
        d_w = [sem("d_w0"), sem("d_w1")]
        d_hist, d_idx, d_lf, d_ptab = sem("d_hist"), sem("d_idx"), sem("d_lf"), sem("d_ptab")
        d_nf, d_fl, d_s0 = sem("d_nf"), sem("d_fl"), sem("d_s0")
        d_out = sem("d_out")
        d_pool_out, d_state_out, d_k_out = sem("d_pool_out"), sem("d_state_out"), sem("d_k_out")
        d_k, d_v = [sem("d_k0"), sem("d_k1")], [sem("d_v0"), sem("d_v1")]
        d_bias = [sem("d_bias0"), sem("d_bias1")]
        d_wo = [sem("d_wo0"), sem("d_wo1")]
        d_post, d_xres, d_y = sem("d_post"), sem("d_xres"), sem("d_y")
        consts_set, pool_step = sem("consts_set"), sem("pool_step")
        wz = sem("wz")
        sq_done, rms_done, xs_done = sem("sq_done"), sem("rms_done"), sem("xs_done")
        xt_full, xg_done, xhi_done, xlo_done = sem("xt_full"), sem("xg_done"), sem("xhi_done"), sem("xlo_done")
        xlo_dve = sem("xlo_dve")
        whi_done, wlo_done = sem("whi_done"), sem("wlo_done")
        in_full = sem("in_full")
        in_free = [sem("in_free0"), sem("in_free1")]
        ring_full = sem("ring_full")
        ring_free = [sem("ring_free0"), sem("ring_free1")]
        ring3_free = [sem(f"ring3_free{i}") for i in range(3)]
        s_full, tail_done = sem("s_full"), sem("tail_done")
        s_free = [sem("s_free0"), sem("s_free1")]
        act_step, dve_step = sem("act_step"), sem("dve_step")
        abs_done, ln_done, b_done, e_done, kd_sub, kd_exp = (
            sem("abs_done"), sem("ln_done"), sem("b_done"), sem("e_done"), sem("kd_sub"), sem("kd_exp"))
        zf_done, negF_done = sem("zf_done"), sem("negF_done")
        page_scanned, fnew_done = sem("page_scanned"), sem("fnew_done")
        kb_moved = sem("kb_moved")
        qheads_done = sem("qheads_done")
        pool_done, kdseq_done, s0_scaled = sem("pool_done"), sem("kdseq_done"), sem("s0_scaled")
        osq_done, orstd_done, o_normed = sem("osq_done"), sem("orstd_done"), sem("o_normed")
        gexp_done, gated = sem("gexp_done"), sem("gated")
        sbias_zero, fprob_done, srows_zero = sem("sbias_zero"), sem("fprob_done"), sem("srows_zero")
        qdiag_zero, qdiag_done = sem("qdiag_zero"), sem("qdiag_done")
        smax_done, sexp_done, sprob_done = sem("smax_done"), sem("sexp_done"), sem("sprob_done")
        fmax_done = sem("fmax_done")
        wohi_done, wolo_done = sem("wohi_done"), sem("wolo_done")
        yhi_done, ylo_done = sem("yhi_done"), sem("ylo_done")
        zstat_done, y_done = sem("zstat_done"), sem("y_done")

        def place(key):
            i = RI[key]
            if i < NSIDE:
                return 6 + i % 2, ring_free[i % 2], i // 2
            i -= NSIDE
            return 5 + i % 3, ring3_free[i % 3], i // 3

        def bank(key):
            return PS[:, place(key)[0], :]

        def ring_take(pe, key):
            n, free, before = place(key)
            if before:
                pe.wait_ge(free, before)
            elif RI[key] >= NSIDE and n >= 6:
                pe.wait_ge(ring_free[n - 6], (NSIDE + 7 - n) // 2)
            return bank(key)

        def ring_ready(eng, key):
            eng.wait_ge(ring_full, RI[key] + 1)
            return bank(key)

        def freed(key):
            return place(key)[1]

        def drained(eng, key):
            _, free, before = place(key)
            eng.wait_ge(free, before + 1)

        def chunk_width(c):
            return max(at + n for _, at, n in CHUNKS[c])

        def chunk_psum(c):
            return PS[:, 3 * (c % 2):3 * (c % 2) + 3, 0:TH]

        def thirds(ap):
            return ap.rearrange("p (a t) -> p a t", t=TH)

        def chunk_stored(eng, c):
            eng.wait_ge(in_free[c % 2], c // 2 + 1)

        def s_slot(user):
            n = slot_of(user)
            return PS[:, 3 * n:3 * n + 3, :].rearrange("p b t -> p (b t)")

        def s_tail(user):
            n = user[1] * P + P + NMETA - 1024
            return PS[:, 2, 0:n] if slot_of(user) == 0 else PS[:, 2, 16:16 + n]

        def s_taken(pe, user):
            if SN[user]:
                pe.wait_ge(s_free[slot_of(user)], SN[user])

        def s_emptied(eng, user):
            eng.wait_ge(s_free[slot_of(user)], SN[user] + 1)

        def s_ready(eng, user):
            eng.wait_ge(s_full, SF[user] + 1)

        def head_rows(h):
            return slice(DK * (h % 4), DK * (h % 4) + DK)

        def group_rows(h):
            return slice(0, P) if h < 4 else slice(0, 64)

        def xcols(t):
            return [(0, P, NMETA + P * t)] if t < NTILE else [(0, NS, LP), (NS, NS + NMETA, 0)]

        def n_of(t):
            return P if t < NTILE else NS + NMETA

        def ycol(t):
            return NMETA + P * t if t < NTILE else LP

        def probsT_drain(eng, key, copy):
            _, j, h, i = key
            u = UI[("fox", j, h)]
            src = ring_ready(eng, key)
            lo, hi = parts(j)[i][0], parts(j)[i][-1] + 1
            full = min(hi, j + 1) - lo
            if full:
                ins = copy(probT[:, u % 2, lo:lo + full, :], src[:, 0:P * full].rearrange("p (b q) -> p b q", q=P))
            if hi == j + 2:
                ins = copy(probT[0:NMETA, u % 2, j + 1, :], src[0:NMETA, P * full:P * full + P])
            ins.then_inc(freed(key), 1)

        def x_low(eng, i):
            eng.wait_ge(xhi_done, i + 1)
            for r0, r1, col in xcols(XORDER[i]):
                ins = eng.tensor_tensor(xl[:, :, col:col + r1 - r0], xg[:, i % 3, :, r0:r1],
                                        xh[:, :, col:col + r1 - r0].bitcast(F32), ALU.subtract)
            return ins

        XORDER = [NTILE] + list(range(NTILE))
        DVE_LOW = (4, 6, 8)

        def x_low_done(eng, i):
            on_dve = sum(x <= i for x in DVE_LOW)
            eng.wait_ge(xlo_done, i + 1 - on_dve)
            if on_dve:
                eng.wait_ge(xlo_dve, on_dve)

        block = ctx.enter_context(nc.Block())
        w_src = a["w_in"][0].rearrange("(k p) n -> p k n", p=P)
        W_COUNT = []
        for c in range(NCHUNK):
            W_COUNT.append((W_COUNT[c - 2] if c >= 2 else 0) + 16 * len(CHUNKS[c]))

        @block.sync
        def _(sp):
            def load_x(t):
                if t < NTILE:
                    sp.dma_start(xrows[:, t, :], a["x_prompt"][0, P * t:P * t + P, :]).then_inc(d_x[t], 16)
                else:
                    sp.dma_start(xrows[0:NS, t, :], a["x_sample"].rearrange("b t n -> (b t) n")).then_inc(d_x[t], 16)
                    sp.dma_start(xrows[NS:NS + NMETA, t, :], a["meta_tokens"]).then_inc(d_x[t], 16)

            def load_w(c):
                if c == 0:
                    sp.wait_ge(wz, 1)
                if c >= 2:
                    sp.wait_ge(whi_done, c - 1)
                    sp.wait_ge(wlo_done, c - 1)
                for col, at_, n in CHUNKS[c]:
                    sp.dma_start(wr[:, c % 2, :, at_:at_ + n], w_src[:, :, col:col + n]).then_inc(d_w[c % 2], 16)

            for i, t in enumerate(XORDER):
                load_x(t)
                if i == 1:
                    with nc.allow_non_contiguous_dma(reason="one value per partition"):
                        sp.dma_start(gpre[:, :], a["norm_pre"][0].rearrange("(k p) -> p k", p=P)).then_inc(d_gpre, 16)
                if i == 3:
                    load_w(0)
            for dst, src in ((bgate[:, 0:1], a["gla_b_gate"][0, 0:P].rearrange("(p a) -> p a", a=1)),
                             (bgate[0:64, 1:2], a["gla_b_gate"][0, P:].rearrange("(p a) -> p a", a=1)),
                             (gnorm[0:DV, :], a["gla_norm"][0].rearrange("(p a) -> p a", a=1)),
                             (gnorm[DV:P, :], a["gla_norm"][0].rearrange("(p a) -> p a", a=1)),
                             (pscale[:, :], a["pool_scale"][0].rearrange("(i p) -> p i", p=P)),
                             (bfox[:, :], a["fox_b_f"][0].rearrange("(p a) -> p a", a=1)),
                             (w_up[:, :], a["gla_w_up"][0])):
                with nc.allow_non_contiguous_dma(reason="small vectors, one value per partition"):
                    sp.dma_start(dst, src).then_inc(d_const, 16)
            load_w(1)

            def outputs(c):
                if c == 1:
                    sp.wait_ge(xs_done, 9)
                    sp.wait_ge(xt_full, 9)
                    sp.dma_start(hist_rows, a["state_pool"][0].rearrange("b t c -> (b t) c")).then_inc(d_hist, 16)
                if c == 3:
                    drained(sp, ("logf_rows",))
                    sp.dma_start(o["logf_p"][0, 0, 0:P * NTILE, :].rearrange("(t p) h -> p t h", p=P),
                                 logf_t[:, 0:NTILE, :]).then_inc(d_out, 16)
                    sp.dma_start(o["logf_p"][0, 0, P * NTILE:LP, :], logf_t[0:NMETA, NTILE, :]).then_inc(d_out, 16)
                    sp.dma_start(o["logf_s"][0].rearrange("b t h -> (b t) h"),
                                 logf_t[NMETA:NMETA + NS, NTILE, :]).then_inc(d_out, 16)
                    drained(sp, ("page_prefix",))
                    for b in range(NB):
                        sp.dma_start(nf_d[b, :, 0:PAST].rearrange("h (g k) -> g h k", k=PAGE),
                                     page_F[NPAGE * b:NPAGE * b + NPAGE]).then_inc(d_nf, 16)
                    sp.wait_ge(d_nf, 16 * NB)
                    with nc.allow_non_contiguous_dma(reason="one value per head and sequence"):
                        sp.dma_start(f_last[:, :], nf_d[:, :, PAST - 1].rearrange("b h -> h b")).then_inc(d_fl, 16)
                if c == 6:
                    sp.wait_ge(fnew_done, 1)
                    sp.dma_start(nf_d[:, :, PAST:PAST + TS].rearrange("b h t -> h b t"),
                                 f_sum[:, :].rearrange("h (b t) -> h b t", t=TS)).then_inc(d_nf, 16)
                    drained(sp, ("pool_last", 0))
                    drained(sp, ("pool_last", 1))
                    sp.dma_start(o["pool_p"][0, 0], last_p).then_inc(d_pool_out, 16)
                    for b in range(NB):
                        sp.dma_start(o["pool_s"][0, b, HIST - TS:HIST, :],
                                     last_s[TS * b:TS * b + TS]).then_inc(d_pool_out, 16)
                    sp.dma_start(o["pool_s"][0, :, 0:HIST - TS, :],
                                 a["state_pool"][0, :, TS:HIST, :]).then_inc(d_out, 16)
                    sp.wait_ge(fnew_done, 1)
                    for g, n in ((0, 4), (1, 2)):
                        sp.dma_start(gstate_s[0:DK * n, g],
                                     a["state_gla"][0, :, 4 * g:4 * g + n].rearrange("b h k v -> (h k) b v")
                                     ).then_inc(d_s0, 16)
                if c == 12:
                    drained(sp, ("state", NCH))
                    for g, n in ((0, 4), (1, 2)):
                        sp.dma_start(o["gla_p"][0, 0, 4 * g:4 * g + n].rearrange("h k v -> (h k) v"),
                                     gstate[0:DK * n, NCH % 3, g, :]).then_inc(d_out, 16)
                if c == 12:
                    drained(sp, ("sample_state", 1, 1))
                    drained(sp, ("sample_state", 1, 0))
                    for g, n in ((0, 4), (1, 2)):
                        sp.dma_start(o["gla_s"][0, :, 4 * g:4 * g + n].rearrange("b h k v -> (h k) b v"),
                                     gstate_s[0:DK * n, g]).then_inc(d_state_out, 16)
                if c == 14:
                    for t in range(9):
                        drained(sp, ("k_rows", t))
                        store_rows("k", k_out, t, d_k_out)
                if c == 25:
                    for t in range(9):
                        drained(sp, ("fv_rows", t))
                        store_rows("v", VR, t, d_out)

            def store_rows(which, src, t, done):
                dp, ds = (o["fox_" + which + x].rearrange("z b t h d -> (z b t) (h d)") for x in "ps")
                if t < NTILE:
                    sp.dma_start(dp[P * t:P * t + P], src[:, t, :]).then_inc(done, 16)
                else:
                    sp.dma_start(dp[P * t:LP], src[0:NMETA, t, :]).then_inc(done, 16)
                    sp.dma_start(ds, src[NMETA:NMETA + NS, t, :]).then_inc(done, 16)

            for c in range(2, NCHUNK):
                load_w(c)
                if c >= 4:
                    outputs(c - 3)
            for c in range(NCHUNK - 3, NCHUNK - 1):
                outputs(c)

            k_cache = a["cache_fox_k"][0].rearrange("g p h d -> g p (h d)")
            sp.wait_ge(d_ptab, 16)
            for b in range(NB):
                u = b % 2
                if b == 0:
                    sp.wait_ge(in_full, NCHUNK)
                elif b == 1:
                    outputs(NCHUNK - 1)
                    drained(sp, ("fv_rows", 7))
                else:
                    sp.wait_ge(ring_full, RI[("page_kT", b - 2, NPAGE - 1)] + 1)
                for g in range(NPAGE):
                    i = NPAGE * b + g
                    page = sp.value_load(ptab[0:1, i:i + 1], min_val=0, max_val=a["cache_fox_k"].shape[1] - 1)
                    sp.dma_start(pages[u][:, 0, g, :],
                                 k_cache[bass.ds(page, 1)].rearrange("a p n -> (a p) n")).then_inc(d_k[u], 16)
                if b == 0:
                    sp.wait_ge(d_nf, 16 * (NB + 1))
                    sp.wait_ge(sbias_zero, 1)
                if b >= 2:
                    sp.wait_ge(smax_done, b - 1)
                for h in range(H):
                    r = 32 * (h // 2) + TS * (h % 2)
                    sp.dma_start(sbias[r:r + TS, u, :],
                                 nf_d[b, h:h + 1, :].to_broadcast([TS, PAST + TS])).then_inc(d_bias[u], 16)

            wo_src = a["w_out"][0].rearrange("(k p) n -> k p n", p=P)
            drained(sp, ("s_outT", NB - 1))
            sp.dma_start(gpost[:, :], a["norm_post"][0:1, :].to_broadcast([P, D])).then_inc(d_post, 16)
            for k in range(KT):
                if k >= 2:
                    sp.wait_ge(wohi_done, k - 1)
                    sp.wait_ge(wolo_done, k - 1)
                sp.dma_start(wo_raw[:, k % 2, :], wo_src[k]).then_inc(d_wo[k % 2], 16)
            for n, t in enumerate(PROJ):
                m = P if t < NTILE else NS
                rows = slice(P * t, P * t + P)
                x, y = ((a["x_prompt"][0, rows], o["y_p"][0, rows]) if t < NTILE else
                        (a["x_sample"].rearrange("b t n -> (b t) n"), o["y_s"].rearrange("b t n -> (b t) n")))
                if n:
                    sp.wait_ge(y_done, 2 * n)
                sp.dma_start(xres[0:m, :], x).then_inc(d_xres, 16)
                for half in range(2):
                    cols = slice(D // 2 * half, D // 2 * half + D // 2)
                    sp.wait_ge(y_done, 2 * n + half + 1)
                    sp.dma_start(y[:, cols], zout[0:m, cols]).then_inc(d_y, 16)
            sp.wait_ge(d_y, 32 * len(PROJ))
            sp.wait_ge(d_k_out, 16 * 10)
            sp.wait_ge(d_state_out, 32)
            sp.wait_ge(d_pool_out, 16 * (NB + 1))
            sp.wait_ge(d_out, 16 * (3 + 1 + 2 + 10))

        @block.gpsimd
        def _(pool):
            g = pool
            n = [0]

            def link(ins):
                n[0] += 1
                ins.then_inc(pool_step, 1)
                g.wait_ge(pool_step, n[0])

            link(g.memset(wr[:, 0, :, LR:32], 0.0))
            g.memset(eps[:, :], EPS).then_inc(wz, 1)

            def keep(ap, pattern, base, mult, fill=0.0, op=ALU.is_ge, last=False):
                ins = g.affine_select(out=ap, in_=ap, compare_op=op, fill=fill, base=base, pattern=pattern,
                                      channel_multiplier=mult)
                if last:
                    ins.then_inc(consts_set, 1)
                else:
                    link(ins)

            g.dma_start(pidx[:, :], a["page_table"].rearrange("b (g a) -> (b g) a", a=1)).then_inc(d_idx, 16)
            g.dma_start(ptab[:, :], a["page_table"].rearrange("(a b) g -> a (b g)", a=1)).then_inc(d_ptab, 16)
            link(g.memset(one[:, :], 1.0))
            for m in (ident, identb):
                link(g.memset(m[:, :], 0.0))
                keep(m[:, :], [[-1, P]], 0, 1, 1.0, ALU.not_equal, last=m is identb)

            def w_low(c):
                g.wait_ge(d_w[c % 2], W_COUNT[c])
                g.wait_ge(whi_done, c + 1)
                if c >= 2:
                    g.wait_ge(in_full, c - 1)
                m = chunk_width(c)
                g.tensor_tensor(wl[:, c % 2, :, 0:m], wr[:, c % 2, :, 0:m], wh[:, c % 2, :, 0:m].bitcast(F32),
                                ALU.subtract).then_inc(wlo_done, 1)

            for i in range(9):
                if i not in DVE_LOW:
                    x_low(g, i).then_inc(xlo_done, 1)
                if i == 2:
                    w_low(0)
            g.wait_ge(xt_full, 9)
            link(g.memset(reset, 1.0))
            link(g.memset(reset[:, 0:1], 0.0))
            link(g.memset(reset[:, NMETA:LP].rearrange("p (c t) -> p c t", t=CH)[:, :, 0:1], 0.0))
            link(g.memset(reset[:, LP:NT].rearrange("p (c t) -> p c t", t=TS)[:, :, 0:1], 0.0))
            g.memset(ones_row, 1.0).then_inc(consts_set, 1)
            w_low(1)
            g.wait_ge(d_idx, 16)
            g.indirect_dma_start(QK[0:NS, 3, 0:PAGE * H], None,
                                 a["cache_fox_logf"][0].rearrange("g p h -> g (p h)"),
                                 bass.IndirectOffsetOnAxis(ap=pidx[:, 0:1], axis=0)).then_inc(d_lf, 16)
            link(g.memset(pool_w[:, :, :], 0.0))
            for i in range(4):
                r = slice(64 * (i % 2), 64 * (i % 2) + 64)
                g.dma_start(pool_w[r, i // 2, r], a["pool_w"][0, i]).then_inc(d_poolw, 16)
            link(g.memset(negF[:, :], 0.0))
            link(g.memset(page_before[:, :], 1.0))
            pb = page_before[:, :].rearrange("p (b g) -> p b g", g=NPAGE)
            keep(pb, [[-NPAGE, NB], [0, NPAGE]], 0, 1)
            keep(pb, [[NPAGE, NB], [1, NPAGE]], -1, -1)
            link(g.memset(head_of[:, :], 1.0))
            keep(head_of[:, :], [[-DK, 4]], 0, 1)
            keep(head_of[:, :], [[DK, 4]], DK - 1, -1)
            link(g.memset(causal[:, :], 1.0))
            keep(causal[:, :], [[1, CH]], CH, -1)
            keep(causal[0:CH, :], [[1, CH]], 0, -1, last=True)
            w_low(2)
            link(g.memset(causal_s[:, :], 1.0))
            cs = causal_s[:, :].rearrange("p (b t) -> p b t", t=TS)
            keep(cs, [[TS, NB], [1, TS]], 0, -1)
            keep(cs, [[-TS, NB], [0, TS]], 0, 1)
            link(g.memset(same_seq[:, :], 1.0))
            keep(same_seq[:, :], [[-TS, NB]], 0, 1)
            keep(same_seq[:, :], [[TS, NB]], TS - 1, -1)
            link(g.memset(block_mean[:, :], 0.0))
            for r in (slice(0, 64), slice(64, P)):
                link(g.memset(block_mean[r, r], 1.0 / DV))
            link(g.memset(pick_row[:, :, :], 0.0))
            for q in range(3):
                keep(pick_row[:, :, :], [[-1, H], [0, P]], -32 * q, 1, 1.0, ALU.not_equal)
            link(g.memset(mask_neg[:, :], 0.0))
            keep(mask_neg[:, :], [[-1, P]], 0, 1, NEG)
            link(g.memset(mask_new[:, :], 0.0))
            keep(mask_new[:, :], [[-1, TS]], 0, 1, NEG)
            link(g.memset(pick_q[:, :], 0.0))
            pq = pick_q[:, :].rearrange("p (h i q) -> p h i q", i=4, q=TS)[:, :, 0:2, :]
            keep(pq, [[0, 3], [0, 2], [1, TS]], 0, -1, 1.0, ALU.not_equal, last=True)
            for c in range(3, NCHUNK):
                w_low(c)
            g.wait_ge(in_full, NCHUNK)
            g.memset(q_diag[:, :, :, :], 0.0).then_inc(qdiag_zero, 1)
            g.memset(sbias[:, :, :], 0.0).then_inc(sbias_zero, 1)

            v_cache = a["cache_fox_v"][0].rearrange("g p h d -> g p (h d)")
            g.wait_ge(d_ptab, 16)
            for b in range(NB):
                u = b % 2
                if b == 1:
                    g.wait_ge(gated, len(GATES))
                    drained(g, ("fv_rows", 8))
                    drained(g, ("fv_rows", 7))
                elif b >= 2:
                    drained(g, ("s_attend", b - 2))
                for i in range(NPAGE * b, NPAGE * b + NPAGE):
                    page = g.value_load(ptab[0:1, i:i + 1], min_val=0, max_val=a["cache_fox_v"].shape[1] - 1)
                    g.dma_start(pages[u][:, 1, i % NPAGE, :],
                                v_cache[bass.ds(page, 1)].rearrange("a p n -> (a p) n")).then_inc(d_v[u], 16)
                if b == 0:
                    drained(g, ("fv_rows", 8))
                g.dma_start(v_new[:, u, :], VR[NMETA + TS * b:NMETA + TS * b + TS, NTILE, :]).then_inc(d_v[u], 16)
            for k in range(KT):
                g.wait_ge(wohi_done, k + 1)
                g.tensor_tensor(wol[k], wo_raw[:, k % 2, :], woh[:, k, :].bitcast(F32), ALU.subtract
                                ).then_inc(wolo_done, 1)
            for n_, t in enumerate(PROJ):
                g.wait_ge(yhi_done, n_ + 1)
                m = P if t < NTILE else NS
                g.tensor_tensor(yl[n_ % 2][:, :, 0:m], Y[:, :, ycol(t):ycol(t) + m], yh[n_ % 2][:, :, 0:m].bitcast(F32),
                                ALU.subtract).then_inc(ylo_done, 1)

        @block.scalar
        def _(act):
            n = [0]

            def link(ins):
                n[0] += 1
                ins.then_inc(act_step, 1)
                act.wait_ge(act_step, n[0])

            def x_squares(t):
                act.wait_ge(d_x[t], 16 if t < NTILE else 32)
                m = n_of(t)
                act.activation(squares[0:m, :], xrows[0:m, t, :], ACT.Square,
                               accum_out=ssq[0:m, t:t + 1]).then_inc(sq_done, 1)
                act.wait_ge(sq_done, XORDER.index(t) + 1)
                act.activation(refine[0:m, t:t + 1], ssq[0:m, t:t + 1], ACT.Identity, bias=eps[0:m, :], scale=1.0 / D)
                act.activation(rstd[0:m, t:t + 1], ssq[0:m, t:t + 1], ACT.Sqrt, bias=eps[0:m, :], scale=1.0 / D
                               ).then_inc(rms_done, 1)

            def x_high(i):
                t = XORDER[i]
                act.wait_ge(xg_done, i + 1)
                for r0, r1, col in xcols(t):
                    ins = act.activation(xh[:, :, col:col + r1 - r0], xg[:, i % 3, :, r0:r1], ACT.Copy)
                ins.then_inc(xhi_done, 1)

            def w_high(c):
                if c >= NCHUNK:
                    return
                act.wait_ge(d_w[c % 2], W_COUNT[c])
                if c >= 2:
                    act.wait_ge(in_full, c - 1)
                m = chunk_width(c)
                act.activation(wh[:, c % 2, :, 0:m], wr[:, c % 2, :, 0:m], ACT.Copy).then_inc(whi_done, 1)

            act.wait_ge(wz, 1)
            for i, t in enumerate(XORDER):
                x_squares(t)
                if i >= 2:
                    x_high(i - 2)
                if i == 4:
                    w_high(0)
            x_high(7)
            x_high(8)
            w_high(1)

            def drain(key):
                kind = key[0]
                if kind == "gate":
                    _, g, t = key
                    if (g, t) == (0, 0):
                        act.wait_ge(d_const, 16 * 7)
                    r = P if g == 0 else 64
                    src = ring_ready(act, key)
                    act.activation(E[0:r, g, TH * t:TH * t + TH], src[0:r, 0:TH], ACT.Identity,
                                   bias=bgate[0:r, g:g + 1]).then_inc(freed(key), 1)
                elif kind == "logf_rows":
                    src = ring_ready(act, key)
                    act.activation(logf_t[:, 0:NTILE, :], src[:, 0:NTILE * H].rearrange("p (t h) -> p t h", h=H), ACT.Copy)
                    act.activation(logf_t[0:NMETA + NS, NTILE, :], src[0:NMETA + NS, NTILE * H:9 * H],
                                   ACT.Copy).then_inc(freed(key), 1)
                elif kind == "v_rows":
                    b = key[1]
                    m = GBLOCKS[b][1]
                    src = ring_ready(act, key)
                    act.activation(VR[0:m, b, :], src[0:m, 0:384], ACT.Copy).then_inc(freed(key), 1)
                elif kind == "pool_last":
                    i = key[1]
                    src = ring_ready(act, key)
                    act.activation(last_p[:, P * i:P * i + P], src[0:HIST, 0:P], ACT.Copy)
                    act.activation(last_s[:, P * i:P * i + P], src[0:NS, P:2 * P], ACT.Copy).then_inc(freed(key), 1)
                elif kind == "pool":
                    _, i, q = key
                    col, m = PIECES[q]
                    src = ring_ready(act, key)
                    if (i, q) == (1, 0):
                        drained(act, ("hist",))
                    act.activation(Y[:, 3 + i, col:col + m], src[:, 0:m], ACT.Copy,
                                   scale=pscale[:, i:i + 1]).then_inc(freed(key), 1)
                elif kind == "kd_rows":
                    i = key[1]
                    src = ring_ready(act, key)
                    if i < 4:
                        act.activation(kd_rows[:, 2 * i:2 * i + 2, :],
                                       src[:, 0:384].rearrange("p (b n) -> p b n", b=2), ACT.Copy
                                       ).then_inc(freed(key), 1)
                    else:
                        act.activation(kd_rows[0:NS, 8, :], src[0:NS, 0:192], ACT.Copy)
                        act.activation(kd_meta, src[0:NMETA, 192:384], ACT.Copy).then_inc(freed(key), 1)
                elif kind == "out":
                    j = key[1]
                    src = ring_ready(act, key)
                    if j == 0:
                        act.wait_ge(d_pool_out, 16 * (NB + 1))
                    act.activation(Y[:, 0:3, NMETA + P * j:NMETA + P * j + P],
                                   src[:, 0:384].rearrange("p (g t) -> p g t", g=3), ACT.Copy).then_inc(freed(key), 1)
                elif kind == "sample_out":
                    src = ring_ready(act, key)
                    act.activation(Y[:, key[1], LP:NT], src[:, 0:NS], ACT.Copy).then_inc(freed(key), 1)
                elif kind == "meansq":
                    _, i, q = key
                    col, m = PIECES[q]
                    src = ring_ready(act, key)
                    act.activation(E[:, 3 + i, col:col + m], src[:, 0:m], ACT.Ln, bias=eps[:, :]).then_inc(freed(key), 1)
                elif kind == "k_rows" or (kind == "fv_rows" and key[1] % 2 == 0):
                    t = key[1]
                    dst = k_out if kind == "k_rows" else VR
                    m = P if t < NTILE else NMETA + NS
                    src = ring_ready(act, key)
                    if key == ("k_rows", 0):
                        act.wait_ge(o_normed, 3)
                    act.activation(dst[0:m, t, :], src[0:m, 0:384], ACT.Copy).then_inc(freed(key), 1)

            def store(c):
                src = chunk_psum(c)
                done = in_free[c % 2]
                if c == C_LF:
                    act.wait_ge(in_full, c + 1)
                    act.activation(thirds(glr), src[0:LR], ACT.Copy)
                    act.activation(thirds(logf), src[32:32 + H], ACT.Copy).then_inc(done, 1)
                elif C_PV <= c < C_PV + 2:
                    act.wait_ge(in_full, c + 1)
                    if c == C_PV:
                        act.wait_ge(b_done, 1)
                    else:
                        act.wait_ge(pool_done, 1)
                    act.activation(thirds(pv), src, ACT.Copy).then_inc(done, 1)
                elif c == C_QKB:
                    act.wait_ge(in_full, c + 1)
                    act.activation(thirds(QK[0:64, 4, :]), src[64:P], ACT.Copy).then_inc(kb_moved, 1)
                elif C_FK <= c < C_FK + 3:
                    act.wait_ge(in_full, c + 1)
                    act.activation(thirds(QK[:, c - C_FK, :]), src, ACT.Copy).then_inc(done, 1)
                elif C_FQ <= c < C_FQ + 3:
                    act.wait_ge(in_full, c + 1)
                    if c == C_FQ + 2:
                        act.wait_ge(d_state_out, 32)
                    act.activation(thirds(QK[:, 3 + c - C_FQ, :]), src, ACT.Copy, scale=HD ** -0.5).then_inc(done, 1)
                elif c in GATES:
                    act.wait_ge(in_full, c + 1)
                    act.wait_ge(o_normed, 3)
                    if c >= C_GG + 2:
                        act.wait_ge(gated, GATES.index(c) - 1)
                    act.activation(thirds(gtmp[GATES.index(c) % 2]), src, ACT.Exp, scale=-1.0).then_inc(gexp_done, 1)
                elif C_FV <= c < C_FV + 3:
                    act.wait_ge(in_full, c + 1)
                    if c == C_FV:
                        act.wait_ge(d_k_out, 16 * 10)
                    act.activation(thirds(E[:, c - C_FV, :]), src, ACT.Copy).then_inc(done, 1)

            def extra(c):
                if c == 0:
                    act.wait_ge(zf_done, 1)
                    for t in range(3):
                        drained(act, ("gate", 1, t))
                        drained(act, ("gate", 0, t))
                    for z, t in gate_parts:
                        act.activation(t, z, ACT.Abs).then_inc(abs_done, 1)
                    act.wait_ge(abs_done, 3)
                    for z, t in gate_parts:
                        link(act.activation(t, t, ACT.Exp, scale=-1.0))
                if c == 1:
                    for (z, t), r in zip(gate_parts, (P, 64, H)):
                        act.activation(t, t, ACT.Ln, bias=one[0:r, :]).then_inc(ln_done, 1)
                if c == 2:
                    act.wait_ge(b_done, 1)
                    for g, r in ((0, P), (1, 64)):
                        act.activation(E[0:r, g, :], E[0:r, 4 + g, :], ACT.Exp, scale=GATE)
                        act.activation(E[0:r, 2 + g, :], E[0:r, 4 + g, :], ACT.Exp, scale=-GATE).then_inc(e_done, 1)
                if c == 3:
                    act.wait_ge(kd_sub, 1)
                    for g, r in ((0, P), (1, 64)):
                        act.activation(E[0:r, 4 + g, :], E[0:r, 4 + g, :], ACT.Exp, scale=GATE)
                        act.activation(ebend[0:r, g, :], ebend[0:r, g, :], ACT.Exp, scale=GATE).then_inc(kd_exp, 1)
                if c == 12:
                    for i in range(3):
                        drained(act, ("sample_out", i))
                    drained(act, ("out", 7))
                    for i in range(3):
                        act.activation(E[:, i, NMETA:NT], Y[:, i, NMETA:NT], ACT.Square).then_inc(osq_done, 1)
                if c == 13:
                    for q in range(3):
                        drained(act, ("meansq", 2, q))
                    for i in range(3):
                        act.activation(E[:, 3 + i, NMETA:NT], E[:, 3 + i, NMETA:NT], ACT.Exp,
                                       scale=-0.5).then_inc(orstd_done, 1)

            for c in range(1, NCHUNK + 1):
                store(c - 1)
                w_high(c + 1)
                for key in SIDE[c - 1]:
                    drain(key)
                extra(c - 1)

            def softmax_exp(user):
                if user[0] == "seq":
                    b = user[1]
                    act.wait_ge(smax_done, b + 1)
                    act.activation(sprob[:, b % 2, :], sprob[:, b % 2, :], ACT.Exp, bias=nmax[0:96, b % 2:b % 2 + 1],
                                   accum_out=rsum[0:96, b % 2:b % 2 + 1]).then_inc(sexp_done, 1)
                elif user[0] == "fox":
                    _, j, h = user
                    m = NMETA + P * (j + 1)
                    u = UI[user]
                    act.wait_ge(fmax_done, u + 1 if m <= 1024 or user[2] % 2 else u + 2)
                    if u >= 3:
                        _, pj, ph = UNITS[u - 3]
                        act.wait_ge(ring_full, RI[("probsT", pj, ph, len(parts(pj)) - 1)] + 1)
                    top, total = nmax[:, 2 + u % 2:3 + u % 2], rsum[:, 2 + u % 2:3 + u % 2]
                    if m > 1024:
                        act.activation(prob[:, u % 3, 1024:m], s_tail(user), ACT.Exp, bias=top,
                                       accum_out=tail_sum[:, u % 2:u % 2 + 1])
                        m = 1024
                    act.activation(prob[:, u % 3, 0:m], s_slot(user)[:, 0:m], ACT.Exp, bias=top,
                                   accum_out=total).then_inc(s_free[slot_of(user)], 1)
                else:
                    t = user[1]
                    n_ = PROJ.index(t)
                    m = P if t < NTILE else NS
                    s_ready(act, user)
                    if n_:
                        act.wait_ge(d_y, 32 * n_)
                    link(act.activation(zout[0:m, :], s_slot(user)[0:m, 0:D], ACT.Square, accum_out=zstat[0:m, 0:1]))
                    act.activation(zvar[0:m, :], zstat[0:m, 0:1], ACT.Identity, bias=eps[0:m, :], scale=1.0 / D)
                    act.activation(zstat[0:m, 1:2], zstat[0:m, 0:1], ACT.Sqrt, bias=eps[0:m, :], scale=1.0 / D
                                   ).then_inc(zstat_done, 1)

            def wo_high(k):
                if k == 0:
                    drained(act, ("s_outT", NB - 1))
                act.wait_ge(d_wo[k % 2], 16 * (k // 2 + 1))
                act.activation(woh[:, k, :], wo_raw[:, k % 2, :], ACT.Copy).then_inc(wohi_done, 1)

            def y_high(n_):
                t = PROJ[n_]
                m = P if t < NTILE else NS
                if t < NTILE:
                    for p_ in range(3):
                        drained(act, ("attend", t, p_))
                else:
                    drained(act, ("s_outT", NB - 1))
                if n_ >= 2:
                    s_ready(act, ("proj", PROJ[n_ - 2]))
                elif n_ == 1:
                    act.wait_ge(wolo_done, KT)
                act.activation(yh[n_ % 2][:, :, 0:m], Y[:, :, ycol(t):ycol(t) + m], ACT.Copy).then_inc(yhi_done, 1)

            for kind, key in PLAN:
                if kind == "Y":
                    y_high(PROJ.index(key[1]))
                elif kind == "W":
                    wo_high(key)
                elif kind == "E":
                    softmax_exp(key)
                elif kind == "S":
                    continue
                elif key[0] == "page_kT" and drains_on_act(key):
                    _, b, g = key
                    src = ring_ready(act, key)
                    act.activation(kT[:, b % 2, :, PAGE * g:PAGE * g + PAGE],
                                   src[:, 0:384].rearrange("p (g t) -> p g t", g=3), ACT.Copy).then_inc(freed(key), 1)
                elif key[0] == "probsT" and drains_on_act(key):
                    probsT_drain(act, key, lambda out, in_: act.activation(out, in_, ACT.Copy))

        @block.vector
        def _(dve):
            n = [0]

            def link(ins):
                n[0] += 1
                ins.then_inc(dve_step, 1)
                dve.wait_ge(dve_step, n[0])

            def rsqrt(r, f):
                link(dve.reciprocal(r, r))
                link(dve.scalar_tensor_tensor(out=f, in0=f, scalar=r, in1=r, op0=ALU.mult, op1=ALU.mult))
                link(dve.tensor_scalar(f, f, -0.5, 1.5, ALU.mult, ALU.add))

            def x_scale(i):
                t = XORDER[i]
                m = n_of(t)
                dve.wait_ge(rms_done, i + 1)
                r, f = (x[0:m, t:t + 1] for x in (rstd, refine))
                rsqrt(r, f)
                dve.tensor_scalar(xrows[0:m, t, :], xrows[0:m, t, :], r, f, ALU.mult, ALU.mult
                                  ).then_inc(xs_done, 1)

            def x_pre(i):
                m = n_of(XORDER[i])
                u = 4 + 2 * (i % 2)
                dve.wait_ge(xt_full, i + 1)
                if i >= 3:
                    x_low_done(dve, i - 3)
                src = PS[:, u:u + 2, :].rearrange("p b (k t) -> p (b k) t", t=P)[:, :, 0:m]
                dve.tensor_tensor(xg[:, i % 3, :, 0:m], src, gpre[:, :, None].to_broadcast([P, KT, m]), ALU.mult
                                  ).then_inc(xg_done, 1)

            dve.wait_ge(d_gpre, 16)
            x_scale(0)
            for i in range(9):
                if i + 1 < 9:
                    x_scale(i + 1)
                x_pre(i)
                if i - 1 in DVE_LOW or i == 8:
                    x_low(dve, i if i == 8 else i - 1).then_inc(xlo_dve, 1)

            def split_heads(j):
                c0, m = GBLOCKS[j]
                if j >= 2:
                    dve.wait_ge(ring_full, RI[("out", j - 2)] + 1)
                for g, r, n_ in ((0, P, 4), (1, 64, 2)):
                    ins = dve.tensor_tensor(q_heads[j % 2][0:r, 4 * g:4 * g + n_, 0:m],
                                            E[0:r, g, c0:c0 + m][:, None, :].to_broadcast([r, n_, m]),
                                            head_of[0:r, 0:n_, None].to_broadcast([r, n_, m]), ALU.mult)
                ins.then_inc(qheads_done, 1)

            def drain(key):
                kind = key[0]
                if kind == "page_prefix":
                    src = ring_ready(dve, key)
                    dve.wait_ge(page_scanned, H)
                    dve.scalar_tensor_tensor(out=page_F, in0=page_F, scalar=-1.0,
                                             in1=src[0:NS, 0:H, None].to_broadcast([NS, H, PAGE]),
                                             op0=ALU.mult, op1=ALU.subtract).then_inc(freed(key), 1)
                elif kind == "hist":
                    src = ring_ready(dve, key)
                    for i in range(2):
                        ins = dve.tensor_copy(hx[i][:, :, 0:HIST], src[:, 128 * i:128 * i + NB * HIST].rearrange(
                            "p (b t) -> p b t", b=NB))
                    ins.then_inc(freed(key), 1)
                elif kind == "state":
                    c = key[1]
                    src = ring_ready(dve, key)
                    if c >= 3 and c % 2:
                        split_heads((c + 1) // 2)
                    if c == 0:
                        dve.tensor_copy(gstate[:, 0, 0, :], src[:, 0:DV])
                        dve.tensor_copy(gstate[0:64, 0, 1, :], src[0:64, DV:2 * DV]).then_inc(freed(key), 1)
                        return
                    drained(dve, ("state", c - 1))
                    for g, r in ((0, P), (1, 64)):
                        ins = dve.scalar_tensor_tensor(out=gstate[0:r, c % 3, g, :], in0=gstate[0:r, (c - 1) % 3, g, :],
                                                       scalar=ebend[0:r, g, c:c + 1], in1=src[0:r, DV * g:DV * g + DV],
                                                       op0=ALU.mult, op1=ALU.add)
                    ins.then_inc(freed(key), 1)
                elif kind == "scores":
                    j = key[1]
                    src = ring_ready(dve, key)
                    for i in range(2):
                        r = slice(CH * i, CH * i + CH)
                        ins = dve.tensor_tensor(aT[r, j % 2, :, r], src[r, 0:384].rearrange("p (h t) -> p h t", h=H),
                                                causal[r, None, :].to_broadcast([CH, H, CH]), ALU.mult)
                    ins.then_inc(freed(key), 1)
                elif kind == "sample_scores":
                    src = ring_ready(dve, key)
                    dve.tensor_tensor(aT[0:NS, 0, :, 0:NS], src[0:NS, 0:384].rearrange("p (h t) -> p h t", h=H),
                                      causal_s[:, None, :].to_broadcast([NS, H, NS]), ALU.mult).then_inc(freed(key), 1)
                    dve.tensor_tensor(kd_seq, kd_rows[0:NS, 8:9, :].to_broadcast([NS, NB, 192]),
                                      same_seq[:, :, None].to_broadcast([NS, NB, 192]), ALU.mult).then_inc(kdseq_done, 1)
                elif kind == "fv_rows" and key[1] % 2:
                    src = ring_ready(dve, key)
                    dve.tensor_copy(VR[:, key[1], :], src[:, 0:384]).then_inc(freed(key), 1)
                elif kind == "sample_state":
                    _, g, i = key
                    r = P if g == 0 else 64
                    src = ring_ready(dve, key)
                    if (g, i) == (0, 0):
                        for gg, rr in ((0, P), (1, 64)):
                            dve.tensor_tensor(gstate_s[0:rr, gg], gstate_s[0:rr, gg],
                                              ebend[0:rr, gg, 17:25, None].to_broadcast([rr, NB, DV]),
                                              ALU.mult).then_inc(s0_scaled, 1)
                        dve.wait_ge(s0_scaled, 2)
                    part = gstate_s[0:r, g, 4 * i:4 * i + 4, :]
                    dve.tensor_tensor(part, part, src[0:r, 0:4 * DV].rearrange("p (b v) -> p b v", v=DV),
                                      ALU.add).then_inc(freed(key), 1)

            def store(c):
                src = chunk_psum(c)
                done = in_free[c % 2]
                if C_GV <= c < C_GV + 3:
                    dve.wait_ge(in_full, c + 1)
                    dve.tensor_copy(thirds(Y[:, c - C_GV, :]), src).then_inc(done, 1)
                elif c == C_GKA:
                    dve.wait_ge(in_full, c + 1)
                    dve.wait_ge(kd_exp, 2)
                    dve.tensor_tensor(thirds(E[:, 2, :]), thirds(E[:, 2, :]), src, ALU.mult)
                    dve.tensor_tensor(thirds(E[:, 4, :]), thirds(E[:, 4, :]), src, ALU.mult).then_inc(done, 1)
                elif c == C_GQA:
                    dve.wait_ge(in_full, c + 1)
                    dve.scalar_tensor_tensor(out=thirds(E[:, 0, :]), in0=src, scalar=DK ** -0.5,
                                             in1=thirds(E[:, 0, :]), op0=ALU.mult, op1=ALU.mult).then_inc(done, 1)
                elif c == C_QKB:
                    dve.wait_ge(in_full, c + 1)
                    dve.wait_ge(kb_moved, 1)
                    kb = QK[0:64, 4, :]
                    dve.tensor_tensor(E[0:64, 3, :], E[0:64, 3, :], kb, ALU.mult)
                    dve.tensor_tensor(E[0:64, 5, :], E[0:64, 5, :], kb, ALU.mult)
                    dve.scalar_tensor_tensor(out=thirds(E[0:64, 1, :]), in0=src[0:64], scalar=DK ** -0.5,
                                             in1=thirds(E[0:64, 1, :]), op0=ALU.mult, op1=ALU.mult).then_inc(done, 1)
                elif c in GATES:
                    g = gtmp[GATES.index(c) % 2]
                    dve.wait_ge(gexp_done, GATES.index(c) + 1)
                    if c < C_FG:
                        y = Y[:, c - C_GG, NMETA:NT]
                        if c >= C_PG:
                            drained(dve, ("pool", 1, 2))
                            drained(dve, ("pool", 1, 1))
                        for t in range(3):
                            c0, c1 = max(TH * t, NMETA), TH * t + TH
                            yt = Y[:, c - C_GG, c0:c1]
                            ins = dve.tensor_tensor(yt, yt, src[:, t, c0 - TH * t:], ALU.mult)
                    else:
                        y = Y[:, 5 + c - C_FG, :]
                        ins = dve.tensor_copy(thirds(y), src)
                    ins.then_inc(done, 1)
                    link(dve.tensor_scalar(g, g, 1.0, None, ALU.add))
                    link(dve.reciprocal(g, g))
                    chunk_stored(dve, c)
                    dve.tensor_tensor(y, y, g if c >= C_FG else g[:, NMETA:NT], ALU.mult).then_inc(gated, 1)

            def pool_windows(i):
                chunk_stored(dve, C_PV + i)
                if i == 0:
                    drained(dve, ("hist",))
                link(dve.tensor_copy(hx[i][:, :, HIST:HX], pv[:, LP:NT].rearrange("p (b t) -> p b t", t=TS)))
                if i == 1:
                    dve.wait_ge(ring_full, RI[("pool", 0, 2)] + 1)
                views = []
                for v, pa, pb_, lead, n_ in ((pv, psA, psB, 1, LP), (hx[i], hA, hB, 2, HX)):
                    cut = (lambda x, r, s0, s1, ld=lead: x[r, s0:s1] if ld == 1 else x[r, :, s0:s1])
                    views.append((v, pa, pb_, n_, cut))

                def add(dst, src, r, w):
                    for v, pa, pb_, n_, cut in views:
                        t = {"v": v, "a": pa, "b": pb_}
                        ins = dve.tensor_tensor(cut(t[dst], r, 2 * w - 1, n_), cut(t[src], r, 2 * w - 1, n_),
                                                cut(t[src], r, w - 1, n_ - w), ALU.add)
                    link(ins)

                every, low, high = slice(0, P), slice(0, 64), slice(64, P)
                add("a", "v", every, 1)
                if i == 0:
                    add("b", "a", high, 2)
                    ends = ((low, "a", 2), (high, "b", 4))
                else:
                    add("b", "a", every, 2)
                    add("a", "b", every, 4)
                    add("b", "a", high, 8)
                    ends = ((low, "a", 8), (high, "b", 16))
                for r, which, w in ends:
                    s = psA if which == "a" else psB
                    hs = hA if which == "a" else hB
                    dve.scalar_tensor_tensor(out=psA[r, NMETA:LP], in0=s[r, NMETA:LP], scalar=1.0 / w,
                                             in1=pv[r, NMETA:LP], op0=ALU.mult, op1=ALU.subtract)
                    ins = dve.scalar_tensor_tensor(out=psA[r, LP:NT].rearrange("p (b t) -> p b t", t=TS),
                                                   in0=hs[r, :, HIST:HX], scalar=1.0 / w, in1=hx[i][r, :, HIST:HX],
                                                   op0=ALU.mult, op1=ALU.subtract)
                ins.then_inc(pool_done, 1)

            def extra(c):
                if c == 0:
                    chunk_stored(dve, C_LF)
                    dve.wait_ge(d_const, 16 * 7)
                    dve.tensor_scalar(logf, logf, bfox[:, 0:1], None, ALU.add).then_inc(zf_done, 1)
                    dve.wait_ge(abs_done, 3)
                    dve.wait_ge(zf_done, 1)
                    for z, t in gate_parts:
                        link(dve.tensor_scalar(z, z, 0.0, None, ALU.min))
                if c == 1:
                    dve.wait_ge(ln_done, 3)
                    for z, t in gate_parts:
                        link(dve.tensor_tensor(z, z, t, ALU.subtract))
                    dve.wait_ge(consts_set, 2)
                    for g, r in ((0, P), (1, 64)):
                        b = E[0:r, 4 + g, :]
                        link(dve.tensor_tensor_scan(b, reset[0:r, :], E[0:r, g, :], 0.0, ALU.mult, ALU.add))
                        dve.tensor_copy(ebend[0:r, g, 0:1], b[:, NMETA - 1:NMETA])
                        dve.tensor_copy(ebend[0:r, g, 1:17, None],
                                        b[:, NMETA:LP].rearrange("p (c t) -> p c t", t=CH)[:, :, CH - 1:CH])
                        link(dve.tensor_copy(ebend[0:r, g, 17:25, None],
                                             b[:, LP:NT].rearrange("p (c t) -> p c t", t=TS)[:, :, TS - 1:TS]))
                    dve.tensor_tensor_scan(f_sum[:, :], reset[0:H, LP:NT], logf[:, LP:NT], 0.0, ALU.mult, ALU.add
                                           ).then_inc(b_done, 1)
                    link(dve.tensor_tensor_scan(fcum[:, 0:LP], ones_row[0:H, :], logf[:, 0:LP], 0.0, ALU.mult, ALU.add))
                if c == 2:
                    dve.wait_ge(e_done, 2)
                    for g, r in ((0, P), (1, 64)):
                        for s, e_, c0, c1, w in ((0, NMETA, 0, 1, NMETA), (NMETA, LP, 1, 17, CH), (LP, NT, 17, 25, TS)):
                            b = E[0:r, 4 + g, s:e_].rearrange("p (c t) -> p c t", t=w)
                            ins = dve.tensor_tensor(b, ebend[0:r, g, c0:c1, None].to_broadcast([r, c1 - c0, w]), b,
                                                    ALU.subtract)
                    ins.then_inc(kd_sub, 1)
                    dve.wait_ge(d_lf, 16)
                    for h in range(H):
                        dve.tensor_tensor_scan(page_F[:, h, :], ones_row[:, 0:PAGE], page_lf[:, :, h], 0.0,
                                               ALU.mult, ALU.add).then_inc(page_scanned, 1)
                if c == 3:
                    dve.wait_ge(consts_set, 3)
                    f, r1 = fcum[:, 0:LP], ftmp[:, 0:LP]
                    link(dve.tensor_scalar(negF[0:H, :], f, -1.0, None, ALU.mult))
                    link(dve.scalar_tensor_tensor(out=r1, in0=f, scalar=-1.0, in1=negF[0:H, :], op0=ALU.mult,
                                                  op1=ALU.subtract))
                    link(dve.tensor_copy(negF[32:32 + H, :], r1))
                    link(dve.tensor_copy(f, negF[32:32 + H, :]))
                    link(dve.tensor_tensor(r1, r1, f, ALU.subtract))
                    dve.tensor_copy(negF[64:64 + H, :], r1).then_inc(negF_done, 1)
                if c == C_QKB:
                    dve.wait_ge(in_free[0], C_QKB // 2 + 1)
                    for x in (gstate[64:P, :, 1, :], gstate_s[64:P, 1], q_heads[0][64:P, 4:H, :], q_heads[1][64:P, 4:H, :]):
                        dve.memset(x, 0.0)
                    dve.wait_ge(ring_full, RI[("pool", 1, 2)] + 1)
                    dve.memset(aT[:, :, :, :], 0.0)
                    split_heads(0)
                    split_heads(1)
                if c == C_PV:
                    dve.wait_ge(consts_set, 4)
                if c in (C_PV, C_PV + 1):
                    pool_windows(c - C_PV)
                if c == C_PV + 1:
                    dve.wait_ge(d_fl, 16)
                    fs = f_sum[:, :].rearrange("h (b t) -> h b t", t=TS)
                    dve.tensor_tensor(fs, f_last[:, :, None].to_broadcast([H, NB, TS]), fs, ALU.subtract
                                      ).then_inc(fnew_done, 1)
                if c == 13:
                    dve.wait_ge(orstd_done, 3)
                    for i in range(3):
                        y = Y[:, i, NMETA:NT]
                        dve.scalar_tensor_tensor(out=y, in0=y, scalar=gnorm[:, 0:1], in1=E[:, 3 + i, NMETA:NT],
                                                 op0=ALU.mult, op1=ALU.mult).then_inc(o_normed, 1)
                    dve.wait_ge(o_normed, 3)

            for c in range(1, NCHUNK + 1):
                store(c - 1)
                for key in SIDE[c - 1]:
                    drain(key)
                extra(c - 1)

            dve.wait_ge(gated, len(GATES))
            dve.wait_ge(qdiag_zero, 1)
            for p_ in range(3):
                for i in range(2):
                    r = slice(64 * i, 64 * i + 64)
                    ins = dve.tensor_copy(q_diag[r, p_, :, TS * i:TS * i + TS],
                                          QK[r, 3 + p_, LP:NT].rearrange("p (b t) -> p b t", t=TS))
            ins.then_inc(qdiag_done, 1)
            dve.memset(s_rows, 0.0).then_inc(srows_zero, 1)

            def row_max(user):
                if user[0] == "seq":
                    b = user[1]
                    u = b % 2
                    s_ready(dve, user)
                    if b == 0:
                        dve.wait_ge(sbias_zero, 1)
                    dve.wait_ge(d_bias[u], 16 * H * (b // 2 + 1))
                    if b >= 2:
                        dve.wait_ge(ring_full, RI[("s_probsT_b", b - 2)] + 1)
                    dve.tensor_tensor_reduce(sprob[:, u, :], s_slot(user)[0:96, 0:PAST + TS], sbias[:, u, :], 1.0,
                                             -3e38, ALU.add, ALU.max, nmax[0:96, 4 + u:5 + u]
                                             ).then_inc(s_free[slot_of(user)], 1)
                    s_emptied(dve, user)
                    dve.tensor_scalar(nmax[0:96, u:u + 1], nmax[0:96, 4 + u:5 + u], -1.0, None, ALU.mult
                                      ).then_inc(smax_done, 1)
                elif user[0] == "fox":
                    u = UI[user]
                    s_ready(dve, user)
                    m = NMETA + P * (user[1] + 1)
                    top = nmax[:, 2 + u % 2:3 + u % 2]
                    if m <= 1024:
                        dve.tensor_reduce(top, s_slot(user)[:, 0:m], AX.X, ALU.max, negate=True).then_inc(fmax_done, 1)
                    else:
                        dve.tensor_reduce(tail_max[:, u % 2:u % 2 + 1], s_tail(user), AX.X, ALU.max, negate=True)
                        link(dve.tensor_reduce(top, s_slot(user)[:, 0:1024], AX.X, ALU.max, negate=True))
                        dve.tensor_tensor(top, top, tail_max[:, u % 2:u % 2 + 1], ALU.min).then_inc(fmax_done, 1)

            def finish(user):
                if user[0] == "seq":
                    b = user[1]
                    u = b % 2
                    dve.wait_ge(sexp_done, b + 1)
                    link(dve.reciprocal(rinv[0:96, u:u + 1], rsum[0:96, u:u + 1]))
                    dve.tensor_scalar(sprob[:, u, :], sprob[:, u, :], rinv[0:96, u:u + 1], None, ALU.mult
                                      ).then_inc(sprob_done, 1)
                elif user[0] == "fox":
                    u = UI[user]
                    m = NMETA + P * (user[1] + 1)
                    s_emptied(dve, user)
                    total = rsum[:, 2 + u % 2:3 + u % 2]
                    if m > 1024:
                        link(dve.tensor_tensor(total, total, tail_sum[:, u % 2:u % 2 + 1], ALU.add))
                    link(dve.reciprocal(rinv[:, 2 + u % 2:3 + u % 2], total))
                    dve.tensor_scalar(prob[:, u % 3, 0:m], prob[:, u % 3, 0:m], rinv[:, 2 + u % 2:3 + u % 2], None,
                                      ALU.mult).then_inc(fprob_done, 1)
                else:
                    t = user[1]
                    n_ = PROJ.index(t)
                    m = P if t < NTILE else NS
                    dve.wait_ge(zstat_done, n_ + 1)
                    if n_ == 0:
                        dve.wait_ge(d_post, 16)
                    rsqrt(zstat[0:m, 1:2], zvar[0:m, :])
                    link(dve.tensor_scalar(zstat[0:m, 1:2], zstat[0:m, 1:2], zvar[0:m, :], None, ALU.mult))
                    for n_half, cols in enumerate((slice(0, D // 2), slice(D // 2, D))):
                        ins = dve.scalar_tensor_tensor(out=zout[0:m, cols], in0=s_slot(user)[0:m, cols],
                                                       scalar=zstat[0:m, 1:2], in1=gpost[0:m, cols],
                                                       op0=ALU.mult, op1=ALU.mult)
                        if n_half:
                            ins.then_inc(s_free[slot_of(user)], 1)
                            s_emptied(dve, user)
                        else:
                            link(ins)
                            dve.wait_ge(d_xres, 16 * (n_ + 1))
                        dve.tensor_tensor(zout[0:m, cols], zout[0:m, cols], xres[0:m, cols], ALU.add
                                          ).then_inc(y_done, 1)

            for kind, key in PLAN:
                if kind == "E":
                    finish(key)
                elif kind == "S":
                    row_max(key)
                if kind != "R":
                    continue
                if key[0] == "page_kT" and not drains_on_act(key):
                    _, b, g = key
                    src = ring_ready(dve, key)
                    dve.tensor_copy(kT[:, b % 2, :, PAGE * g:PAGE * g + PAGE],
                                    src[:, 0:384].rearrange("p (g t) -> p g t", g=3)).then_inc(freed(key), 1)
                elif key[0] == "probsT" and not drains_on_act(key):
                    probsT_drain(dve, key, dve.tensor_copy)
                elif key[0] in ("s_probsT_a", "s_probsT_b"):
                    u = key[1] % 2
                    g0 = 0 if key[0] == "s_probsT_a" else 4
                    src = ring_ready(dve, key)
                    ins = dve.tensor_copy(sprobT[u][:, g0:g0 + 4, :].rearrange("p g (a q) -> p g a q", a=3),
                                          src[:, 0:384].rearrange("p (g a q) -> p g a q", g=4, a=3)[:, :, :, 0:16])
                    if g0:
                        ins = dve.tensor_copy(sprobT[u][0:TS, NPAGE, :].rearrange("p (a q) -> p a q", a=3),
                                              src[0:TS, 384:480].rearrange("p (a q) -> p a q", a=3)[:, :, 0:16])
                    ins.then_inc(freed(key), 1)
                elif key[0] == "s_attend":
                    src = ring_ready(dve, key)
                    dve.wait_ge(srows_zero, 1)
                    for p_ in range(3):
                        r = slice(32 * p_, 32 * p_ + 16)
                        ins = dve.tensor_copy(s_rows[r, :], src[r, 0:P])
                    ins.then_inc(freed(key), 1)
                elif key[0] == "s_outT":
                    src = ring_ready(dve, key)
                    c0 = LP + TS * key[1]
                    for i in range(2):
                        r = slice(64 * i, 64 * i + 64)
                        y = Y[r, 5:8, c0:c0 + TS]
                        ins = dve.tensor_tensor(y, y, src[r, 0:96].rearrange("p (g q) -> p g q", g=3)[
                            :, :, TS * i:TS * i + TS], ALU.mult)
                    ins.then_inc(freed(key), 1)
                elif key[0] == "attend":
                    _, j, p_ = key
                    src = ring_ready(dve, key)
                    y = Y[:, 5 + p_, NMETA + P * j:NMETA + P * j + P]
                    dve.tensor_tensor(y, y, src[:, 0:P], ALU.mult).then_inc(freed(key), 1)

        @block.tensor
        def _(pe):
            pe.wait_ge(consts_set, 1)
            def product(out, parts, rhs_of):
                for k in range(KT):
                    sh, sl = parts(k)
                    mh, ml = rhs_of(k)
                    pe.matmul(out, sh, mh, start=(k == 0), stop=False)
                    pe.matmul(out, sh, ml, start=False, stop=False)
                    ins = pe.matmul(out, sl, mh, start=False, stop=(k == KT - 1))
                return ins

            def x_transposes(i):
                t = XORDER[i]
                u = 4 + 2 * (i % 2)
                m = n_of(t)
                pe.wait_ge(xs_done, i + 1)
                if i >= 2:
                    pe.wait_ge(xg_done, i - 1)
                for k in range(KT):
                    ins = pe.transpose(PS[:, u + k // 4, P * (k % 4):P * (k % 4) + m],
                                       xrows[0:m, t, P * k:P * k + P], ident[0:m, 0:m])
                ins.then_inc(xt_full, 1)

            def project_in(c):
                pe.wait_ge(wlo_done, c + 1)
                pe.wait_ge(whi_done, c + 1)
                if c >= 2:
                    chunk_stored(pe, c - 2)
                if c == 1:
                    pe.wait_ge(xg_done, 9)
                jobs = SIDE[c - 1] if c else []
                first, last = STEPS.get(c - 1, (3, 3 * KT))
                given = 0
                for t in range(3):
                    if c == 0:
                        x_low_done(pe, (3, 6, 8)[t])
                    cols = slice(TH * t, TH * t + TH)
                    m = chunk_width(c)
                    out = PS[0:m, 3 * (c % 2) + t, 0:TH]
                    for k in range(KT):
                        high, low = wh[:, c % 2, k, 0:m], wl[:, c % 2, k, 0:m]
                        pe.matmul(out, high, xh[:, k, cols], start=(k == 0), stop=False)
                        pe.matmul(out, high, xl[:, k, cols], start=False, stop=False)
                        ins = pe.matmul(out, low, xh[:, k, cols], start=False, stop=(k == KT - 1))
                        if (t, k) == (2, KT - 1):
                            ins.then_inc(in_full, 1)
                        step = KT * t + k + 1
                        if c == 0 and step in (2, 5, 8):
                            x_transposes(6 + (step - 2) // 3)
                        upto = len(jobs) * (min(max(step, first), last) - first) // (last - first)
                        for key in jobs[given:upto]:
                            side(key)
                        given = upto

            def side(key):
                kind = key[0]
                out = ring_take(pe, key)
                if kind == "gate":
                    _, g, t = key
                    if (g, t) == (0, 0):
                        chunk_stored(pe, C_LF)
                        pe.wait_ge(d_const, 16 * 7)
                    m = P if g == 0 else 64
                    ins = pe.matmul(out[0:m, 0:TH], w_up[:, P * g:P * g + m], glr[:, TH * t:TH * t + TH],
                                    start=True, stop=True)
                elif kind == "logf_rows":
                    pe.wait_ge(b_done, 1)
                    for t in range(9):
                        m = P if t < NTILE else NMETA + NS
                        ins = pe.transpose(out[0:m, H * t:H * t + H], logf[:, P * t:P * t + m], ident[0:H, 0:H])
                elif kind == "page_prefix":
                    pe.wait_ge(page_scanned, H)
                    pe.wait_ge(consts_set, 3)
                    ins = pe.matmul(out[0:NS, 0:H], page_before[:, :], page_F[:, :, PAGE - 1], start=True, stop=True)
                elif kind == "v_rows":
                    b = key[1]
                    col, m = GBLOCKS[b]
                    if b == 0:
                        pe.wait_ge(consts_set, 4)
                        chunk_stored(pe, C_GV + 1)
                        chunk_stored(pe, C_GV + 2)
                    for i in range(3):
                        ins = pe.transpose(out[0:m, P * i:P * i + P], Y[:, i, col:col + m], ident[:, :])
                elif kind == "hist":
                    pe.wait_ge(d_hist, 16)
                    m = NB * HIST
                    for i in range(2):
                        ins = pe.transpose(out[:, 128 * i:128 * i + m], hist_rows[:, P * i:P * i + P], ident[0:m, 0:m])
                elif kind == "pool_last":
                    i = key[1]
                    chunk_stored(pe, C_PV + i)
                    pe.transpose(out[0:HIST, 0:P], pv[:, LP - HIST:LP], ident[:, :])
                    ins = pe.transpose(out[0:NS, P:2 * P], pv[:, LP:NT], ident[:, :])
                elif kind == "pool":
                    _, i, q = key
                    col, m = PIECES[q]
                    pe.wait_ge(pool_done, i + 1)
                    pe.wait_ge(d_poolw, 16 * 4)
                    ins = pe.matmul(out[:, 0:m], pool_w[:, i, :], psA[:, col:col + m], start=True, stop=True)
                elif kind == "kd_rows":
                    i = key[1]
                    if i == 0:
                        chunk_stored(pe, C_QKB)
                        chunk_stored(pe, C_GQA)
                        drained(pe, ("pool", 1, 2))
                    for n_, b in enumerate((2 * i, 2 * i + 1)):
                        col, m = GBLOCKS[b]
                        pe.transpose(out[0:m, 192 * n_:192 * n_ + P], E[:, 4, col:col + m], ident[:, :])
                        ins = pe.transpose(out[0:m, 192 * n_ + P:192 * n_ + 192], E[0:64, 5, col:col + m],
                                           ident[0:64, 0:64])
                elif kind == "state":
                    c = key[1]
                    b, r0, m = (9, 0, NMETA) if c == 0 else ((c - 1) // 2, CH * ((c - 1) % 2), CH)
                    if c == 0:
                        drained(pe, ("kd_rows", 4))
                        drained(pe, ("kd_rows", 3))
                        drained(pe, ("v_rows", 9))
                        drained(pe, ("v_rows", 8))
                    rows = slice(r0, r0 + m)
                    kd = kd_meta if c == 0 else kd_rows[rows, b, :]
                    for h in range(H):
                        ins = pe.matmul(out[head_rows(h), DV * (h // 4):DV * (h // 4) + DV],
                                        kd[:, DK * h:DK * h + DK], VR[rows, b, DV * h:DV * h + DV],
                                        start=True, stop=True)
                elif kind == "scores":
                    j = key[1]
                    pe.wait_ge(qheads_done, j + 1)
                    for i in range(2):
                        c0 = NMETA + P * j + CH * i
                        for h in range(H):
                            r = group_rows(h)
                            ins = pe.matmul(out[CH * i:CH * i + CH, CH * h:CH * h + CH], E[r, 2 + h // 4, c0:c0 + CH],
                                            q_heads[j % 2][r, h, CH * i:CH * i + CH], start=True, stop=True)
                elif kind == "out":
                    j = key[1]
                    drained(pe, ("scores", j))
                    drained(pe, ("state", 2 * j + 1))
                    drained(pe, ("state", 2 * j))
                    for h in range(H):
                        rows = slice(64 * (h % 2), 64 * (h % 2) + 64)
                        dst = out[rows, P * (h // 2):P * (h // 2) + P]
                        pe.matmul(dst, VR[:, j, DV * h:DV * h + DV], aT[:, j % 2, h, :], start=True, stop=False,
                                  skip_group_check=True)
                        for i in range(2):
                            ins = pe.matmul(dst[:, CH * i:CH * i + CH], gstate[:, (2 * j + i) % 3, h // 4, :],
                                            q_heads[j % 2][:, h, CH * i:CH * i + CH], start=False, stop=(i == 1),
                                            skip_group_check=True)
                elif kind == "sample_scores":
                    pe.wait_ge(qheads_done, NTILE + 1)
                    for h in range(H):
                        r = group_rows(h)
                        ins = pe.matmul(out[0:NS, CH * h:CH * h + CH], E[r, 2 + h // 4, LP:NT],
                                        q_heads[0][r, h, 0:NS], start=True, stop=True)
                elif kind == "sample_out":
                    drained(pe, ("sample_scores",))
                    pe.wait_ge(d_s0, 32)
                    for h in (2 * key[1], 2 * key[1] + 1):
                        rows = slice(64 * (h % 2), 64 * (h % 2) + 64)
                        pe.matmul(out[rows, 0:NS], VR[0:NS, 8, DV * h:DV * h + DV], aT[0:NS, 0, h, 0:NS],
                                  start=True, stop=False, skip_group_check=True)
                        for b in range(NB):
                            ins = pe.matmul(out[rows, TS * b:TS * b + TS], gstate_s[:, h // 4, b, :],
                                            q_heads[0][:, h, TS * b:TS * b + TS],
                                            start=False, stop=(b == NB - 1), skip_group_check=True)
                elif kind == "sample_state":
                    _, g, i = key
                    pe.wait_ge(kdseq_done, 1)
                    for h in range(4 * g, min(4 * g + 4, H)):
                        for b in range(4):
                            ins = pe.matmul(out[head_rows(h), DV * b:DV * b + DV],
                                            kd_seq[:, 4 * i + b, DK * h:DK * h + DK], VR[0:NS, 8, DV * h:DV * h + DV],
                                            start=True, stop=True)
                elif kind == "meansq":
                    _, i, q = key
                    col, m = PIECES[q]
                    pe.wait_ge(osq_done, i + 1)
                    ins = pe.matmul(out[:, 0:m], block_mean[:, :], E[:, i, col:col + m], start=True, stop=True)
                elif kind in ("k_rows", "fv_rows"):
                    t = key[1]
                    src = QK if kind == "k_rows" else E
                    last = C_FK if kind == "k_rows" else C_FV
                    if t == 0:
                        chunk_stored(pe, last + 1)
                        chunk_stored(pe, last + 2)
                    m = P if t < NTILE else NMETA + NS
                    for i in range(3):
                        ins = pe.transpose(out[0:m, P * i:P * i + P], src[:, i, P * t:P * t + m], ident[:, :])
                ins.then_inc(ring_full, 1)

            for i in range(6):
                x_transposes(i)
            for c in range(NCHUNK):
                project_in(c)

            def page_kT(key):
                _, b, g = key
                out = ring_take(pe, key)
                if g == 0:
                    pe.wait_ge(d_k[b % 2], 16 * NPAGE * (b // 2 + 1))
                for i in range(3):
                    ins = pe.transpose(out[:, P * i:P * i + P], pages[b % 2][:, 0, g, P * i:P * i + P], ident[:, :])
                ins.then_inc(ring_full, 1)

            def sample_scores(user):
                b = user[1]
                s_taken(pe, user)
                out = s_slot(user)
                drained(pe, ("page_kT", b, NPAGE - 1))
                drained(pe, ("page_kT", b, NPAGE - 2))
                pe.wait_ge(qdiag_done, 1)
                for half in range(2):
                    for p_ in range(3):
                        pe.matmul(out[32 * p_:32 * p_ + 32, 512 * half:512 * half + 512], q_diag[:, p_, b, :],
                                  kT[:, b % 2, p_, 512 * half:512 * half + 512], start=True, stop=True)
                for p_ in range(3):
                    pe.matmul(out[32 * p_:32 * p_ + 32, PAST:PAST + TS], q_diag[:, p_, b, :],
                              QK[:, p_, LP + TS * b:LP + TS * b + TS], start=True, stop=False)
                pe.matmul(out[0:96, PAST:PAST + TS], pick_q[:, :], mask_new[:, :], start=False, stop=True
                          ).then_inc(s_full, 1)

            def sample_probsT(key):
                b = key[1]
                u = b % 2
                out = ring_take(pe, key)
                pe.wait_ge(sprob_done, b + 1)
                g0 = 0 if key[0] == "s_probsT_a" else 4
                for g in range(4):
                    c0 = PAGE * (g0 + g)
                    ins = pe.transpose(out[:, 96 * g:96 * g + 96], sprob[:, u, c0:c0 + PAGE], ident[0:96, 0:96])
                if g0:
                    ins = pe.transpose(out[0:TS, 384:480], sprob[:, u, PAST:PAST + TS], ident[0:96, 0:96])
                ins.then_inc(ring_full, 1)

            def sample_attend(key):
                b = key[1]
                u = b % 2
                drained(pe, ("s_probsT_a", b))
                drained(pe, ("s_probsT_b", b))
                out = ring_take(pe, key)
                pe.wait_ge(d_v[u], 16 * (NPAGE + 1) * (b // 2 + 1))
                for g in range(NPAGE + 1):
                    for p_ in range(3):
                        cols, qs = slice(P * p_, P * p_ + P), slice(16 * p_, 16 * p_ + 16)
                        v = pages[u][:, 1, g, cols] if g < NPAGE else v_new[:, u, cols]
                        pt = sprobT[u][:, g, qs] if g < NPAGE else sprobT[u][0:TS, g, qs]
                        ins = pe.matmul(out[32 * p_:32 * p_ + 16, 0:P], pt, v, start=(g == 0), stop=(g == NPAGE))
                ins.then_inc(ring_full, 1)

            def sample_outT(key):
                drained(pe, ("s_attend", key[1]))
                out = ring_take(pe, key)
                pe.transpose(out[:, 0:96], s_rows, ident[0:96, 0:96]).then_inc(ring_full, 1)

            pe.wait_ge(negF_done, 1)
            chunk_stored(pe, NCHUNK - 1)
            chunk_stored(pe, NCHUNK - 2)

            def fox_scores(j, p_):
                m = NMETA + P * (j + 1)
                q0 = NMETA + P * j
                heads = [(h, ("fox", j, h), slice(64 * (h % 2), 64 * (h % 2) + 64)) for h in (2 * p_, 2 * p_ + 1)]

                for _, user, _ in heads:
                    s_taken(pe, user)
                def tail(h, user, rows):
                    if h % 2:
                        pe.wait_ge(tail_done, p_ + 1)
                    pe.matmul(s_tail(user), QK[rows, 3 + p_, q0:q0 + P], QK[rows, p_, 1024:m], start=True, stop=False)
                    pe.matmul(s_tail(user), pick_row[0:64 + H, h, :], negF[0:64 + H, 1024:m], start=False, stop=False)
                    ins = pe.matmul(s_tail(user), identb[:, :], mask_neg[:, 1024 - q0:m - q0], start=False, stop=True)
                    if h % 2 == 0:
                        ins.then_inc(tail_done, 1)

                if m > 1024:
                    tail(*heads[0])
                for c0 in range(0, min(m, 1024), 512):
                    c1 = min(c0 + 512, m)
                    for h, user, rows in heads:
                        pe.matmul(s_slot(user)[:, c0:c1], QK[rows, 3 + p_, q0:q0 + P], QK[rows, p_, c0:c1],
                                  start=True, stop=False)
                if m > 1024:
                    tail(*heads[1])
                for h, user, rows in heads:
                    for c0 in range(0, min(m, 1024), 512):
                        c1 = min(c0 + 512, m, 1024)
                        d0 = max(c0, q0)
                        ins = pe.matmul(s_slot(user)[:, c0:c1], pick_row[0:64 + H, h, :], negF[0:64 + H, c0:c1],
                                        start=False, stop=(d0 >= c1))
                        if d0 < c1:
                            ins = pe.matmul(s_slot(user)[:, d0:c1], identb[:, :], mask_neg[:, d0 - q0:c1 - q0],
                                            start=False, stop=True)
                    ins.then_inc(s_full, 1)

            def project_out(user):
                t = user[1]
                n_ = PROJ.index(t)
                m = P if t < NTILE else NS
                s_taken(pe, user)
                out = s_slot(user)
                pe.wait_ge(yhi_done, n_ + 1)
                pe.wait_ge(ylo_done, n_ + 1)
                pe.wait_ge(wolo_done, KT)
                for half in range(2):
                    cols = slice(512 * half, 512 * half + 512)
                    ins = product(out[0:m, cols], lambda k: (yh[n_ % 2][:, k, 0:m], yl[n_ % 2][:, k, 0:m]),
                                  lambda k: (woh[:, k, cols], wol[k][:, cols]))
                ins.then_inc(s_full, 1)

            fox_scores(0, 0)
            for key in SIDE[NCHUNK - 1]:
                side(key)
            for kind, key in PLAN:
                if kind in ("E", "Y", "W"):
                    continue
                if kind == "S" and key[0] == "fox":
                    if key[2] % 2 == 0 and key[1:] != (0, 0):
                        fox_scores(key[1], key[2] // 2)
                elif kind == "S" and key[0] == "seq":
                    sample_scores(key)
                elif kind == "S":
                    project_out(key)
                elif key[0] == "page_kT":
                    page_kT(key)
                elif key[0] in ("s_probsT_a", "s_probsT_b"):
                    sample_probsT(key)
                elif key[0] == "s_attend":
                    sample_attend(key)
                elif key[0] == "s_outT":
                    sample_outT(key)
                elif key[0] == "probsT":
                    _, j, h, i = key
                    u = UI[("fox", j, h)]
                    out = ring_take(pe, key)
                    pe.wait_ge(fprob_done, u + 1)
                    for n_, b in enumerate(parts(j)[i]):
                        w = P if b <= j else NMETA
                        ins = pe.transpose(out[0:w, P * n_:P * n_ + P], prob[:, u % 3, P * b:P * b + w], ident[:, :])
                    ins.then_inc(ring_full, 1)
                else:
                    _, j, p_ = key
                    out = ring_take(pe, key)
                    for h in (2 * p_, 2 * p_ + 1):
                        for i in range(len(parts(j))):
                            drained(pe, ("probsT", j, h, i))
                    for b in range(j + 2):
                        w = P if b <= j else NMETA
                        for i in range(2):
                            h = 2 * p_ + i
                            ins = pe.matmul(out[64 * i:64 * i + 64, 0:P], VR[0:w, b, HD * h:HD * h + HD],
                                            probT[0:w, UI[("fox", j, h)] % 2, b, :], start=(b == 0), stop=(b == j + 1))
                    ins.then_inc(ring_full, 1)


INPUTS = ["x_prompt", "x_sample", "cache_fox_k", "cache_fox_v", "cache_fox_logf", "state_gla", "state_pool",
          "page_table", "meta_tokens", "norm_pre", "norm_post", "w_in", "gla_w_up", "gla_b_gate", "gla_norm",
          "pool_w", "pool_scale", "fox_b_f", "w_out"]
OUTPUTS = [("y_p", (1, SEQ, D)), ("y_s", (NB, TS, D)), ("fox_kp", (1, 1, LP, H, HD)), ("fox_vp", (1, 1, LP, H, HD)),
           ("logf_p", (1, 1, LP, H)), ("gla_p", (1, 1, H, DK, DV)), ("pool_p", (1, 1, HIST, 256)),
           ("fox_ks", (1, NB, TS, H, HD)), ("fox_vs", (1, NB, TS, H, HD)), ("logf_s", (1, NB, TS, H)),
           ("gla_s", (1, NB, H, DK, DV)), ("pool_s", (1, NB, HIST, 256))]


def kernel(**inputs):
    import numpy as np
    import concourse.bacc as bacc
    from concourse.bass_utils import run_bass_kernel_spmd

    nc = bacc.Bacc("TRN2", target_bir_lowering=False, num_devices=1)
    arrays, a, o = {}, {}, {}
    for name in INPUTS:
        x = np.ascontiguousarray(inputs[name])
        arrays[f"in_{name}_dram"] = x
        a[name] = nc.dram_tensor(f"in_{name}_dram", x.shape, mybir.dt.from_np(x.dtype), kind="ExternalInput").ap()
    for name, shape in OUTPUTS:
        o[name] = nc.dram_tensor(f"out_{name}_dram", shape, F32, kind="ExternalOutput").ap()
    build(nc, a, o)
    r = run_bass_kernel_spmd(nc, [arrays], core_ids=[0])
    return tuple(r.results[0][f"out_{name}_dram"] for name, _ in OUTPUTS)
```
